# Optimizing a Trainium2 kernel written in Bass

```python
import jax, jax.numpy as jnp
from jax import lax
import numpy as np

D_MODEL = 1024
BATCH = 1
SEQ = 512
DEPTH = 1
DEC_BATCH = 1
DEC_SEQ = 64
PAST_LEN = 1024

CHUNK = 64
EPS = 1e-6
WINDOW = 128
A_HEADS = 8
A_KV_HEADS = 2
A_HEAD_DIM = 64
A_GROUP = A_HEADS // A_KV_HEADS
A_WIDTH = A_HEADS * A_HEAD_DIM
A_KV_WIDTH = A_KV_HEADS * A_HEAD_DIM
B_HEADS = 4
B_KEY_DIM = 128
B_VAL_DIM = 128
B_KEY_WIDTH = B_HEADS * B_KEY_DIM
B_WIDTH = B_HEADS * B_VAL_DIM
MIX_WIDTH = A_WIDTH + B_WIDTH
N_IN = A_WIDTH + 2 * A_KV_WIDTH + 2 * B_KEY_WIDTH + 2 * B_WIDTH
N_GROUPS = 4
EXPERTS_PER_GROUP = 4
N_EXPERTS = N_GROUPS * EXPERTS_PER_GROUP
TOP_K = 2
D_EXPERT = 256

kernel_name = "hybrid_swa_sink_hgrn2_hmoe_stream_step"

def rmsnorm(x, g):
    xf = x.astype(jnp.float32)
    y = xf * lax.rsqrt(jnp.mean(xf * xf, axis=-1, keepdims=True) + EPS)
    return (y * g.astype(jnp.float32)).astype(x.dtype)

def alibi_slopes(n):
    return jnp.exp2(-8.0 * jnp.arange(1, n + 1, dtype=jnp.float32) / n)

def swa_sink_attention(q, k, v, k_hist, v_hist, pos0, sink):
    bsz, seq = q.shape[0], q.shape[1]
    hist = k_hist.shape[1]
    cq = min(CHUNK, seq)
    nc = seq // cq
    kp = jnp.concatenate([k_hist, k], axis=1)
    vp = jnp.concatenate([v_hist, v], axis=1)
    idx = jnp.arange(nc)[:, None] * cq + jnp.arange(hist + cq)[None, :]
    kw = kp[:, idx]
    vw = vp[:, idx]
    qb = q.reshape(bsz, nc, cq, A_KV_HEADS, A_GROUP, A_HEAD_DIM)
    s = jnp.einsum('bcqhgd,bckhd->bhgcqk', qb, kw,
                   preferred_element_type=jnp.float32) * (A_HEAD_DIM ** -0.5)
    qpos = jnp.arange(nc)[:, None] * cq + jnp.arange(cq)[None, :]
    kpos = idx - hist
    dist = jnp.abs(qpos[:, :, None] - kpos[:, None, :]).astype(jnp.float32)
    slopes = alibi_slopes(A_HEADS).reshape(A_KV_HEADS, A_GROUP)
    s = s - slopes[:, :, None, None, None] * dist
    valid = (pos0 + kpos) >= 0
    s = jnp.where(valid[:, None, :], s, -jnp.inf)
    sink_l = sink.astype(jnp.float32).reshape(A_KV_HEADS, A_GROUP)[None, :, :, None, None, None]
    m = jnp.maximum(jnp.max(s, axis=-1, keepdims=True), sink_l)
    p = jnp.exp(s - m)
    denom = jnp.sum(p, axis=-1, keepdims=True) + jnp.exp(sink_l - m)
    o = jnp.einsum('bhgcqk,bckhd->bcqhgd', (p / denom).astype(vw.dtype), vw)
    return o.reshape(bsz, seq, A_WIDTH), kp[:, -hist:], vp[:, -hist:]

def hgrn2(q, f_logit, i_in, g_in, lb, norm_g, s0):
    bsz, seq = q.shape[0], q.shape[1]
    cq = min(CHUNK, seq)
    nc = seq // cq
    f32 = jnp.float32
    qf = jax.nn.silu(q.astype(f32)).reshape(bsz, nc, cq, B_HEADS, B_KEY_DIM)
    f = lb + (1.0 - lb) * jax.nn.sigmoid(f_logit.astype(f32))
    kf = (1.0 - f).reshape(bsz, nc, cq, B_HEADS, B_KEY_DIM)
    logf = jnp.log(f).reshape(bsz, nc, cq, B_HEADS, B_KEY_DIM)
    vf = i_in.astype(f32).reshape(bsz, nc, cq, B_HEADS, B_VAL_DIM)
    cum = jnp.cumsum(logf, axis=2)
    ref = cum[:, :, cq // 2][:, :, None]
    q_in = qf * jnp.exp(cum - ref)
    k_in = kf * jnp.exp(ref - cum)
    a = jnp.einsum('bcthk,bcshk->bchts', q_in, k_in)
    a = jnp.where(jnp.tril(jnp.ones((cq, cq), dtype=bool)), a, 0.0)
    o_intra = jnp.einsum('bchts,bcshv->bcthv', a, vf)
    tot = cum[:, :, -1]
    ds = jnp.einsum('bcshk,bcshv->bchkv', kf * jnp.exp(tot[:, :, None] - cum), vf)
    decay = jnp.exp(tot)

    def step(state, inp):
        ds_c, dec_c = inp
        return dec_c[..., None] * state + ds_c, state

    s_fin, s_in = lax.scan(step, s0.astype(f32),
                           (jnp.moveaxis(ds, 1, 0), jnp.moveaxis(decay, 1, 0)))
    s_in = jnp.moveaxis(s_in, 0, 1)
    o_inter = jnp.einsum('bcthk,bchkv->bcthv', qf * jnp.exp(cum), s_in)
    o = (o_intra + o_inter).reshape(bsz, seq, B_HEADS, B_VAL_DIM)
    o = o * lax.rsqrt(jnp.mean(o * o, axis=-1, keepdims=True) + EPS)
    o = o * norm_g.astype(f32).reshape(B_HEADS, B_VAL_DIM)
    o = o.reshape(bsz, seq, B_WIDTH) * jax.nn.silu(g_in.astype(f32))
    return o.astype(q.dtype), s_fin.astype(s0.dtype)

def hier_moe(h, w_rg, b_rg, w_re, b_re, w_gate, w_up, w_down):
    f32 = jnp.float32
    g_logits = jnp.einsum('bld,dg->blg', h, w_rg, preferred_element_type=f32) + b_rg.astype(f32)
    g_prob = jax.nn.softmax(g_logits, axis=-1)
    g_idx = jnp.argmax(g_logits, axis=-1)
    p_group = jnp.max(g_prob, axis=-1, keepdims=True)
    e_all = jnp.einsum('bld,gde->blge', h, w_re, preferred_element_type=f32) + b_re.astype(f32)
    e_logits = jnp.einsum('blg,blge->ble', jax.nn.one_hot(g_idx, N_GROUPS, dtype=f32), e_all)
    e_top, e_idx = lax.top_k(e_logits, TOP_K)
    e_w = jax.nn.softmax(e_top, axis=-1) * p_group
    ids = g_idx[..., None] * EXPERTS_PER_GROUP + e_idx
    gates = jnp.sum(jax.nn.one_hot(ids, N_EXPERTS, dtype=f32) * e_w[..., None], axis=-2)
    out = jnp.zeros(h.shape, f32)
    for e in range(N_EXPERTS):
        y = (jax.nn.silu(h @ w_gate[e]) * (h @ w_up[e])) @ w_down[e]
        out = out + gates[..., e:e + 1] * y.astype(f32)
    return out.astype(h.dtype)

def layer(x, k_hist, v_hist, s0, pos0, lb, norm1_g, w_in, attn_sink, hgrn_norm_g, w_o,
          norm2_g, w_rg, b_rg, w_re, b_re, w_gate, w_up, w_down):
    bsz, seq = x.shape[0], x.shape[1]
    h = rmsnorm(x, norm1_g)
    proj = h @ w_in
    o1 = A_WIDTH
    o2 = o1 + A_KV_WIDTH
    o3 = o2 + A_KV_WIDTH
    o4 = o3 + B_KEY_WIDTH
    o5 = o4 + B_KEY_WIDTH
    o6 = o5 + B_WIDTH
    qa, ka, va, qb, fb, ib, gb = jnp.split(proj, [o1, o2, o3, o4, o5, o6], axis=-1)
    att, k_new, v_new = swa_sink_attention(
        qa.reshape(bsz, seq, A_HEADS, A_HEAD_DIM),
        ka.reshape(bsz, seq, A_KV_HEADS, A_HEAD_DIM),
        va.reshape(bsz, seq, A_KV_HEADS, A_HEAD_DIM),
        k_hist, v_hist, pos0, attn_sink)
    rec, s_new = hgrn2(qb, fb, ib, gb, lb, hgrn_norm_g, s0)
    x = x + jnp.concatenate([att, rec], axis=-1) @ w_o
    x = x + hier_moe(rmsnorm(x, norm2_g), w_rg, b_rg, w_re, b_re, w_gate, w_up, w_down)
    return x, k_new, v_new, s_new

def setup_inputs(seed: int = 0) -> dict:
    key = jax.random.key(seed)
    ks = jax.random.split(key, 24)
    f32 = jnp.float32
    w_hist = min(WINDOW, PAST_LEN)
    nrm = lambda k, shape, scale: jax.random.normal(k, shape, f32) * scale
    return {
        "x_prompt": nrm(ks[0], (BATCH, SEQ, D_MODEL), 1.0),
        "x_sample": nrm(ks[1], (DEC_BATCH, DEC_SEQ, D_MODEL), 1.0),
        "cache_k": nrm(ks[2], (DEPTH, DEC_BATCH, w_hist, A_KV_HEADS, A_HEAD_DIM), 1.0),
        "cache_v": nrm(ks[3], (DEPTH, DEC_BATCH, w_hist, A_KV_HEADS, A_HEAD_DIM), 1.0),
        "state_hgrn": nrm(ks[4], (DEPTH, DEC_BATCH, B_HEADS, B_KEY_DIM, B_VAL_DIM), 0.5),
        "norm1_g": 1.0 + nrm(ks[5], (DEPTH, D_MODEL), 0.05),
        "w_in": nrm(ks[6], (DEPTH, D_MODEL, N_IN), D_MODEL ** -0.5),
        "attn_sink": nrm(ks[7], (DEPTH, A_HEADS), 0.5),
        "lower_bounds": nrm(ks[8], (DEPTH + 1, B_KEY_WIDTH), 0.1),
        "hgrn_norm_g": 1.0 + nrm(ks[9], (DEPTH, B_WIDTH), 0.05),
        "w_o": nrm(ks[10], (DEPTH, MIX_WIDTH, D_MODEL), MIX_WIDTH ** -0.5),
        "norm2_g": 1.0 + nrm(ks[11], (DEPTH, D_MODEL), 0.05),
        "w_router_group": nrm(ks[12], (DEPTH, D_MODEL, N_GROUPS), D_MODEL ** -0.5),
        "b_router_group": nrm(ks[13], (DEPTH, N_GROUPS), 0.01),
        "w_router_expert": nrm(ks[14], (DEPTH, N_GROUPS, D_MODEL, EXPERTS_PER_GROUP), D_MODEL ** -0.5),
        "b_router_expert": nrm(ks[15], (DEPTH, N_GROUPS, EXPERTS_PER_GROUP), 0.01),
        "w_gate": nrm(ks[16], (DEPTH, N_EXPERTS, D_MODEL, D_EXPERT), D_MODEL ** -0.5),
        "w_up": nrm(ks[17], (DEPTH, N_EXPERTS, D_MODEL, D_EXPERT), D_MODEL ** -0.5),
        "w_down": nrm(ks[18], (DEPTH, N_EXPERTS, D_EXPERT, D_MODEL), D_EXPERT ** -0.5),
        "final_norm_g": 1.0 + nrm(ks[19], (D_MODEL,), 0.05),
    }

def reference(x_prompt, x_sample, cache_k, cache_v, state_hgrn, norm1_g, w_in, attn_sink,
              lower_bounds, hgrn_norm_g, w_o, norm2_g, w_router_group, b_router_group,
              w_router_expert, b_router_expert, w_gate, w_up, w_down, final_norm_g):
    lbs = jnp.cumsum(jax.nn.softmax(lower_bounds.astype(jnp.float32), axis=0), axis=0)
    bp = x_prompt.shape[0]
    w_hist = cache_k.shape[2]
    yp, ys = x_prompt, x_sample
    kp_l, vp_l, sp_l, ks_l, vs_l, ss_l = [], [], [], [], [], []
    for l in range(DEPTH):
        w = (lbs[l], norm1_g[l], w_in[l], attn_sink[l], hgrn_norm_g[l], w_o[l], norm2_g[l],
             w_router_group[l], b_router_group[l], w_router_expert[l], b_router_expert[l],
             w_gate[l], w_up[l], w_down[l])
        zk = jnp.zeros((bp, w_hist, A_KV_HEADS, A_HEAD_DIM), x_prompt.dtype)
        zs = jnp.zeros((bp, B_HEADS, B_KEY_DIM, B_VAL_DIM), state_hgrn.dtype)
        yp, kp, vp, sp = layer(yp, zk, zk, zs, 0, *w)
        ys, kn, vn, sn = layer(ys, cache_k[l], cache_v[l], state_hgrn[l], PAST_LEN, *w)
        kp_l.append(kp); vp_l.append(vp); sp_l.append(sp)
        ks_l.append(kn); vs_l.append(vn); ss_l.append(sn)
    y_prompt = rmsnorm(yp, final_norm_g)
    y_sample = rmsnorm(ys, final_norm_g)
    return (y_prompt, y_sample, jnp.stack(kp_l), jnp.stack(vp_l), jnp.stack(sp_l),
            jnp.stack(ks_l), jnp.stack(vs_l), jnp.stack(ss_l))


_drawn_inputs = setup_inputs


def setup_inputs(seed=0):
    import zlib

    import numpy as np

    out = dict(_drawn_inputs(seed))
    spreads = {}
    factors = {'attn_sink': 5.756, 'b_router_group': 4.888, 'b_router_expert': 8.0}
    for name, (base, spread) in spreads.items():
        noise = np.random.default_rng([zlib.crc32(name.encode()), seed]).standard_normal(out[name].shape)
        drawn = base * np.exp(spread * noise) if base else spread * noise
        out[name] = __import__('jax').numpy.asarray(drawn.astype(out[name].dtype))
    for name, factor in factors.items():
        out[name] = (out[name] * factor).astype(out[name].dtype)
    return out
```

```python
from contextlib import ExitStack

import numpy as np

import concourse.bass as bass
from concourse import mybir

ALU = mybir.AluOpType
ACT = mybir.ActivationFunctionType
AX = mybir.AxisListType
F32 = mybir.dt.float32
I32 = mybir.dt.int32

P = 128
D = 1024
KC = D // P
SEQ, DEC = 512, 64
TOK = SEQ + DEC
NT = (TOK + P - 1) // P
PROMPT_TILES = SEQ // P
CHUNK = 64
NCHUNK = TOK // CHUNK
WINDOW = 128
HEADS, KV, HD = 8, 2, 64
GROUP = HEADS // KV
KVW = KV * HD
BH, BK = 4, 128
BW = BH * BK
EPS = 1e-6
NG, EPG = 4, 4
NE = NG * EPG
FE = 256
PAIRS = 2 * TOK
MAX_OVER = (PAIRS - NE) // P
MAX_OVER = min(MAX_OVER, PAIRS // (P + 1))
UNROLL = 4
BLOCKS = NE + MAX_OVER
NOWHERE = 4096
TERMS = (TOK - 1) // P
Q0, K0, V0 = 0, 512, 640
QB0, F0, I0, G0 = 768, 1280, 1792, 2304
W_GROUPS = [(F0, BW), (K0, 2 * KVW), (Q0, BW), (I0, BW), (QB0, BW), (G0, BW)]
RING = 3
HALF = TOK // 2


def rows_of(t):
    return min(P, TOK - t * P)


def window(c):
    odd = c % 2
    sample = c == NCHUNK - 1
    lo = CHUNK * odd if sample or c >= 2 else P
    hi = P + CHUNK + CHUNK * odd
    start = SEQ if sample else (c - 2) * CHUNK + lo - CHUNK * odd
    return lo, hi, CHUNK * odd, start


def has_before(c):
    return c >= 2


def v_slots(c):
    return (4, 5) if c == NCHUNK - 1 else (c // 2 - 1, c // 2)


def program(nc, io):
    ctx = ExitStack()
    with ctx:
        def sem(name):
            return ctx.enter_context(nc.semaphore(name))

        def sems(name, n):
            return [sem(f"{name}{i}") for i in range(n)]

        cursor = [(nc.sbuf_base + 63) // 64 * 64]

        def place(name, shape, dt=F32):
            n = int(np.prod(shape[1:])) * 4
            t = nc.alloc_sbuf_tensor_at(name, shape, dt, offset=cursor[0])
            cursor[0] += (n + 31) // 32 * 32
            return t

        x = place("x", [P, NT, D])
        ident = place("ident", [P, P])
        ones = place("ones", [P, P])
        earlier = place("earlier", [P, P])
        decay_m = place("decay_m", [P, 2, P])
        tail_m = place("tail_m", [P, P])
        causal = place("causal", [P, P])
        neghalf = place("neghalf", [P, 8])
        iota4 = place("iota4", [P, 4])
        iota16 = place("iota16", [P, NE])
        iota8 = place("iota8", [P, MAX_OVER])
        pair_id = place("pair_id", [P, 2, NT], I32)
        g2_bc = place("g2_bc", [P, D])
        ng_bc = place("ng_bc", [P, BW])
        w_route = place("w_route", [P, KC, NG + NE])
        b_route = place("b_route", [P, NG + NE])
        sink_bc = place("sink_bc", [P, GROUP])
        stats = place("stats", [P, 6, 8])
        ms = place("ms", [P, 3 * NT + BH * NT])
        ro = place("ro", [P, BH])
        osq = place("osq", [P, BH])
        small = place("small", [P, 8, 2, GROUP])
        logits = place("logits", [P, NT, NG])
        elogits = place("elogits", [P, NT, NE])
        gates = place("gates", [P, 2, NT])
        picks = place("picks", [P, 3, NT, NE])
        rank = place("rank", [P, NT, NE])
        rt = place("rt", [P, 24, NE])
        rb = place("rb", [P, NT, NE])
        place_i = place("place_i", [P, 2, NT], I32)
        steer = place("steer", [P, 2 + MAX_OVER], I32)
        table = place("table", [P, BLOCKS + 1], I32)
        table_tok = place("table_tok", [P, BLOCKS + 1], I32)
        now_tok = place("now_tok", [P, UNROLL, 1], I32)
        now_pair = place("now_pair", [P, UNROLL, 1], I32)
        dec = place("dec", [P, BH, 2])
        kout = place("kout", [P, 2, KVW])

        after_small = cursor[0]
        ring = place("ring", [P, RING, KC, 512])
        mixT = place("mixT", [P, KC, TOK])
        end_small = cursor[0]

        after_weights = cursor[0]
        hT = place("hT", [P, KC, TOK])
        kf = place("kf", [P, NT, BW])
        logf = place("logf", [P, NT, BW])
        gg = place("gg", [P, NT, BW])
        vf = place("vf", [P, NT, BW])
        qf = place("qf", [P, BH, TOK])
        qa = place("qa", [P, GROUP, TOK])
        kT = place("kT", [P, SEQ + WINDOW + DEC])
        V = place("V", [P, 6, KVW])
        bias = place("bias", [P, GROUP, WINDOW + CHUNK])
        qbd = place("qbd", [P, 2, GROUP, P])
        s_at = cursor[0]
        s_buf = place("s_buf", [P, 2, GROUP, 2 * P])
        pt_at = cursor[0]
        pt = place("pt", [P, 2, 2, GROUP * P])
        assert cursor[0] <= nc.sbuf_usable_end, (cursor[0], nc.sbuf_usable_end)
        late = cursor[0]
        hn = s_buf[:, :, :, :].rearrange("p a m k -> p a (m k)")
        h2 = hn
        h2T = pt[:, :, :, :].rearrange("p a b k -> p a (b k)")
        g1_bc = pt[:, 0, :, :].rearrange("p b k -> p (b k)")
        mix_flat = mixT[:, :, :].rearrange("p k t -> p (k t)")
        lb_bc = mix_flat[:, 0:2 * BW]
        lb = lb_bc[:, 0:BW]
        oml = lb_bc[:, BW:2 * BW]
        lb_t = mix_flat[:, 2 * BW:4 * BW]
        junk = mix_flat[:, 4 * BW:4 * BW + D]
        hT_flat = hT[:, :, :].rearrange("p k t -> p (k t)")
        hb = [hT_flat[:, i * BW:(i + 1) * BW].rearrange("p (h t) -> p h t", h=BH) for i in range(5)]
        qin, kin, qex, aT, kdec = hb
        rec = hT_flat[:, 5 * BW:6 * BW]
        St = [hT_flat[:, (6 + i) * BW:(7 + i) * BW] for i in range(3)]
        qa_flat = qa[:, :, :].rearrange("p m t -> p (m t)")
        s_sample = qa_flat[:, D:D + BW]

        cursor[0] = after_small
        xg = place("xg", [P, 2, D])
        xT = place("xT", [P, KC, P])
        y = place("y", [P, 2, D])
        sg = place("sg", [P, FE])
        hh = place("hh", [P, FE])
        hhT = place("hhT", [P, 2, P])
        pair = place("pair", [P, 2, 2 * D])
        outb = place("outb", [P, 2, D])
        gf_bc = place("gf_bc", [P, D])
        assert cursor[0] <= end_small
        cursor[0] = after_weights
        we_gu = [place(f"we_gu{i}", [P, KC, 2 * FE]) for i in range(UNROLL)]
        we_d = [place(f"we_d{i}", [P, 2, D]) for i in range(UNROLL)]
        assert cursor[0] <= late

        ps = ctx.enter_context(nc.psum_tensor("ps", [P, 8, 512], F32))

        h2_dram = nc.dram_tensor("h2_rows", (TOK, D), F32, kind="Internal").ap()
        y_dram = nc.dram_tensor("y_pairs", (PAIRS, D), F32, kind="Internal").ap()
        slots_dram = nc.dram_tensor("slots", ((BLOCKS + 1) * P, 1), I32, kind="Internal").ap()

        x_in = sems("x_in", NT)
        g1_in, lb_in, ng_in, sink_in, route_in = (sem(n) for n in ("g1_in", "lb_in", "ng_in", "sink_in", "route_in"))
        g2_in, gf_in, ck_in, cv_in, s_in, table_in = (sem(n) for n in ("g2_in", "gf_in", "ck_in", "cv_in", "s_in", "table_in"))
        w_in = sems("w_in", len(W_GROUPS) + 2)
        consts, consts_chain, bias_ready = sem("consts"), sem("consts_chain"), sem("bias_ready")
        dve_chain, pool_chain, dve_consts = sem("dve_chain"), sem("pool_chain"), sem("dve_consts")
        ssq_ready, rstd_ready, hn_ready, turned, hT_act, hT_dve = (
            sem(n) for n in ("ssq_ready", "rstd_ready", "hn_ready", "turned", "hT_act", "hT_dve"))
        proj_ready, proj_act, proj_dve = (sem(n) for n in ("proj_ready", "proj_act", "proj_dve"))
        f_ready, f_freed, logf_ready, oml_ready = sem("f_ready"), sem("f_freed"), sem("logf_ready"), sem("oml_ready")
        lb_exp, lb_diff = sem("lb_exp"), sem("lb_diff")
        cache_turned, cache_taken, qf_ready, gg_ready = (
            sem(n) for n in ("cache_turned", "cache_taken", "qf_ready", "gg_ready"))
        qbd_ready, scores_ready, scores_taken, negm_ready, exp_done, p_ready = (
            sem(n) for n in ("qbd_ready", "scores_ready", "scores_taken", "negm_ready", "exp_done", "p_ready"))
        p_turned, pt_act, pt_dve, pv_done, o_taken = (
            sem(n) for n in ("p_turned", "pt_act", "pt_dve", "pv_done", "o_taken"))
        kout_turned, kout_ready = sem("kout_turned"), sem("kout_ready")
        cum_ready, cum_exp, hops_ready, inner_ready, at_ready, state_ready = (
            sem(n) for n in ("cum_ready", "cum_exp", "hops_ready", "inner_ready", "at_ready", "state_ready"))
        rec_sum, osq_ready, ro_ready, rec_ready, rec_turned, rec_taken = (
            sem(n) for n in ("rec_sum", "osq_ready", "ro_ready", "rec_ready", "rec_turned", "rec_taken"))
        out_ready, x2_ready, ssq2_ready, rstd2_ready, h2_ready = (
            sem(n) for n in ("out_ready", "x2_ready", "ssq2_ready", "rstd2_ready", "h2_ready"))
        h2_stored = sems("h2_stored", NT)
        h2_turned, h2T_act, h2T_dve, logits_ready, logits_taken = (
            sem(n) for n in ("h2_turned", "h2T_act", "h2T_dve", "logits_ready", "logits_taken"))
        route_diff, route_exp, picks_ready, rank_ready, places_ready, slots_cleared, slots_written = (
            sem(n) for n in ("route_diff", "route_exp", "picks_ready", "rank_ready", "places_ready",
                             "slots_cleared", "slots_written"))
        table_ready, steer_ready, xg_clear = sem("table_ready"), sem("steer_ready"), sem("xg_clear")
        expert_in = sems("expert_in", UNROLL)
        gathered, stored = sems("gathered", 2), sems("stored", 2)
        col_copied, dma_cleared = sem("col_copied"), sem("dma_cleared")
        x_turned, xT_act, xT_dve, gu_ready, silu_ready, hh_ready = (
            sem(n) for n in ("x_turned", "xT_act", "xT_dve", "gu_ready", "silu_ready", "hh_ready"))
        hh_turned, hhT_ready, y_ready, y_act, y_dve = (
            sem(n) for n in ("hh_turned", "hhT_ready", "y_ready", "y_act", "y_dve"))
        pair_in = sems("pair_in", 2)
        sum_ready, ssq3_ready, rstd3_ready, final_ready = (
            sem(n) for n in ("sum_ready", "ssq3_ready", "rstd3_ready", "final_ready"))
        out_stored = sem("out_stored")

        groups = []
        for t in range(NT):
            groups.append(("f", t, "act"))
        groups += [("k", 0, "dve"), ("k", 1, "dve")]
        groups += [("v", t, "act") for t in range(NT)]
        groups += [("q", i, "act" if i % 2 else "dve") for i in range(2 * GROUP)]
        first_filler = len(groups)
        groups += [("i", t, "act") for t in range(NT)]
        groups += [("b", i, "dve") for i in range(2 * BH)]
        groups += [("g", t, "act") for t in range(NT)]
        ring_of = {"f": 0, "k": 1, "v": 1, "q": 2, "i": 3, "b": 4, "g": 5}
        emptied = {}
        count = {"act": 0, "dve": 0}
        for n, (_, _, who) in enumerate(groups):
            count[who] += 1
            emptied[n] = (who, count[who])
        last_of = {}
        for n, (kind, _, _) in enumerate(groups):
            last_of[ring_of[kind]] = n
        of_kind = {kind: [n for n, g in enumerate(groups) if g[0] == kind] for kind in ring_of}

        def wait_emptied(eng, kinds):
            for who, s in (("act", proj_act), ("dve", proj_dve)):
                last = [emptied[n][1] for k in kinds for n in of_kind[k] if emptied[n][0] == who]
                if last:
                    eng.wait_ge(s, max(last))

        slots = [[n] for n in of_kind["i"]] + [of_kind["b"][2 * m:2 * m + 2] for m in range(BH)] + \
                [[n] for n in of_kind["g"]]
        assert len(slots) >= NCHUNK + 2

        def w_slot(k):
            return ring[:, k % RING, :, :]

        def bank(b, n=512):
            return ps[:, b, 0:n]

        def tok(t):
            return slice(t * P, t * P + rows_of(t))

        block = ctx.enter_context(nc.Block())

        @block.sync
        def _(sp):
            def store_out(t):
                sp.wait_ge(final_ready, t + 1)
                dst = io["y_p"][tok(t), :] if t < PROMPT_TILES else io["y_s"]
                sp.dma_start(dst, outb[0:rows_of(t), t % 2, :]).then_inc(out_stored, 16)

            def w_group(k):
                if k < len(W_GROUPS) and W_GROUPS[k][0] == Q0:
                    src = io["w_in"][:, Q0:Q0 + BW].rearrange("(c p) (b m d) -> p b c m d", p=P, b=KV, m=GROUP)
                    dst = w_slot(k)[:, :, :].rearrange("p c (m b d) -> p b c m d", b=KV, m=GROUP)
                    for b in range(KV):
                        for c in range(KC):
                            sp.dma_start(dst[:, b, c, :, :], src[:, b, c, :, :]).then_inc(w_in[k], 16)
                elif k < len(W_GROUPS):
                    a, n = W_GROUPS[k]
                    sp.dma_start(w_slot(k)[:, :, 0:n],
                                 io["w_in"][:, a:a + n].rearrange("(c p) n -> p c n", p=P)).then_inc(w_in[k], 16)
                else:
                    cols = slice(512 * (k - len(W_GROUPS)), 512 * (k - len(W_GROUPS)) + 512)
                    att = io["w_o"][0:HEADS * HD, cols].rearrange("(b m d) n -> b d m n", b=KV, m=GROUP)
                    for b in range(KV):
                        sp.dma_start(w_slot(k)[b * HD:(b + 1) * HD, 0:GROUP, :], att[b]).then_inc(w_in[k], 16)
                    sp.dma_start(w_slot(k)[:, GROUP:KC, :],
                                 io["w_o"][HEADS * HD:, cols].rearrange("(h p) n -> p h n", p=P)).then_inc(w_in[k], 16)

            w_group(0)
            w_group(1)
            w_group(2)
            sp.dma_start(kout[:, 0, :], io["cache_k"]).then_inc(ck_in, 16)
            sp.dma_start(V[:, 4, :], io["cache_v"]).then_inc(cv_in, 16)
            sp.dma_start(io["k_win_s"][0:CHUNK, :], io["cache_k"][CHUNK:WINDOW, :]).then_inc(out_stored, 16)
            sp.dma_start(io["v_win_s"][0:CHUNK, :], io["cache_v"][CHUNK:WINDOW, :]).then_inc(out_stored, 16)
            sp.wait_ge(slots_cleared, 1)
            sp.dma_start(slots_dram.rearrange("(p b) o -> p (b o)", p=P), table[:, :]).then_inc(slots_cleared, 16)
            for k in range(RING, len(W_GROUPS) + 2):
                sp.wait_ge(proj_ready, last_of[k - RING] + 1)
                w_group(k)
                if k == 4:
                    wait_emptied(sp, "v")
                    sp.dma_start(io["v_win_p"], V[:, PROMPT_TILES - 1, :]).then_inc(out_stored, 16)
                    sp.dma_start(io["v_win_s"][CHUNK:WINDOW, :], V[0:DEC, 5, :]).then_inc(out_stored, 16)
            sp.wait_ge(kout_ready, 1)
            sp.dma_start(io["k_win_p"], kout[:, 0, :]).then_inc(out_stored, 16)
            sp.dma_start(io["k_win_s"][CHUNK:WINDOW, :], kout[0:DEC, 1, :]).then_inc(out_stored, 16)
            sp.dma_start(s_sample[:, :].rearrange("k (h v) -> k h v", h=BH),
                         io["state"].rearrange("h k v -> k h v")).then_inc(s_in, 16)
            for t in range(NT):
                if t == PROMPT_TILES - 1:
                    sp.wait_ge(state_ready, 2 * PROMPT_TILES)
                    sp.dma_start(io["state_p"].rearrange("h k v -> k h v"),
                                 St[2 * PROMPT_TILES % 3].rearrange("k (h v) -> k h v", h=BH)).then_inc(out_stored, 16)
                if t == NT - 1:
                    sp.wait_ge(state_ready, 2 * PROMPT_TILES + 1)
                    sp.dma_start(io["state_s"].rearrange("h k v -> k h v"),
                                 St[0].rearrange("k (h v) -> k h v", h=BH)).then_inc(out_stored, 16)
                sp.wait_ge(h2_ready, t + 1)
                sp.dma_start(h2_dram[tok(t), :], h2[0:rows_of(t), t % 2, :]).then_inc(h2_stored[t], 16)

            def expert(slot, e):
                gate, up = (we_gu[slot][:, :, i * FE:(i + 1) * FE] for i in range(2))
                for dst, src in ((gate, io["w_gate"]), (up, io["w_up"]), (we_d[slot], io["w_down"])):
                    v = src[bass.ds(e, 1), :, :] if not isinstance(e, int) else src[e:e + 1, :, :]
                    sp.dma_start(dst[:, :, :] if dst is we_d[slot] else dst,
                                 v.rearrange("e (c p) n -> p (e c) n", p=P)).then_inc(expert_in[slot], 16)

            sp.wait_ge(out_stored, 16 * 8)
            sp.wait_ge(rec_taken, NT)
            sp.wait_ge(h2T_act, NT)
            sp.wait_ge(h2T_dve, NT)
            for t in range(NT):
                sp.wait_ge(h2_stored[t], 16)
            for slot in range(UNROLL):
                expert(slot, slot)
            sp.wait_ge(out_ready, 2 * NT)
            sp.dma_start(gf_bc[:, :], io["gf"].partition_broadcast(P)).then_inc(gf_in, 16)
            sp.wait_ge(slots_written, 16 * 2 * (NT - 1))
            for par in range(2):
                sp.wait_ge(stored[par], 16)
            sp.dma_start(table[:, :], slots_dram.rearrange("(p b) o -> p (b o)", p=P)).then_inc(table_in, 16)
            with sp.Fori(1, NE // UNROLL) as i:
                for slot in range(UNROLL):
                    sp.wait_ge(y_ready, UNROLL * (i - 1) + slot + 1)
                    expert(slot, UNROLL * i + slot)
            sp.wait_ge(steer_ready, 1)
            turns = sp.value_load(steer[0:1, 0:1], min_val=NE // UNROLL, max_val=BLOCKS // UNROLL)
            with sp.If(turns > NE // UNROLL):
                with sp.Fori(0, turns - NE // UNROLL) as i:
                    for slot in range(UNROLL):
                        sp.wait_ge(y_ready, NE - UNROLL + UNROLL * i + slot + 1)
                        e = sp.value_load(steer[0:1, bass.ds(UNROLL * i + slot + 1, 1)], min_val=0, max_val=NE - 1)
                        expert(slot, e)
            for par in range(2):
                sp.wait_ge(stored[par], 8 * UNROLL * turns + 16)
            pairs = y_dram.rearrange("(t a) d -> t (a d)", a=2)
            for t in range(NT):
                if t >= 2:
                    sp.wait_ge(sum_ready, 2 * (t - 1))
                sp.dma_start(pair[0:rows_of(t), t % 2, :], pairs[tok(t), :]).then_inc(pair_in[t % 2], 16)
                if t >= 1:
                    store_out(t - 1)
            store_out(NT - 1)
            sp.wait_ge(out_stored, 16 * (8 + NT))

        @block.gpsimd
        def _(pool):
            done = [0]

            def chain(ins):
                done[0] += 1
                ins.then_inc(pool_chain, 1)
                pool.wait_ge(pool_chain, done[0])

            used = [0]
            chain(pool.memset(neghalf[:, :], -0.5))
            chain(pool.memset(ident[:, :], 0.0))
            pool.affine_select(out=ident[:, :], in_=ident[:, :], compare_op=ALU.not_equal, fill=1.0, base=0,
                               pattern=[[-1, P]], channel_multiplier=1).then_inc(consts, 1)

            def rstd(which, t, n, scale, waited, signal, src=None, dst=None, rows=P):
                pool.wait_ge(waited, t + 1)
                src = stats[:, which, t:t + 1] if src is None else src
                dst = stats[:, which + 3, t:t + 1] if dst is None else dst
                at = used[0]
                used[0] += n
                chain(pool.tensor_scalar(ms[0:rows, at:at + n], src[0:rows], scale, EPS, ALU.mult, ALU.add))
                pool.tensor_tensor(dst[0:rows], ms[0:rows, at:at + n], neghalf[0:rows, 0:n], ALU.pow).then_inc(signal, 1)

            rstd(0, 0, 1, 1.0 / D, ssq_ready, rstd_ready)
            rstd(0, 1, 1, 1.0 / D, ssq_ready, rstd_ready)
            chain(pool.memset(causal[:, :], 1.0))
            chain(pool.affine_select(out=causal[:, :], in_=causal[:, :], compare_op=ALU.is_ge, fill=0.0,
                                     base=0, pattern=[[1, P]], channel_multiplier=-1))
            chain(pool.memset(causal[0:CHUNK, CHUNK:P], 0.0))
            chain(pool.memset(decay_m[:, 0, :], 0.0))
            for c in range(2):
                part = decay_m[c * CHUNK:(c + 1) * CHUNK, 0, c * CHUNK:(c + 1) * CHUNK]
                chain(pool.memset(part, 1.0))
                chain(pool.affine_select(out=part, in_=part, compare_op=ALU.is_ge, fill=0.0, base=CHUNK // 2,
                                         pattern=[[0, CHUNK]], channel_multiplier=-1))
            chain(pool.tensor_tensor(decay_m[:, 0, :], causal[:, :], decay_m[:, 0, :], ALU.subtract))
            chain(pool.tensor_copy(decay_m[:, 1, :], causal[:, :]))
            chain(pool.memset(tail_m[:, :], 1.0))
            chain(pool.affine_select(out=tail_m[:, :], in_=tail_m[:, :], compare_op=ALU.is_ge, fill=0.0, base=-1,
                                     pattern=[[-1, P]], channel_multiplier=1))
            chain(pool.memset(tail_m[CHUNK:P, 0:CHUNK], 0.0))
            chain(pool.memset(ones[:, :], 1.0))
            chain(pool.affine_select(out=earlier[:, :], in_=ones[:, :], compare_op=ALU.is_ge, fill=0.0, base=-1,
                                     pattern=[[1, P]], channel_multiplier=-1))
            chain(pool.memset(qbd[:, :, :, :], 0.0))
            for t in range(2, NT):
                rstd(0, t, 1, 1.0 / D, ssq_ready, rstd_ready, rows=rows_of(t))
            base = rt[:, :, :].rearrange("p a b -> p (a b)")[:, 0:WINDOW + CHUNK]
            for b in range(KV):
                chain(pool.iota(base[b * CHUNK:(b + 1) * CHUNK, :], pattern=[[-1, WINDOW + CHUNK]], base=WINDOW,
                                channel_multiplier=1, allow_small_or_imprecise_dtypes=True))
            chain(pool.tensor_scalar(bias[:, 0, :], base, 0.0, None, ALU.min))
            chain(pool.tensor_scalar(base, base, 0.0, None, ALU.max))
            chain(pool.tensor_tensor(base, base, bias[:, 0, :], ALU.subtract))
            for b in range(KV):
                for m in range(GROUP):
                    slope = 2.0 ** (-8.0 * (m + GROUP * b + 1) / HEADS)
                    rows = slice(b * CHUNK, (b + 1) * CHUNK)
                    chain(pool.tensor_scalar(bias[rows, m, :], base[rows, :], -slope, None, ALU.mult))
            pool.sem_inc(bias_ready, 1)
            pool.memset(table[:, :], NOWHERE).then_inc(slots_cleared, 1)
            for out, n, k in ((iota4, 4, 1), (iota16, NE, 1), (iota8, MAX_OVER, 1)):
                chain(pool.iota(out[:, :], pattern=[[k, n]], base=0, channel_multiplier=0,
                                allow_small_or_imprecise_dtypes=True))
            pool.iota(pair_id[:, :, :], pattern=[[1, 2], [2 * P, NT]], base=0,
                      channel_multiplier=2).then_inc(consts, 1)

            wait_emptied(pool, "q")
            for c in range(NCHUNK):
                if c >= 2:
                    pool.wait_ge(scores_ready, c - 1)
                for b in range(KV):
                    rows = slice(b * HD, (b + 1) * HD)
                    pool.tensor_copy(qbd[rows, c % 2, :, b * CHUNK:(b + 1) * CHUNK],
                                     qa[rows, :, c * CHUNK:(c + 1) * CHUNK]).then_inc(qbd_ready, 1)
                    pool.wait_ge(qbd_ready, KV * c + b + 1)

            for t in range(NT):
                if t:
                    rstd(1, t - 1, 1, 1.0 / D, ssq2_ready, rstd2_ready)
                rstd(0, t, BH, 1.0 / BK, osq_ready, ro_ready, osq[:, :], ro[:, :], rows_of(t))
            rstd(1, NT - 1, 1, 1.0 / D, ssq2_ready, rstd2_ready, rows=rows_of(NT - 1))

            pool.wait_ge(out_ready, 2 * NT)
            pool.memset(xg[:, :, :], 0.0).then_inc(xg_clear, 1)
            pool.wait_ge(slots_cleared, 17)
            pool.wait_ge(places_ready, 2)
            for t in range(NT):
                for i in range(2):
                    r = rows_of(t)
                    pool.indirect_dma_start(
                        slots_dram, bass.IndirectOffsetOnAxis(ap=place_i[0:r, i, t:t + 1], axis=0),
                        pair_id[0:r, i, t:t + 1], None).then_inc(slots_written if t < NT - 1 else stored[i], 16)

            pool.wait_ge(table_ready, 1)
            pool.wait_ge(xg_clear, 1)
            for t in range(NT):
                pool.wait_ge(h2_stored[t], 16)

            def gather(s, slot, copies):
                pool.tensor_copy(now_tok[:, slot, :], table_tok[:, bass.ds(s, 1)]).then_inc(col_copied, 1)
                pool.wait_ge(col_copied, copies)
                if not isinstance(s, int):
                    pool.wait_ge(x_turned, s - 1 if slot != 1 else s)
                    pool.sem_inc(dma_cleared, 1)
                pool.indirect_dma_start(
                    xg[:, slot % 2, :], None, h2_dram, bass.IndirectOffsetOnAxis(ap=now_tok[:, slot, :], axis=0),
                    bounds_check=TOK - 1, oob_is_err=False).then_inc(gathered[slot % 2], 16)

            gather(0, 0, 1)
            pool.wait_ge(steer_ready, 1)
            turns = pool.value_load(steer[0:1, 0:1], min_val=NE // UNROLL, max_val=BLOCKS // UNROLL)
            with pool.Fori(0, turns) as i:
                for slot in range(UNROLL):
                    s = UNROLL * i + slot
                    gather(s + 1, (slot + 1) % UNROLL, 2 * s + 2)
                    pool.tensor_copy(now_pair[:, slot, :], table[:, bass.ds(s, 1)]).then_inc(col_copied, 1)
                    pool.wait_ge(col_copied, 2 * s + 3)
                    pool.wait_ge(y_act, s + 2)
                    pool.wait_ge(y_dve, s + 2)
                    pool.sem_inc(dma_cleared, 1)
                    pool.indirect_dma_start(
                        y_dram, bass.IndirectOffsetOnAxis(ap=now_pair[:, slot, :], axis=0),
                        y[:, slot % 2, :], None, bounds_check=PAIRS - 1, oob_is_err=False).then_inc(
                            stored[slot % 2], 16)

            for t in range(NT):
                rstd(2, t, 1, 1.0 / D, ssq3_ready, rstd3_ready, rows=rows_of(t))

        @block.scalar
        def _(act):
            for t in range(NT):
                src = io["x_p"][tok(t), :] if t < PROMPT_TILES else io["x_s"]
                act.dma_start(x[0:rows_of(t), t, :], src).then_inc(x_in[t], 16)
                if t == 0:
                    act.dma_start(g1_bc, io["g1"].partition_broadcast(P)).then_inc(g1_in, 16)
            act.dma_start(lb_t[:, :], io["lower"].rearrange("a k -> (a k)").partition_broadcast(P)).then_inc(lb_in, 16)
            for b in range(KV):
                act.dma_start(sink_bc[b * CHUNK:(b + 1) * CHUNK, :],
                              io["sink"][b * GROUP:(b + 1) * GROUP].partition_broadcast(CHUNK)).then_inc(sink_in, 16)
            act.dma_start(ng_bc[:, :], io["ng"].partition_broadcast(P)).then_inc(ng_in, 16)
            act.dma_start(g2_bc[:, :], io["g2"].partition_broadcast(P)).then_inc(g2_in, 16)
            act.dma_start(w_route[:, :, 0:NG], io["w_rg"].rearrange("(c p) g -> p c g", p=P)).then_inc(route_in, 16)
            for g in range(NG):
                act.dma_start(w_route[:, :, NG + g * EPG:NG + (g + 1) * EPG],
                              io["w_re"][g].rearrange("(c p) e -> p c e", p=P)).then_inc(route_in, 16)
            act.dma_start(b_route[:, 0:NG], io["b_rg"].partition_broadcast(P)).then_inc(route_in, 16)
            act.dma_start(b_route[:, NG:NG + NE], io["b_re"].rearrange("g e -> (g e)").partition_broadcast(P)).then_inc(
                route_in, 16)

            def square_sum(t, which, signal):
                r = rows_of(t)
                if t:
                    act.wait_ge(signal, t)
                act.activation(junk[0:r, :], x[0:r, t, :], ACT.Square,
                               accum_out=stats[0:r, which, t:t + 1]).then_inc(signal, 1)

            def hT_half(t):
                act.wait_ge(turned, t + 1)
                r = rows_of(t)
                act.activation(hT[:, 0:4, tok(t)], bank(2 + 2 * (t % 3)).rearrange("p (c t) -> p c t", c=4)[:, :, 0:r],
                               ACT.Copy).then_inc(hT_act, 1)

            for t in range(2):
                act.wait_ge(x_in[t], 16)
                square_sum(t, 0, ssq_ready)
            act.wait_ge(lb_diff, 1)
            act.activation(lb_t[:, :], lb_t[:, :], ACT.Exp).then_inc(lb_exp, 1)
            for t in range(2, NT):
                act.wait_ge(x_in[t], 16)
                square_sum(t, 0, ssq_ready)
                hT_half(t - 2)
            hT_half(NT - 2)
            hT_half(NT - 1)

            def empty(n):
                kind, t, _ = groups[n]
                act.wait_ge(proj_ready, n + 1)
                b = n % 2
                if kind == "f":
                    ins = act.activation(logf[0:rows_of(t), t, :], ps[0:rows_of(t), b, :], ACT.Sigmoid)
                elif kind == "v":
                    slot = t if t < PROMPT_TILES else 5
                    ins = act.activation(V[0:rows_of(t), slot, :], ps[0:rows_of(t), b, 0:KVW], ACT.Copy)
                elif kind == "q":
                    ins = act.activation(qa[:, t // 2, t % 2 * HALF:(t % 2 + 1) * HALF], bank(b, HALF), ACT.Copy,
                                         scale=float(HD) ** -0.5)
                elif kind == "i":
                    ins = act.activation(vf[0:rows_of(t), t, :], ps[0:rows_of(t), b, :], ACT.Copy)
                else:
                    ins = act.activation(gg[0:rows_of(t), t, :], ps[0:rows_of(t), b, :], ACT.Silu)
                ins.then_inc(proj_act, 1)

            for n in range(first_filler):
                if groups[n][2] == "act":
                    empty(n)
                if groups[n][0] == "k" and groups[n][1] == 1:
                    for t in range(NT):
                        act.wait_ge(f_ready, t + 1)
                        act.activation(logf[0:rows_of(t), t, :], logf[0:rows_of(t), t, :], ACT.Ln).then_inc(logf_ready, 1)

            def exps(c):
                lo, hi, _, _ = window(c)
                par = c % 2
                act.wait_ge(negm_ready, c + 1)
                act.activation(small[:, 3, par, :], small[:, 2, par, :], ACT.Exp)
                for m in range(GROUP):
                    last = act.activation(s_buf[:, par, m, lo:hi], s_buf[:, par, m, lo:hi], ACT.Exp,
                                          bias=small[:, 1, par, m:m + 1], accum_out=small[:, 4, par, m:m + 1])
                last.then_inc(exp_done, 1)

            def pt_before(c):
                act.wait_ge(p_turned, c + 1)
                act.wait_ge(pv_done, c - 1)
                act.activation(pt[:, c % 2, 0, :], bank(4), ACT.Copy).then_inc(pt_act, 1)

            for s, fill in enumerate(slots):
                if s == NCHUNK:
                    wait_emptied(act, "b")
                    act.activation(qf[:, :, :], qf[:, :, :], ACT.Silu).then_inc(qf_ready, 1)
                for n in fill:
                    if groups[n][2] == "act":
                        empty(n)
                if has_before(s - 1) and s - 1 < NCHUNK:
                    pt_before(s - 1)
                if s < NCHUNK:
                    exps(s)

            def cum_exps(t):
                r = rows_of(t)
                act.wait_ge(cum_ready, t + 1)
                if t:
                    act.wait_ge(rec_sum, t)
                cums = ps[:, 2:4, :].rearrange("p b (h w t) -> p (b h) w t", h=2, w=2)
                act.activation(qin[:, :, 0:r], cums[:, :, 0, 0:r], ACT.Exp).then_inc(cum_exp, 1)
                act.activation(kin[:, :, 0:r], cums[:, :, 0, 0:r], ACT.Exp, scale=-1.0).then_inc(cum_exp, 1)
                act.activation(qex[:, :, 0:r], cums[:, :, 1, 0:r], ACT.Exp).then_inc(cum_exp, 1)
                act.activation(kdec[0:r, :, :], ps[0:r, 5, :].rearrange("p (h k) -> p h k", h=BH),
                               ACT.Exp).then_inc(cum_exp, 1)

            def second_norm(t):
                act.wait_ge(x2_ready, 2 * t + 2)
                r = rows_of(t)
                act.activation(qa_flat[0:r, 0:D], x[0:r, t, :], ACT.Square,
                               accum_out=stats[0:r, 1, t:t + 1]).then_inc(ssq2_ready, 1)

            def h2T_half(t):
                act.wait_ge(h2_turned, t + 1)
                act.activation(h2T[:, t % 2, 0:512], bank(2), ACT.Copy).then_inc(h2T_act, 1)

            for t in range(NT):
                r = rows_of(t)
                cum_exps(t)
                if t:
                    second_norm(t - 1)
                act.wait_ge(rec_sum, t + 1)
                for h in range(BH):
                    cols = slice(h * BK, (h + 1) * BK)
                    last = act.activation(logf[0:r, t, cols], ps[0:r, 5, cols], ACT.Square,
                                          accum_out=osq[0:r, h:h + 1])
                last.then_inc(osq_ready, 1)
                act.wait_ge(rec_turned, t + 1)
                act.activation(mixT[:, BH:KC, tok(t)], bank(6).rearrange("p (h t) -> p h t", h=BH)[:, :, 0:r],
                               ACT.Copy).then_inc(rec_taken, 1)
                if t:
                    h2T_half(t - 1)
            second_norm(NT - 1)
            h2T_half(NT - 1)

            for k in range(2):
                act.wait_ge(route_diff, k + 1)
                act.activation(rb[:, :, 0:4] if k == 0 else rb[:, :, 4:5],
                               rb[:, :, 0:4] if k == 0 else rb[:, :, 4:5], ACT.Exp).then_inc(route_exp, 1)

            def x_half(s):
                act.wait_ge(x_turned, s + 1)
                act.activation(xT[:, 0:4, :], bank(1).rearrange("p (c t) -> p c t", c=4), ACT.Copy).then_inc(xT_act, 1)

            x_half(0)
            act.sem_inc(y_act, 1)
            act.wait_ge(steer_ready, 1)
            turns = act.value_load(steer[0:1, 0:1], min_val=NE // UNROLL, max_val=BLOCKS // UNROLL)
            with act.Fori(0, turns) as i:
                for slot in range(UNROLL):
                    s = UNROLL * i + slot
                    act.wait_ge(gu_ready, s + 1)
                    act.activation(sg[:, :], ps[:, 0, 0:FE], ACT.Silu).then_inc(silu_ready, 1)
                    x_half(s + 1)
                    act.wait_ge(y_ready, s + 1)
                    act.wait_ge(stored[slot % 2], 16 * (2 * i + slot // 2 + 1))
                    act.activation(y[:, slot % 2, 0:512], bank(4), ACT.Copy).then_inc(y_act, 1)

            for t in range(NT):
                r = rows_of(t)
                act.wait_ge(sum_ready, 2 * t + 2)
                if t:
                    act.wait_ge(ssq3_ready, t)
                act.activation(xT[0:r, :, :].rearrange("p c t -> p (c t)"), x[0:r, t, :], ACT.Square,
                               accum_out=stats[0:r, 2, t:t + 1]).then_inc(ssq3_ready, 1)

        @block.vector
        def _(dve):
            done = [0]

            def chain(ins):
                done[0] += 1
                ins.then_inc(dve_chain, 1)
                dve.wait_ge(dve_chain, done[0])

            def h_tile(t):
                dve.wait_ge(rstd_ready, t + 1)
                if t >= 2:
                    dve.wait_ge(turned, t - 1)
                r = rows_of(t)
                dve.scalar_tensor_tensor(hn[0:r, t % 2, :], x[0:r, t, :], stats[0:r, 3, t:t + 1], g1_bc[0:r, :],
                                         ALU.mult, ALU.mult).then_inc(hn_ready, 1)

            def hT_half(t):
                dve.wait_ge(turned, t + 1)
                r = rows_of(t)
                dve.tensor_copy(hT[:, 4:8, tok(t)],
                                bank(3 + 2 * (t % 3)).rearrange("p (c t) -> p c t", c=4)[:, :, 0:r]).then_inc(hT_dve, 1)

            dve.wait_ge(g1_in, 16)
            h_tile(0)
            h_tile(1)
            hT_half(0)
            dve.wait_ge(lb_in, 16)
            l0, l1 = lb_t[:, 0:BW], lb_t[:, BW:2 * BW]
            chain(dve.tensor_tensor(lb, l0, l1, ALU.max))
            chain(dve.tensor_tensor(l0, l0, lb, ALU.subtract))
            dve.tensor_tensor(l1, l1, lb, ALU.subtract).then_inc(lb_diff, 1)
            for t in range(2, NT):
                h_tile(t)
                hT_half(t - 1)
            hT_half(NT - 1)
            dve.wait_ge(lb_exp, 1)
            chain(dve.tensor_tensor(oml, l0, l1, ALU.add))
            chain(dve.reciprocal(oml, oml))
            chain(dve.tensor_tensor(lb, l0, oml, ALU.mult))
            chain(dve.tensor_scalar(oml, lb, -1.0, 1.0, ALU.mult, ALU.add))

            def gate_f(t):
                r = rows_of(t)
                dve.wait_ge(proj_act, t + 1)
                chain(dve.tensor_tensor(logf[0:r, t, :], logf[0:r, t, :], oml[0:r, :], ALU.mult))
                chain(dve.tensor_tensor(logf[0:r, t, :], logf[0:r, t, :], lb[0:r, :], ALU.add))
                dve.tensor_scalar(kf[0:r, t, :], logf[0:r, t, :], -1.0, 1.0, ALU.mult, ALU.add).then_inc(f_ready, 1)

            def empty(n):
                kind, i, _ = groups[n]
                dve.wait_ge(proj_ready, n + 1)
                b = n % 2
                if kind == "k":
                    if i == 0:
                        ins = dve.tensor_copy(kT[:, 0:HALF], bank(b, HALF))
                    else:
                        dve.tensor_copy(kT[:, HALF:SEQ], ps[:, b, 0:SEQ - HALF])
                        ins = dve.tensor_copy(kT[:, SEQ + WINDOW:], ps[:, b, SEQ - HALF:HALF])
                elif kind == "q":
                    ins = dve.tensor_scalar(qa[:, i // 2, i % 2 * HALF:(i % 2 + 1) * HALF], bank(b, HALF),
                                            float(HD) ** -0.5, None, ALU.mult)
                else:
                    ins = dve.tensor_copy(qf[:, i // 2, i % 2 * HALF:(i % 2 + 1) * HALF], bank(b, HALF))
                ins.then_inc(proj_dve, 1)

            for t in range(NT):
                gate_f(t)
            dve.memset(s_buf[:, 1, :, 0:CHUNK], 0.0).then_inc(dve_consts, 1)
            dve.wait_ge(cache_turned, 1)
            dve.tensor_copy(kT[:, SEQ:SEQ + WINDOW], ps[:, 7, 0:P]).then_inc(cache_taken, 1)
            for n in range(first_filler):
                if groups[n][2] == "dve":
                    empty(n)

            def softmax_head(c):
                lo, hi, off, _ = window(c)
                par = c % 2
                dve.wait_ge(scores_ready, c + 1)
                if c == 0:
                    dve.wait_ge(bias_ready, 1)
                    dve.wait_ge(sink_in, 32)
                dve.tensor_tensor(s_buf[:, par, :, lo:hi],
                                  ps[:, 2:4, :].rearrange("p b (m k) -> p (b m) k", m=2)[:, :, lo:hi],
                                  bias[:, :, lo - off:hi - off], ALU.add).then_inc(scores_taken, 1)
                dve.wait_ge(scores_taken, c + 1)
                chain(dve.tensor_reduce(small[:, 0, par, :], s_buf[:, par, :, lo:hi], AX.X, ALU.max))
                chain(dve.tensor_tensor(small[:, 0, par, :], small[:, 0, par, :], sink_bc[:, :], ALU.max))
                chain(dve.tensor_scalar(small[:, 1, par, :], small[:, 0, par, :], -1.0, None, ALU.mult))
                dve.tensor_tensor(small[:, 2, par, :], sink_bc[:, :], small[:, 0, par, :],
                                  ALU.subtract).then_inc(negm_ready, 1)

            def softmax_tail(c):
                lo, hi, _, _ = window(c)
                par = c % 2
                dve.wait_ge(exp_done, c + 1)
                chain(dve.tensor_tensor(small[:, 5, par, :], small[:, 4, par, :], small[:, 3, par, :], ALU.add))
                chain(dve.reciprocal(small[:, 5, par, :], small[:, 5, par, :]))
                for m in range(GROUP):
                    last = dve.tensor_scalar(s_buf[:, par, m, lo:hi], s_buf[:, par, m, lo:hi],
                                             small[:, 5, par, m:m + 1], None, ALU.mult)
                last.then_inc(p_ready, 1)

            def pt_with(c):
                r = P if c % 2 else CHUNK
                dve.wait_ge(p_turned, c + 1)
                if c >= 2:
                    dve.wait_ge(pv_done, c - 1)
                dve.tensor_copy(pt[0:r, c % 2, 1, :], ps[0:r, 5, :]).then_inc(pt_dve, 1)

            def take_o(c):
                dve.wait_ge(pv_done, c + 1)
                dve.tensor_copy(mixT[:, 0:GROUP, c * CHUNK:(c + 1) * CHUNK],
                                ps[:, 6, 0:GROUP * CHUNK].rearrange("p (m q) -> p m q", m=GROUP)).then_inc(o_taken, 1)

            def gain(t):
                r = rows_of(t)
                dve.wait_ge(proj_act, emptied[of_kind["g"][t]][1])
                if t == 0:
                    dve.wait_ge(ng_in, 16)
                dve.tensor_tensor(gg[0:r, t, :], gg[0:r, t, :], ng_bc[0:r, :], ALU.mult).then_inc(gg_ready, 1)

            for s, fill in enumerate(slots):
                if 1 <= s <= NCHUNK:
                    softmax_tail(s - 1)
                for n in fill:
                    if groups[n][2] == "dve":
                        empty(n)
                if s < NCHUNK:
                    softmax_head(s)
                if 1 <= s <= NCHUNK:
                    pt_with(s - 1)
                if 2 <= s < NCHUNK + 2:
                    take_o(s - 2)
            dve.wait_ge(kout_turned, 1)
            chain(dve.tensor_copy(kout[:, 0, :], ps[:, 6, 0:P]))
            dve.tensor_copy(kout[0:DEC, 1, :], ps[0:DEC, 6, P:2 * P]).then_inc(kout_ready, 1)
            for t in range(NT):
                gain(t)
            dve.wait_ge(proj_ready, len(groups))
            chain(dve.memset(aT[:, :, :], 0.0))

            def operands(t):
                r = rows_of(t)
                nch = r // CHUNK
                dve.wait_ge(cum_exp, 4 * t + 1)
                dve.wait_ge(qf_ready, 1)
                dve.tensor_tensor(qin[:, :, 0:r], qin[:, :, 0:r], qf[:, :, tok(t)], ALU.mult).then_inc(hops_ready, 1)
                dve.wait_ge(cum_exp, 4 * t + 2)
                dve.tensor_tensor(kin[:, :, 0:r], kin[:, :, 0:r],
                                  bank(4).rearrange("p (h t) -> p h t", h=BH)[:, :, 0:r],
                                  ALU.mult).then_inc(hops_ready, 1)
                dve.wait_ge(cum_exp, 4 * t + 3)
                chain(dve.tensor_copy(dec[:, :, 0:nch], qex[:, :, CHUNK - 1:r:CHUNK]))
                dve.tensor_tensor(qex[:, :, 0:r], qex[:, :, 0:r], qf[:, :, tok(t)], ALU.mult).then_inc(hops_ready, 1)
                dve.wait_ge(cum_exp, 4 * t + 4)
                dve.tensor_tensor(kdec[0:r, :, :], kdec[0:r, :, :],
                                  kf[0:r, t, :].rearrange("p (h k) -> p h k", h=BH), ALU.mult).then_inc(hops_ready, 1)

            def add_out(t, half):
                r = rows_of(t)
                dve.wait_ge(out_ready, 2 * t + half + 1)
                cols = slice(512 * half, 512 * half + 512)
                dve.tensor_tensor(x[0:r, t, cols], x[0:r, t, cols], ps[0:r, half, :], ALU.add).then_inc(x2_ready, 1)

            def inner_and_states(t):
                r = rows_of(t)
                dve.wait_ge(inner_ready, t + 1)
                dve.copy_predicated(aT[0:r, :, 0:r], causal[0:r, 0:r].bitcast(I32).unsqueeze(1).to_broadcast([r, BH, r]),
                                    ps[0:r, 6, :].rearrange("p (h t) -> p h t", h=BH)[:, :, 0:r]).then_inc(at_ready, 1)
                for c in range(r // CHUNK):
                    n = 2 * t + c
                    before = St[n % 3] if t < PROMPT_TILES else s_sample
                    after = St[(n + 1) % 3] if t < PROMPT_TILES else St[0]
                    ds = bank(7) if c == 0 else bank(4)
                    if c:
                        dve.wait_ge(state_ready, n)
                    if n == 0:
                        last = dve.tensor_copy(after[:, :], ds)
                    else:
                        if t == NT - 1:
                            dve.wait_ge(s_in, 16)
                        for h in range(BH):
                            cols = slice(h * BK, (h + 1) * BK)
                            last = dve.scalar_tensor_tensor(after[:, cols], before[:, cols], dec[:, h, c:c + 1],
                                                            ds[:, cols], ALU.mult, ALU.add)
                    last.then_inc(state_ready, 1)

            def normed(t):
                r = rows_of(t)
                dve.wait_ge(ro_ready, t + 1)
                dve.wait_ge(gg_ready, t + 1)
                if t:
                    dve.wait_ge(rec_turned, t)
                for h in range(BH):
                    cols = slice(h * BK, (h + 1) * BK)
                    last = dve.scalar_tensor_tensor(rec[0:r, cols], ps[0:r, 5, cols], ro[0:r, h:h + 1],
                                                    gg[0:r, t, cols], ALU.mult, ALU.mult)
                last.then_inc(rec_ready, 1)

            def second(t):
                r = rows_of(t)
                dve.wait_ge(rstd2_ready, t + 1)
                if t == 0:
                    dve.wait_ge(g2_in, 16)
                    dve.wait_ge(route_in, 16 * (3 + NG))
                if t >= 2:
                    dve.wait_ge(h2_stored[t - 2], 16)
                    dve.wait_ge(h2_turned, t - 1)
                dve.scalar_tensor_tensor(h2[0:r, t % 2, :], x[0:r, t, :], stats[0:r, 4, t:t + 1], g2_bc[0:r, :],
                                         ALU.mult, ALU.mult).then_inc(h2_ready, 1)
                dve.wait_ge(h2_turned, t + 1)
                dve.tensor_copy(h2T[:, t % 2, 512:1024], bank(3)).then_inc(h2T_dve, 1)
                dve.wait_ge(logits_ready, t + 1)
                dve.tensor_tensor(logits[0:r, t, :], ps[0:r, 7, 0:NG], b_route[0:r, 0:NG], ALU.add)
                dve.tensor_tensor(elogits[0:r, t, :], ps[0:r, 7, NG:NG + NE], b_route[0:r, NG:NG + NE],
                                  ALU.add).then_inc(logits_taken, 1)

            dve.memset(logits[:, :, :], 0.0)
            chain(dve.memset(elogits[:, :, :], 0.0))
            for t in range(NT):
                operands(t)
                if t:
                    add_out(t - 1, 0)
                inner_and_states(t)
                if t:
                    add_out(t - 1, 1)
                normed(t)
                if t:
                    second(t - 1)
            add_out(NT - 1, 0)
            add_out(NT - 1, 1)
            second(NT - 1)

            dve.wait_ge(logits_taken, NT)
            dve.wait_ge(consts, 2)
            rv = rt[:, :, :].rearrange("p a b -> p (a b)")

            def col(i, n=1):
                v = rv[:, i * NT:(i + n) * NT]
                return v if n == 1 else v.rearrange("p (t k) -> p t k", k=n)

            def spread(v, n):
                return v.unsqueeze(2).to_broadcast([P, NT, n])

            def first_max(v, top, hot, scratch):
                chain(dve.tensor_reduce(top, v, AX.X, ALU.max))
                chain(dve.tensor_tensor(scratch, v, spread(top, 4), ALU.is_ge))
                chain(dve.tensor_scalar(scratch, scratch, -8.0, None, ALU.mult))
                chain(dve.tensor_tensor(scratch, scratch, i4, ALU.add))
                chain(dve.tensor_reduce(col(3), scratch, AX.X, ALU.min))
                chain(dve.tensor_scalar(col(3), col(3), 8.0, None, ALU.add))
                chain(dve.tensor_tensor(hot, i4, spread(col(3), 4), ALU.is_equal))

            i4 = iota4[:, :].unsqueeze(1).to_broadcast([P, NT, 4])
            i16 = iota16[:, :].unsqueeze(1).to_broadcast([P, NT, NE])
            group_hot, hot1, hot2, el, scr = (col(a, 4) for a in (8, 12, 16, 20, 24))
            first_max(logits[:, :, :], col(0), group_hot, scr)
            dve.tensor_tensor(rb[:, :, 0:4], logits[:, :, :], spread(col(0), 4), ALU.subtract).then_inc(route_diff, 1)
            picked = picks[:, 0, :, :]
            chain(dve.tensor_tensor(picked.rearrange("p t (g e) -> p (t g) e", g=NG),
                                    elogits[:, :, :].rearrange("p t (g e) -> p (t g) e", g=NG),
                                    group_hot.rearrange("p t g -> p (t g)").unsqueeze(2).to_broadcast(
                                        [P, NT * NG, EPG]), ALU.mult))
            chain(dve.tensor_reduce(el, picked.rearrange("p t (g e) -> p t e g", g=NG), AX.X, ALU.add))
            first_max(el, col(1), hot1, scr)
            chain(dve.tensor_scalar(scr, hot1, -3.0e38, None, ALU.mult))
            chain(dve.tensor_tensor(el, el, scr, ALU.add))
            first_max(el, col(2), hot2, scr)
            dve.tensor_tensor(rb[:, :, 4:5], spread(col(2), 1), spread(col(1), 1), ALU.subtract).then_inc(route_diff, 1)
            for i, hot in enumerate((hot1, hot2)):
                for t in range(NT):
                    last = dve.tensor_tensor(picks[:, i, t, :].rearrange("p (g e) -> p g e", g=NG),
                                             group_hot[:, t, :].unsqueeze(2).to_broadcast([P, NG, EPG]),
                                             hot[:, t, :].unsqueeze(1).to_broadcast([P, NG, EPG]), ALU.mult)
            chain(last)
            chain(dve.memset(picks[rows_of(NT - 1):P, 0:2, NT - 1, :], 0.0))
            dve.tensor_tensor(picks[:, 2, :, :], picks[:, 0, :, :], picks[:, 1, :, :], ALU.add).then_inc(picks_ready, 1)
            dve.wait_ge(route_exp, 2)
            chain(dve.tensor_reduce(col(4), rb[:, :, 0:4], AX.X, ALU.add))
            chain(dve.tensor_scalar(col(5), rb[:, :, 4], 1.0, None, ALU.add))
            chain(dve.tensor_tensor(col(4), col(4), col(5), ALU.mult))
            chain(dve.reciprocal(gates[:, 0, :], col(4)))
            chain(dve.tensor_tensor(gates[:, 1, :], gates[:, 0, :], rb[:, :, 4], ALU.mult))
            dve.wait_ge(rank_ready, 1)
            chain(dve.tensor_copy(rank[:, :, :], ps[:, 0, 0:NT * NE].rearrange("p (t e) -> p t e", e=NE)))
            count_e, over, incl, spare = (rv[:, (12 + a) * NE:(13 + a) * NE] for a in range(4))
            chain(dve.tensor_copy(count_e, ps[:, 1, 0:NE]))
            chain(dve.tensor_scalar(over, count_e, float(P), None, ALU.is_gt))
            for j in range(2, TERMS + 1):
                chain(dve.tensor_scalar(spare, count_e, float(P * j), None, ALU.is_gt))
                chain(dve.tensor_tensor(over, over, spare, ALU.add))
            a, b = incl, spare
            chain(dve.tensor_copy(a, over))
            for k in (1, 2, 4, 8):
                chain(dve.tensor_copy(b, a))
                chain(dve.tensor_tensor(b[:, k:NE], a[:, k:NE], a[:, 0:NE - k], ALU.add))
                a, b = b, a
            incl, spare = a, b
            total = incl[:, NE - 1:NE]
            turn = col(6)[:, 0:1]
            chain(dve.tensor_scalar(turn, total, 0.0, None, ALU.is_gt))
            for k in range(UNROLL, MAX_OVER, UNROLL):
                chain(dve.tensor_scalar(col(6)[:, 1:2], total, float(k), None, ALU.is_gt))
                chain(dve.tensor_tensor(turn, turn, col(6)[:, 1:2], ALU.add))
            chain(dve.tensor_scalar(turn, turn, float(NE // UNROLL), None, ALU.add))
            for k in range(MAX_OVER):
                chain(dve.tensor_scalar(spare, incl, float(k), None, ALU.is_le))
                chain(dve.tensor_reduce(col(7)[:, 0:1], spare, AX.X, ALU.add))
                chain(dve.tensor_scalar(steer[:, k + 1:k + 2], col(7)[:, 0:1], float(NE - 1), None, ALU.min))
            dve.tensor_copy(steer[:, 0:1], turn).then_inc(steer_ready, 1)
            start = spare
            chain(dve.tensor_tensor(start, incl, over, ALU.subtract))
            start_t = start.unsqueeze(1).to_broadcast([P, NT, NE])
            r_i, e_i, s_i, j_i, n_i = (col(a) for a in (0, 1, 2, 3, 4))
            for i in range(2):
                pick = picks[:, i, :, :]
                for dst, w in ((r_i, rank[:, :, :]), (e_i, i16), (s_i, start_t)):
                    chain(dve.tensor_tensor(rb[:, :, :], pick, w, ALU.mult))
                    chain(dve.tensor_reduce(dst, rb[:, :, :], AX.X, ALU.add))
                chain(dve.tensor_scalar(j_i, r_i, float(P), None, ALU.is_ge))
                for j in range(2, TERMS + 1):
                    chain(dve.tensor_scalar(n_i, r_i, float(P * j), None, ALU.is_ge))
                    chain(dve.tensor_tensor(j_i, j_i, n_i, ALU.add))
                chain(dve.tensor_scalar(n_i, j_i, 0.0, None, ALU.is_gt))
                chain(dve.tensor_tensor(s_i, s_i, j_i, ALU.add))
                chain(dve.tensor_scalar(s_i, s_i, float(NE - 1), None, ALU.add))
                chain(dve.tensor_tensor(s_i, s_i, e_i, ALU.subtract))
                chain(dve.tensor_tensor(s_i, s_i, n_i, ALU.mult))
                chain(dve.tensor_tensor(e_i, e_i, s_i, ALU.add))
                chain(dve.tensor_scalar(j_i, j_i, -float(P), None, ALU.mult))
                chain(dve.tensor_tensor(r_i, r_i, j_i, ALU.add))
                chain(dve.tensor_scalar(r_i, r_i, float(BLOCKS + 1), None, ALU.mult))
                chain(dve.tensor_tensor(e_i, e_i, r_i, ALU.add))
                dve.tensor_copy(place_i[:, i, :], e_i).then_inc(places_ready, 1)
                dve.wait_ge(places_ready, i + 1)
            dve.wait_ge(table_in, 16)
            dve.tensor_scalar(table_tok[:, :], table[:, :], 1, None, ALU.logical_shift_right).then_inc(table_ready, 1)

            def x_half(s):
                dve.wait_ge(x_turned, s + 1)
                dve.tensor_copy(xT[:, 4:8, :], bank(2).rearrange("p (c t) -> p c t", c=4)).then_inc(xT_dve, 1)

            x_half(0)
            dve.sem_inc(y_dve, 1)
            dve.wait_ge(steer_ready, 1)
            turns = dve.value_load(steer[0:1, 0:1], min_val=NE // UNROLL, max_val=BLOCKS // UNROLL)
            with dve.Fori(0, turns) as i:
                for slot in range(UNROLL):
                    s = UNROLL * i + slot
                    dve.wait_ge(silu_ready, s + 1)
                    dve.tensor_tensor(hh[:, :], sg[:, :], ps[:, 0, FE:2 * FE], ALU.mult).then_inc(hh_ready, 1)
                    x_half(s + 1)
                    dve.wait_ge(hh_turned, s + 1)
                    dve.tensor_copy(hhT[:, :, :], ps[:, 3, 0:2 * P].rearrange("p (c t) -> p c t", c=2)).then_inc(
                        hhT_ready, 1)
                    dve.wait_ge(y_ready, s + 1)
                    dve.wait_ge(stored[slot % 2], 16 * (2 * i + slot // 2 + 1))
                    dve.tensor_copy(y[:, slot % 2, 512:1024], bank(5)).then_inc(y_dve, 1)

            def weigh(t):
                r = rows_of(t)
                dve.wait_ge(pair_in[t % 2], 16 * (t // 2 + 1))
                for i in range(2):
                    dve.scalar_tensor_tensor(x[0:r, t, :], pair[0:r, t % 2, i * D:(i + 1) * D], gates[0:r, i, t:t + 1],
                                             x[0:r, t, :], ALU.mult, ALU.add).then_inc(sum_ready, 1)
                    dve.wait_ge(sum_ready, 2 * t + i + 1)

            def final(t):
                r = rows_of(t)
                dve.wait_ge(rstd3_ready, t + 1)
                if t == 0:
                    dve.wait_ge(gf_in, 16)
                if t >= 2:
                    dve.wait_ge(out_stored, 16 * (8 + t - 1))
                dve.scalar_tensor_tensor(outb[0:r, t % 2, :], x[0:r, t, :], stats[0:r, 5, t:t + 1], gf_bc[0:r, :],
                                         ALU.mult, ALU.mult).then_inc(final_ready, 1)

            weigh(0)
            for t in range(1, NT):
                weigh(t)
                final(t - 1)
            final(NT - 1)

        @block.tensor
        def _(pe):
            def turn_x(t):
                r = rows_of(t)
                pe.wait_ge(hn_ready, t + 1)
                if t >= 3:
                    pe.wait_ge(hT_act, t - 2)
                    pe.wait_ge(hT_dve, t - 2)
                for c in range(KC):
                    b = 2 + 2 * (t % 3) + c // 4
                    last = pe.transpose(ps[:, b, (c % 4) * P:(c % 4) * P + r], hn[0:r, t % 2, c * P:(c + 1) * P],
                                        ident[0:r, 0:r])
                last.then_inc(turned, 1)

            def project(n):
                kind, i, _ = groups[n]
                k = ring_of[kind]
                w = w_slot(k)
                if n >= 2:
                    who, v = emptied[n - 2]
                    pe.wait_ge(proj_act if who == "act" else proj_dve, v)
                if i == 0:
                    pe.wait_ge(w_in[k], 16 * KV * KC if kind == "q" else 16)
                b = n % 2
                for c in range(KC):
                    if kind in "fig":
                        r = rows_of(i)
                        last = pe.matmul(ps[0:r, b, :], hT[:, c, tok(i)], w[:, c, :], start=c == 0, stop=c == KC - 1)
                    elif kind == "v":
                        r = rows_of(i)
                        last = pe.matmul(ps[0:r, b, 0:KVW], hT[:, c, tok(i)], w[:, c, KVW:2 * KVW],
                                         start=c == 0, stop=c == KC - 1)
                    else:
                        m, half = i // 2, i % 2
                        if kind == "k":
                            m, half, lhs = 0, i, w[:, c, 0:KVW]
                        elif kind == "q":
                            lhs = w[:, c, m * P:(m + 1) * P]
                        else:
                            lhs = w[:, c, m * BK:(m + 1) * BK]
                        last = pe.matmul(bank(b, HALF), lhs, hT[:, c, half * HALF:(half + 1) * HALF],
                                         start=c == 0, stop=c == KC - 1)
                last.then_inc(proj_ready, 1)

            pe.wait_ge(consts, 1)
            turn_x(0)
            turn_x(1)
            turn_x(2)
            for t in range(NT):
                pe.wait_ge(hT_act, t + 1)
                pe.wait_ge(hT_dve, t + 1)
                project(t)
                if t + 3 < NT:
                    turn_x(t + 3)
            pe.wait_ge(ck_in, 16)
            pe.wait_ge(hT_dve, NT)
            pe.transpose(ps[:, 7, 0:P], kout[:, 0, :], ident[:, :]).then_inc(cache_turned, 1)
            for n in range(NT, first_filler):
                project(n)

            def scores(c):
                lo, hi, _, start = window(c)
                pe.wait_ge(qbd_ready, KV * (c + 1))
                if c == 0:
                    wait_emptied(pe, "k")
                    pe.wait_ge(cache_taken, 1)
                else:
                    pe.wait_ge(scores_taken, c)
                for m in range(GROUP):
                    last = pe.matmul(ps[:, 2 + m // 2, (m % 2) * 2 * P + lo:(m % 2) * 2 * P + hi], qbd[:, c % 2, m, :],
                                     kT[:, start:start + hi - lo], start=True, stop=True)
                last.then_inc(scores_ready, 1)

            def turn_p(c):
                pe.wait_ge(p_ready, c + 1)
                if c == 1:
                    pe.wait_ge(dve_consts, 1)
                if c >= 1:
                    pe.wait_ge(pt_dve, c)
                if c >= 3:
                    pe.wait_ge(pt_act, c - 2)
                r = P if c % 2 else CHUNK
                for m in range(GROUP):
                    if has_before(c):
                        pe.transpose(ps[:, 4, m * P:(m + 1) * P], s_buf[:, c % 2, m, 0:P], ident[:, :])
                    last = pe.transpose(ps[0:r, 5, m * P:(m + 1) * P], s_buf[:, c % 2, m, P:P + r], ident[:, :])
                last.then_inc(p_turned, 1)

            def attend(c):
                slot_a, slot_b = v_slots(c)
                rows_a = slice(CHUNK, P) if c % 2 else slice(0, P)
                rows_b = slice(0, P if c % 2 else CHUNK)
                if c == 0:
                    wait_emptied(pe, "v")
                if c == NCHUNK - 1:
                    pe.wait_ge(cv_in, 16)
                pe.wait_ge(pt_dve, c + 1)
                if has_before(c):
                    pe.wait_ge(pt_act, c - 1)
                if c:
                    pe.wait_ge(o_taken, c)
                for b in range(KV):
                    def probs(part, rows):
                        return pt[rows, c % 2, part, :].rearrange("p (m b q) -> p m b q", m=GROUP, b=KV)[:, :, b, :]
                    out = ps[b * HD:(b + 1) * HD, 6, 0:GROUP * CHUNK]
                    heads = slice(b * HD, (b + 1) * HD)
                    if has_before(c):
                        pe.matmul(out, V[rows_a, slot_a, heads], probs(0, rows_a), start=True, stop=False)
                    last = pe.matmul(out, V[rows_b, slot_b, heads], probs(1, rows_b), start=not has_before(c),
                                     stop=True)
                last.then_inc(pv_done, 1)

            for s, fill in enumerate(slots):
                for n in fill:
                    project(n)
                if s < NCHUNK:
                    scores(s)
                if 1 <= s <= NCHUNK:
                    turn_p(s - 1)
                if 2 <= s < NCHUNK + 2:
                    attend(s - 2)
            pe.wait_ge(o_taken, NCHUNK)
            pe.transpose(ps[:, 6, 0:P], kT[:, SEQ - P:SEQ], ident[:, :])
            pe.transpose(ps[0:DEC, 6, P:2 * P], kT[:, SEQ + WINDOW:], ident[:, :]).then_inc(kout_turned, 1)

            def decays(t):
                r = rows_of(t)
                pe.wait_ge(logf_ready, t + 1)
                if t >= 2:
                    pe.wait_ge(h2T_act, t - 1)
                    pe.wait_ge(h2T_dve, t - 1)
                if t:
                    pe.wait_ge(state_ready, 2 * t)
                    pe.wait_ge(rec_ready, t)
                for h in range(BH):
                    cols = slice(h * BK, (h + 1) * BK)
                    pe.matmul(ps[:, 2 + h // 2, (h % 2) * 2 * P:(h % 2 + 1) * 2 * P], logf[0:r, t, cols],
                              decay_m[0:r, :, :], start=True, stop=True)
                    pe.transpose(ps[:, 4, h * P:h * P + r], kf[0:r, t, cols], ident[0:r, 0:r])
                pe.matmul(ps[0:r, 5, :], tail_m[0:r, 0:r], logf[0:r, t, :], start=True, stop=True).then_inc(cum_ready, 1)

            def inner(t):
                r = rows_of(t)
                pe.wait_ge(hops_ready, 4 * t + 4)
                if t:
                    pe.wait_ge(rec_taken, t)
                if t >= 2:
                    pe.wait_ge(logits_taken, t - 1)
                for h in range(BH):
                    pe.matmul(ps[0:r, 6, h * P:h * P + r], kin[:, h, 0:r], qin[:, h, 0:r], start=True, stop=True)
                for c in range(r // CHUNK):
                    rows = slice(c * CHUNK, (c + 1) * CHUNK)
                    for h in range(BH):
                        cols = slice(h * BK, (h + 1) * BK)
                        last = pe.matmul(ps[:, 4 if c else 7, cols], kdec[rows, h, :], vf[rows, t, cols],
                                         start=True, stop=True)
                last.then_inc(inner_ready, 1)

            def sums(t):
                r = rows_of(t)
                pe.wait_ge(at_ready, t + 1)
                if t == NT - 1:
                    pe.wait_ge(s_in, 16)
                elif r > CHUNK:
                    pe.wait_ge(state_ready, 2 * t + 1)
                for h in range(BH):
                    cols = slice(h * BK, (h + 1) * BK)
                    terms = []
                    for c in range(r // CHUNK):
                        before = s_sample if t == NT - 1 else St[(2 * t + c) % 3]
                        if 2 * t + c:
                            terms.append((c, before))
                    pe.matmul(ps[0:r, 5, cols], aT[0:r, h, 0:r], vf[0:r, t, cols], start=True, stop=True)
                    for c, before in terms:
                        rows = slice(c * CHUNK, (c + 1) * CHUNK)
                        last = pe.matmul(ps[rows, 5, cols], qex[:, h, rows], before[:, cols], start=False,
                                         stop=True, skip_group_check=True)
                last.then_inc(rec_sum, 1)

            def turn_rec(t):
                r = rows_of(t)
                pe.wait_ge(rec_ready, t + 1)
                for h in range(BH):
                    last = pe.transpose(ps[:, 6, h * P:h * P + r], rec[0:r, h * BK:(h + 1) * BK], ident[0:r, 0:r])
                last.then_inc(rec_turned, 1)

            def out_half(t, half):
                r = rows_of(t)
                k = len(W_GROUPS) + half
                if t == 0:
                    pe.wait_ge(w_in[k], 48)
                    wait_emptied(pe, "g")
                    wait_emptied(pe, "b")
                else:
                    pe.wait_ge(x2_ready, 2 * (t - 1) + half + 1)
                pe.wait_ge(rec_taken, t + 1)
                for c in range(KC):
                    last = pe.matmul(ps[0:r, half, :], mixT[:, c, tok(t)], w_slot(k)[:, c, :], start=c == 0,
                                     stop=c == KC - 1)
                last.then_inc(out_ready, 1)

            def route(t):
                r = rows_of(t)
                pe.wait_ge(h2_ready, t + 1)
                if t + 1 < NT:
                    pe.wait_ge(state_ready, 2 * (t + 1) + 1)
                for c in range(KC):
                    last = pe.transpose(ps[:, 2 + c // 4, (c % 4) * P:(c % 4) * P + r],
                                        h2[0:r, t % 2, c * P:(c + 1) * P], ident[0:r, 0:r])
                last.then_inc(h2_turned, 1)
                pe.wait_ge(h2T_act, t + 1)
                pe.wait_ge(h2T_dve, t + 1)
                for c in range(KC):
                    last = pe.matmul(ps[0:r, 7, 0:NG + NE], h2T[:, t % 2, c * P:c * P + r], w_route[:, c, :],
                                     start=c == 0, stop=c == KC - 1)
                last.then_inc(logits_ready, 1)

            pe.wait_ge(kout_ready, 1)
            for t in range(NT):
                decays(t)
                if t:
                    out_half(t - 1, 0)
                inner(t)
                if t:
                    out_half(t - 1, 1)
                sums(t)
                turn_rec(t)
                if t:
                    route(t - 1)
            out_half(NT - 1, 0)
            out_half(NT - 1, 1)
            route(NT - 1)

            pe.wait_ge(picks_ready, 1)
            pe.wait_ge(x2_ready, 2 * NT)
            for t in range(NT):
                for u in range(t + 1):
                    pe.matmul(ps[:, 0, t * NE:(t + 1) * NE], (earlier if u == t else ones)[:, :], picks[:, 2, u, :],
                              start=u == 0, stop=u == t)
            for t in range(NT):
                last = pe.matmul(ps[:, 1, 0:NE], ones[:, :], picks[:, 2, t, :], start=t == 0, stop=t == NT - 1)
            last.then_inc(rank_ready, 1)

            def turn_xg(s, par, waited):
                pe.wait_ge(gathered[par], waited)
                for c in range(KC):
                    last = pe.transpose(ps[:, 1 + c // 4, (c % 4) * P:(c % 4 + 1) * P], xg[:, par, c * P:(c + 1) * P],
                                        ident[:, :])
                last.then_inc(x_turned, 1)

            pe.wait_ge(places_ready, 2)
            turn_xg(0, 0, 16)
            pe.wait_ge(steer_ready, 1)
            turns = pe.value_load(steer[0:1, 0:1], min_val=NE // UNROLL, max_val=BLOCKS // UNROLL)
            with pe.Fori(0, turns) as i:
                for slot in range(UNROLL):
                    s = UNROLL * i + slot
                    pe.wait_ge(expert_in[slot], 48 * (i + 1))
                    pe.wait_ge(xT_act, s + 1)
                    pe.wait_ge(xT_dve, s + 1)
                    for c in range(KC):
                        last = pe.matmul(bank(0), xT[:, c, :], we_gu[slot][:, c, :], start=c == 0, stop=c == KC - 1)
                    last.then_inc(gu_ready, 1)
                    turn_xg(s + 1, (slot + 1) % 2, 16 * (2 * i + (slot + 1) // 2 + 1))
                    pe.wait_ge(hh_ready, s + 1)
                    for f in range(2):
                        last = pe.transpose(ps[:, 3, f * P:(f + 1) * P], hh[:, f * P:(f + 1) * P], ident[:, :])
                    last.then_inc(hh_turned, 1)
                    pe.wait_ge(hhT_ready, s + 1)
                    pe.wait_ge(y_act, s + 1)
                    pe.wait_ge(y_dve, s + 1)
                    for half in range(2):
                        for f in range(2):
                            last = pe.matmul(bank(4 + half), hhT[:, f, :], we_d[slot][:, f, 512 * half:512 * half + 512],
                                             start=f == 0, stop=f == 1)
                    last.then_inc(y_ready, 1)
    return nc


def kernel(**inputs):
    import numpy as _np
    import concourse.bacc as _bacc
    from concourse import mybir as _mybir
    from concourse.bass_utils import run_bass_kernel_spmd as _run

    nc = _bacc.Bacc("TRN2", target_bir_lowering=False, num_devices=1)
    layout = {
        "x_p": ("x_prompt", (SEQ, D)), "x_s": ("x_sample", (DEC, D)),
        "cache_k": ("cache_k", (WINDOW, KVW)), "cache_v": ("cache_v", (WINDOW, KVW)),
        "state": ("state_hgrn", (BH, BK, BK)), "g1": ("norm1_g", (D,)), "w_in": ("w_in", (D, G0 + BW)),
        "sink": ("attn_sink", (HEADS,)), "lower": ("lower_bounds", (2, BW)), "ng": ("hgrn_norm_g", (BW,)),
        "w_o": ("w_o", (D, D)), "g2": ("norm2_g", (D,)), "w_rg": ("w_router_group", (D, NG)),
        "b_rg": ("b_router_group", (NG,)), "w_re": ("w_router_expert", (NG, D, EPG)),
        "b_re": ("b_router_expert", (NG, EPG)), "w_gate": ("w_gate", (NE, D, FE)), "w_up": ("w_up", (NE, D, FE)),
        "w_down": ("w_down", (NE, FE, D)), "gf": ("final_norm_g", (D,)),
    }
    results = {
        "y_p": ((SEQ, D), (1, SEQ, D)), "y_s": ((DEC, D), (1, DEC, D)),
        "k_win_p": ((WINDOW, KVW), (1, 1, WINDOW, KV, HD)), "v_win_p": ((WINDOW, KVW), (1, 1, WINDOW, KV, HD)),
        "state_p": ((BH, BK, BK), (1, 1, BH, BK, BK)),
        "k_win_s": ((WINDOW, KVW), (1, 1, WINDOW, KV, HD)), "v_win_s": ((WINDOW, KVW), (1, 1, WINDOW, KV, HD)),
        "state_s": ((BH, BK, BK), (1, 1, BH, BK, BK)),
    }
    arrays, io = {}, {}
    for name, (key, shape) in layout.items():
        arrays[f"in_{name}"] = _np.ascontiguousarray(inputs[key]).reshape(shape)
        io[name] = nc.dram_tensor(f"in_{name}", shape, _mybir.dt.float32, kind="ExternalInput").ap()
    for name, (shape, _) in results.items():
        io[name] = nc.dram_tensor(f"out_{name}", shape, _mybir.dt.float32, kind="ExternalOutput").ap()
    program(nc, io)
    r = _run(nc, [arrays], core_ids=[0])
    return tuple(r.results[0][f"out_{name}"].reshape(shape) for name, (_, shape) in results.items())
```

```python
from contextlib import ExitStack

import numpy as np

import concourse.bass as bass
from concourse import mybir

ALU = mybir.AluOpType
ACT = mybir.ActivationFunctionType
AX = mybir.AxisListType
F32 = mybir.dt.float32
I32 = mybir.dt.int32

P = 128
D = 1024
KC = D // P
SEQ, DEC = 512, 64
TOK = SEQ + DEC
NT = (TOK + P - 1) // P
PROMPT_TILES = SEQ // P
CHUNK = 64
NCHUNK = TOK // CHUNK
WINDOW = 128
HEADS, KV, HD = 8, 2, 64
GROUP = HEADS // KV
KVW = KV * HD
BH, BK = 4, 128
BW = BH * BK
EPS = 1e-6
NG, EPG = 4, 4
NE = NG * EPG
FE = 256
PAIRS = 2 * TOK
MAX_OVER = (PAIRS - NE) // P
MAX_OVER = min(MAX_OVER, PAIRS // (P + 1))
UNROLL = 4
BLOCKS = NE + MAX_OVER
AHEAD = 3
COLS = BLOCKS + AHEAD
NOWHERE = 4096
TERMS = (TOK - 1) // P
Q0, K0, V0 = 0, 512, 640
QB0, F0, I0, G0 = 768, 1280, 1792, 2304
W_GROUPS = [(F0, BW), (K0, 2 * KVW), (Q0, BW), (I0, BW), (QB0, BW), (G0, BW)]
RING = 3
HALF = TOK // 2


def rows_of(t):
    return min(P, TOK - t * P)


def window(c):
    odd = c % 2
    sample = c == NCHUNK - 1
    lo = CHUNK * odd if sample or c >= 2 else P
    hi = P + CHUNK + CHUNK * odd
    start = SEQ if sample else (c - 2) * CHUNK + lo - CHUNK * odd
    return lo, hi, CHUNK * odd, start


def has_before(c):
    return c >= 2


def v_slots(c):
    return (4, 5) if c == NCHUNK - 1 else (c // 2 - 1, c // 2)


def program(nc, io):
    ctx = ExitStack()
    with ctx:
        def sem(name):
            return ctx.enter_context(nc.semaphore(name))

        def sems(name, n):
            return [sem(f"{name}{i}") for i in range(n)]

        cursor = [(nc.sbuf_base + 63) // 64 * 64]

        def place(name, shape, dt=F32):
            n = int(np.prod(shape[1:])) * 4
            t = nc.alloc_sbuf_tensor_at(name, shape, dt, offset=cursor[0])
            cursor[0] += (n + 31) // 32 * 32
            return t

        x = place("x", [P, NT, D])
        ident = place("ident", [P, P])
        ones = place("ones", [P, P])
        earlier = place("earlier", [P, P])
        decay_m = place("decay_m", [P, 2, P])
        tail_m = place("tail_m", [P, P])
        causal = place("causal", [P, P])
        neghalf = place("neghalf", [P, 8])
        iota4 = place("iota4", [P, 4])
        iota16 = place("iota16", [P, NE])
        iota8 = place("iota8", [P, MAX_OVER])
        iota_p = place("iota_p", [P, P])
        limits = place("limits", [P, TERMS])
        upto = place("upto", [P, NE, NE])
        pair_val = place("pair_val", [P, 2, NT])
        g2_bc = place("g2_bc", [P, D])
        ng_bc = place("ng_bc", [P, BW])
        w_route = place("w_route", [P, KC, NG + NE])
        b_route = place("b_route", [P, NG + NE])
        sink_bc = place("sink_bc", [P, GROUP])
        stats = place("stats", [P, 6, 8])
        ms = place("ms", [P, 3 * NT + BH * NT])
        ro = place("ro", [P, BH])
        osq = place("osq", [P, BH])
        small = place("small", [P, 8, 2, GROUP])
        logits = place("logits", [P, NT, NG])
        elogits = place("elogits", [P, NT, NE])
        gates = place("gates", [P, 2, NT])
        rt = place("rt", [P, 12, NE])
        steer = place("steer", [P, 2 + MAX_OVER], I32)
        table = place("table", [P, COLS], I32)
        table_tok = place("table_tok", [P, COLS], I32)
        now_tok = place("now_tok", [P, UNROLL, 1], I32)
        now_pair = place("now_pair", [P, UNROLL, 1], I32)
        dec = place("dec", [P, BH, 2])
        kout = place("kout", [P, 2, KVW])

        after_small = cursor[0]
        ring = place("ring", [P, RING, KC, 512])
        mixT = place("mixT", [P, KC, TOK])
        end_small = cursor[0]

        after_weights = cursor[0]
        hT = place("hT", [P, KC, TOK])
        kf = place("kf", [P, NT, BW])
        logf = place("logf", [P, NT, BW])
        gg = place("gg", [P, NT, BW])
        vf = place("vf", [P, NT, BW])
        qf = place("qf", [P, BH, TOK])
        qa = place("qa", [P, GROUP, TOK])
        kT = place("kT", [P, SEQ + WINDOW + DEC])
        V = place("V", [P, 6, KVW])
        bias = place("bias", [P, GROUP, WINDOW + CHUNK])
        qbd = place("qbd", [P, 2, GROUP, P])
        s_at = cursor[0]
        s_buf = place("s_buf", [P, 2, GROUP, 2 * P])
        pt_at = cursor[0]
        pt = place("pt", [P, 2, 2, GROUP * P])
        assert cursor[0] <= nc.sbuf_usable_end, (cursor[0], nc.sbuf_usable_end)
        late = cursor[0]
        hn = s_buf[:, :, :, :].rearrange("p a m k -> p a (m k)")
        h2 = hn
        h2T = pt[:, :, :, :].rearrange("p a b k -> p a (b k)")
        g1_bc = pt[:, 0, :, :].rearrange("p b k -> p (b k)")
        mix_flat = mixT[:, :, :].rearrange("p k t -> p (k t)")
        lb_bc = mix_flat[:, 0:2 * BW]
        lb = lb_bc[:, 0:BW]
        oml = lb_bc[:, BW:2 * BW]
        lb_t = mix_flat[:, 2 * BW:4 * BW]
        junk = mix_flat[:, 4 * BW:4 * BW + D]
        hT_flat = hT[:, :, :].rearrange("p k t -> p (k t)")
        hb = [hT_flat[:, i * BW:(i + 1) * BW].rearrange("p (h t) -> p h t", h=BH) for i in range(5)]
        qin, kin, qex, aT, kdec = hb
        rec = hT_flat[:, 5 * BW:6 * BW]
        St = [hT_flat[:, (6 + i) * BW:(7 + i) * BW] for i in range(3)]
        qa_flat = qa[:, :, :].rearrange("p m t -> p (m t)")
        s_sample = qa_flat[:, D:D + BW]

        cursor[0] = after_small
        xg = place("xg", [P, UNROLL, D])
        xT = place("xT", [P, KC, P])
        y = place("y", [P, 2, D])
        sg = place("sg", [P, FE])
        hh = place("hh", [P, FE])
        hhT = place("hhT", [P, 2, P])
        gf_bc = place("gf_bc", [P, D])
        picks = place("picks", [P, 3, NT, NE])
        before = place("before", [P, NT + 1, NE])
        rank_v = place("rank_v", [P, NT, NE])
        picked_v = place("picked_v", [P, 2, NT, NE])
        rb = place("rb", [P, NT, 5])
        compared = place("compared", [P, NE, NE])
        per_pair = place("per_pair", [P, 4, 2, NT])
        per_expert = place("per_expert", [P, 3, NE])
        over_hot = place("over_hot", [P, MAX_OVER, NE])
        table_f = place("table_f", [P, COLS])
        slot_hot = place("slot_hot", [P, 2, NT, P])
        block_hot = place("block_hot", [P, 2, NT, COLS])
        assert cursor[0] <= end_small
        cursor[0] = after_weights
        we_gu = [place(f"we_gu{i}", [P, 2, KC, FE]) for i in range(UNROLL)]
        we_d = [place(f"we_d{i}", [P, 2, D]) for i in range(UNROLL)]
        assert cursor[0] <= late
        cursor[0] = after_weights
        pair = place("pair", [P, NT, 2 * D])
        assert cursor[0] <= late

        ps = ctx.enter_context(nc.psum_tensor("ps", [P, 8, 512], F32))

        h2_dram = nc.dram_tensor("h2_rows", (TOK, D), F32, kind="Internal").ap()
        y_dram = nc.dram_tensor("y_pairs", (PAIRS, D), F32, kind="Internal").ap()

        x_in = sems("x_in", NT)
        g1_in, lb_in, ng_in, sink_in, route_in = (sem(n) for n in ("g1_in", "lb_in", "ng_in", "sink_in", "route_in"))
        g2_in, ck_in, cv_in, s_in = (sem(n) for n in ("g2_in", "ck_in", "cv_in", "s_in"))
        w_in = sems("w_in", len(W_GROUPS) + 2)
        consts, consts_chain, bias_ready = sem("consts"), sem("consts_chain"), sem("bias_ready")
        dve_chain, pool_chain, dve_consts = sem("dve_chain"), sem("pool_chain"), sem("dve_consts")
        ssq_ready, rstd_ready, hn_ready, turned, hT_act, hT_dve = (
            sem(n) for n in ("ssq_ready", "rstd_ready", "hn_ready", "turned", "hT_act", "hT_dve"))
        proj_ready, proj_act, proj_dve = (sem(n) for n in ("proj_ready", "proj_act", "proj_dve"))
        f_ready, f_freed, logf_ready, oml_ready = sem("f_ready"), sem("f_freed"), sem("logf_ready"), sem("oml_ready")
        lb_exp, lb_diff = sem("lb_exp"), sem("lb_diff")
        cache_turned, cache_taken, qf_ready, gg_ready = (
            sem(n) for n in ("cache_turned", "cache_taken", "qf_ready", "gg_ready"))
        qbd_ready, scores_ready, scores_taken, negm_ready, exp_done, p_ready = (
            sem(n) for n in ("qbd_ready", "scores_ready", "scores_taken", "negm_ready", "exp_done", "p_ready"))
        p_turned, pt_act, pt_dve, pv_done, o_taken = (
            sem(n) for n in ("p_turned", "pt_act", "pt_dve", "pv_done", "o_taken"))
        kout_turned, kout_ready = sem("kout_turned"), sem("kout_ready")
        cum_ready, cum_exp, hops_ready, inner_ready, at_ready, state_ready = (
            sem(n) for n in ("cum_ready", "cum_exp", "hops_ready", "inner_ready", "at_ready", "state_ready"))
        rec_sum, osq_ready, ro_ready, rec_ready, rec_turned, rec_taken = (
            sem(n) for n in ("rec_sum", "osq_ready", "ro_ready", "rec_ready", "rec_turned", "rec_taken"))
        out_ready, x2_ready, ssq2_ready, rstd2_ready, h2_ready = (
            sem(n) for n in ("out_ready", "x2_ready", "ssq2_ready", "rstd2_ready", "h2_ready"))
        h2_stored = sems("h2_stored", NT)
        h2_turned, h2T_act, h2T_dve, logits_ready, logits_taken = (
            sem(n) for n in ("h2_turned", "h2T_act", "h2T_dve", "logits_ready", "logits_taken"))
        route_diff, route_exp, picks_ready, rank_ready, hot_ready, slots_ready = (
            sem(n) for n in ("route_diff", "route_exp", "picks_ready", "rank_ready", "hot_ready", "slots_ready"))
        table_ready, steer_ready, xg_clear = sem("table_ready"), sem("steer_ready"), sem("xg_clear")
        expert_in = sems("expert_in", UNROLL)
        gathered, stored = sems("gathered", UNROLL), sems("stored", 2)
        col_copied, dma_cleared = sem("col_copied"), sem("dma_cleared")
        x_turned_a, x_turned_b, xT_act, xT_dve, gu_ready, silu_ready, hh_ready = (
            sem(n) for n in ("x_turned_a", "x_turned_b", "xT_act", "xT_dve", "gu_ready", "silu_ready", "hh_ready"))
        hh_turned, hhT_ready, y_ready, y_act, y_dve = (
            sem(n) for n in ("hh_turned", "hhT_ready", "y_ready", "y_act", "y_dve"))
        pair_in = sems("pair_in", NT)
        sum_ready, ssq3_ready, rstd3_ready, final_ready = (
            sem(n) for n in ("sum_ready", "ssq3_ready", "rstd3_ready", "final_ready"))
        out_stored = sem("out_stored")

        groups = []
        for t in range(NT):
            groups.append(("f", t, "act"))
        groups += [("k", 0, "dve"), ("k", 1, "dve")]
        groups += [("v", t, "act") for t in range(NT)]
        groups += [("q", i, "act" if i % 2 else "dve") for i in range(2 * GROUP)]
        first_filler = len(groups)
        groups += [("i", t, "act") for t in range(NT)]
        groups += [("b", i, "dve") for i in range(2 * BH)]
        groups += [("g", t, "act") for t in range(NT)]
        ring_of = {"f": 0, "k": 1, "v": 1, "q": 2, "i": 3, "b": 4, "g": 5}
        emptied = {}
        count = {"act": 0, "dve": 0}
        for n, (_, _, who) in enumerate(groups):
            count[who] += 1
            emptied[n] = (who, count[who])
        last_of = {}
        for n, (kind, _, _) in enumerate(groups):
            last_of[ring_of[kind]] = n
        of_kind = {kind: [n for n, g in enumerate(groups) if g[0] == kind] for kind in ring_of}

        def wait_emptied(eng, kinds):
            for who, s in (("act", proj_act), ("dve", proj_dve)):
                last = [emptied[n][1] for k in kinds for n in of_kind[k] if emptied[n][0] == who]
                if last:
                    eng.wait_ge(s, max(last))

        slots = [[n] for n in of_kind["i"]] + [of_kind["b"][2 * m:2 * m + 2] for m in range(BH)] + \
                [[n] for n in of_kind["g"]]
        assert len(slots) >= NCHUNK + 2

        def w_slot(k):
            return ring[:, k % RING, :, :]

        def bank(b, n=512):
            return ps[:, b, 0:n]

        def tok(t):
            return slice(t * P, t * P + rows_of(t))

        block = ctx.enter_context(nc.Block())

        @block.sync
        def _(sp):
            def store_out(t):
                sp.wait_ge(final_ready, t + 1)
                dst = io["y_p"][tok(t), :] if t < PROMPT_TILES else io["y_s"]
                sp.dma_start(dst, pair[0:rows_of(t), t, 0:D]).then_inc(out_stored, 16)

            def w_group(k):
                if k < len(W_GROUPS) and W_GROUPS[k][0] == Q0:
                    src = io["w_in"][:, Q0:Q0 + BW].rearrange("(c p) (b m d) -> p b c m d", p=P, b=KV, m=GROUP)
                    dst = w_slot(k)[:, :, :].rearrange("p c (m b d) -> p b c m d", b=KV, m=GROUP)
                    for b in range(KV):
                        for c in range(KC):
                            sp.dma_start(dst[:, b, c, :, :], src[:, b, c, :, :]).then_inc(w_in[k], 16)
                elif k < len(W_GROUPS):
                    a, n = W_GROUPS[k]
                    sp.dma_start(w_slot(k)[:, :, 0:n],
                                 io["w_in"][:, a:a + n].rearrange("(c p) n -> p c n", p=P)).then_inc(w_in[k], 16)
                else:
                    cols = slice(512 * (k - len(W_GROUPS)), 512 * (k - len(W_GROUPS)) + 512)
                    att = io["w_o"][0:HEADS * HD, cols].rearrange("(b m d) n -> b d m n", b=KV, m=GROUP)
                    for b in range(KV):
                        sp.dma_start(w_slot(k)[b * HD:(b + 1) * HD, 0:GROUP, :], att[b]).then_inc(w_in[k], 16)
                    sp.dma_start(w_slot(k)[:, GROUP:KC, :],
                                 io["w_o"][HEADS * HD:, cols].rearrange("(h p) n -> p h n", p=P)).then_inc(w_in[k], 16)

            w_group(0)
            w_group(1)
            w_group(2)
            sp.dma_start(kout[:, 0, :], io["cache_k"]).then_inc(ck_in, 16)
            sp.dma_start(V[:, 4, :], io["cache_v"]).then_inc(cv_in, 16)
            sp.dma_start(io["k_win_s"][0:CHUNK, :], io["cache_k"][CHUNK:WINDOW, :]).then_inc(out_stored, 16)
            sp.dma_start(io["v_win_s"][0:CHUNK, :], io["cache_v"][CHUNK:WINDOW, :]).then_inc(out_stored, 16)
            for k in range(RING, len(W_GROUPS) + 2):
                sp.wait_ge(proj_ready, last_of[k - RING] + 1)
                w_group(k)
                if k == 4:
                    wait_emptied(sp, "v")
                    sp.dma_start(io["v_win_p"], V[:, PROMPT_TILES - 1, :]).then_inc(out_stored, 16)
                    sp.dma_start(io["v_win_s"][CHUNK:WINDOW, :], V[0:DEC, 5, :]).then_inc(out_stored, 16)
            sp.wait_ge(kout_ready, 1)
            sp.dma_start(io["k_win_p"], kout[:, 0, :]).then_inc(out_stored, 16)
            sp.dma_start(io["k_win_s"][CHUNK:WINDOW, :], kout[0:DEC, 1, :]).then_inc(out_stored, 16)
            sp.dma_start(s_sample[:, :].rearrange("k (h v) -> k h v", h=BH),
                         io["state"].rearrange("h k v -> k h v")).then_inc(s_in, 16)
            for t in range(NT):
                if t == PROMPT_TILES - 1:
                    sp.wait_ge(state_ready, 2 * PROMPT_TILES)
                    sp.dma_start(io["state_p"].rearrange("h k v -> k h v"),
                                 St[2 * PROMPT_TILES % 3].rearrange("k (h v) -> k h v", h=BH)).then_inc(out_stored, 16)
                if t == NT - 1:
                    sp.wait_ge(state_ready, 2 * PROMPT_TILES + 1)
                    sp.dma_start(io["state_s"].rearrange("h k v -> k h v"),
                                 St[0].rearrange("k (h v) -> k h v", h=BH)).then_inc(out_stored, 16)
                sp.wait_ge(h2_ready, t + 1)
                sp.dma_start(h2_dram[tok(t), :], h2[0:rows_of(t), t % 2, :]).then_inc(h2_stored[t], 16)

            def expert(slot, e):
                gate, up = (we_gu[slot][:, i, :, :] for i in range(2))
                for dst, src in ((gate, io["w_gate"]), (up, io["w_up"]), (we_d[slot][:, :, :], io["w_down"])):
                    v = src[bass.ds(e, 1), :, :] if not isinstance(e, int) else src[e:e + 1, :, :]
                    sp.dma_start(dst, v.rearrange("e (p c) n -> p (e c) n", p=P)).then_inc(expert_in[slot], 16)

            sp.wait_ge(out_stored, 16 * 8)
            sp.wait_ge(rec_taken, NT)
            sp.wait_ge(h2T_act, NT)
            sp.wait_ge(h2T_dve, NT)
            for t in range(NT):
                sp.wait_ge(h2_stored[t], 16)
            for slot in range(UNROLL):
                if slot == 2:
                    for b in range(AHEAD):
                        sp.wait_ge(gathered[b], 16)
                expert(slot, slot)
            with sp.Fori(1, NE // UNROLL) as i:
                for slot in range(UNROLL):
                    sp.wait_ge(y_ready, UNROLL * (i - 1) + slot + 1)
                    expert(slot, UNROLL * i + slot)
            sp.wait_ge(steer_ready, 1)
            turns = sp.value_load(steer[0:1, 0:1], min_val=NE // UNROLL, max_val=BLOCKS // UNROLL)
            with sp.If(turns > NE // UNROLL):
                with sp.Fori(0, turns - NE // UNROLL) as i:
                    for slot in range(UNROLL):
                        sp.wait_ge(y_ready, NE - UNROLL + UNROLL * i + slot + 1)
                        e = sp.value_load(steer[0:1, bass.ds(UNROLL * i + slot + 1, 1)], min_val=0, max_val=NE - 1)
                        expert(slot, e)
            for par in range(2):
                sp.wait_ge(stored[par], 8 * UNROLL * turns + 16)
            pairs = y_dram.rearrange("(t a) d -> t (a d)", a=2)
            for t in range(NT):
                sp.dma_start(pair[0:rows_of(t), t, :], pairs[tok(t), :]).then_inc(pair_in[t], 16)
            for t in range(NT):
                store_out(t)
            sp.wait_ge(out_stored, 16 * (8 + NT))

        @block.gpsimd
        def _(pool):
            done = [0]

            def chain(ins):
                done[0] += 1
                ins.then_inc(pool_chain, 1)
                pool.wait_ge(pool_chain, done[0])

            used = [0]
            chain(pool.memset(neghalf[:, :], -0.5))
            chain(pool.memset(ident[:, :], 0.0))
            pool.affine_select(out=ident[:, :], in_=ident[:, :], compare_op=ALU.not_equal, fill=1.0, base=0,
                               pattern=[[-1, P]], channel_multiplier=1).then_inc(consts, 1)

            def rstd(which, t, n, scale, waited, signal, src=None, dst=None, rows=P):
                pool.wait_ge(waited, t + 1)
                src = stats[:, which, t:t + 1] if src is None else src
                dst = stats[:, which + 3, t:t + 1] if dst is None else dst
                at = used[0]
                used[0] += n
                chain(pool.tensor_scalar(ms[0:rows, at:at + n], src[0:rows], scale, EPS, ALU.mult, ALU.add))
                pool.tensor_tensor(dst[0:rows], ms[0:rows, at:at + n], neghalf[0:rows, 0:n], ALU.pow).then_inc(signal, 1)

            rstd(0, 0, 1, 1.0 / D, ssq_ready, rstd_ready)
            rstd(0, 1, 1, 1.0 / D, ssq_ready, rstd_ready)
            chain(pool.memset(causal[:, :], 1.0))
            chain(pool.affine_select(out=causal[:, :], in_=causal[:, :], compare_op=ALU.is_ge, fill=0.0,
                                     base=0, pattern=[[1, P]], channel_multiplier=-1))
            chain(pool.memset(causal[0:CHUNK, CHUNK:P], 0.0))
            chain(pool.memset(decay_m[:, 0, :], 0.0))
            for c in range(2):
                part = decay_m[c * CHUNK:(c + 1) * CHUNK, 0, c * CHUNK:(c + 1) * CHUNK]
                chain(pool.memset(part, 1.0))
                chain(pool.affine_select(out=part, in_=part, compare_op=ALU.is_ge, fill=0.0, base=CHUNK // 2,
                                         pattern=[[0, CHUNK]], channel_multiplier=-1))
            chain(pool.tensor_tensor(decay_m[:, 0, :], causal[:, :], decay_m[:, 0, :], ALU.subtract))
            chain(pool.tensor_copy(decay_m[:, 1, :], causal[:, :]))
            chain(pool.memset(tail_m[:, :], 1.0))
            chain(pool.affine_select(out=tail_m[:, :], in_=tail_m[:, :], compare_op=ALU.is_ge, fill=0.0, base=-1,
                                     pattern=[[-1, P]], channel_multiplier=1))
            chain(pool.memset(tail_m[CHUNK:P, 0:CHUNK], 0.0))
            chain(pool.memset(ones[:, :], 1.0))
            chain(pool.affine_select(out=earlier[:, :], in_=ones[:, :], compare_op=ALU.is_ge, fill=0.0, base=-1,
                                     pattern=[[1, P]], channel_multiplier=-1))
            chain(pool.memset(qbd[:, :, :, :], 0.0))
            for t in range(2, NT):
                rstd(0, t, 1, 1.0 / D, ssq_ready, rstd_ready, rows=rows_of(t))
            base = rt[:, :, :].rearrange("p a b -> p (a b)")[:, 0:WINDOW + CHUNK]
            for b in range(KV):
                chain(pool.iota(base[b * CHUNK:(b + 1) * CHUNK, :], pattern=[[-1, WINDOW + CHUNK]], base=WINDOW,
                                channel_multiplier=1, allow_small_or_imprecise_dtypes=True))
            chain(pool.tensor_scalar(bias[:, 0, :], base, 0.0, None, ALU.min))
            chain(pool.tensor_scalar(base, base, 0.0, None, ALU.max))
            chain(pool.tensor_tensor(base, base, bias[:, 0, :], ALU.subtract))
            for b in range(KV):
                for m in range(GROUP):
                    slope = 2.0 ** (-8.0 * (m + GROUP * b + 1) / HEADS)
                    rows = slice(b * CHUNK, (b + 1) * CHUNK)
                    chain(pool.tensor_scalar(bias[rows, m, :], base[rows, :], -slope, None, ALU.mult))
            pool.sem_inc(bias_ready, 1)
            for out, n, first, step in ((iota4, 4, 0, 1), (iota16, NE, 0, 1), (iota8, MAX_OVER, 0, 1),
                                        (iota_p, P, 0, 1), (limits, TERMS, P, P)):
                chain(pool.iota(out[:, :], pattern=[[step, n]], base=first, channel_multiplier=0,
                                allow_small_or_imprecise_dtypes=True))
            chain(pool.memset(upto[:, :, :], 1.0))
            chain(pool.affine_select(out=upto[:, :, :], in_=upto[:, :, :], compare_op=ALU.is_ge, fill=0.0, base=0,
                                     pattern=[[1, NE], [-1, NE]], channel_multiplier=0))
            chain(pool.iota(pair_val[:, :, :], pattern=[[1, 2], [2 * P, NT]], base=1, channel_multiplier=2,
                            allow_small_or_imprecise_dtypes=True))
            pool.memset(pair_val[rows_of(NT - 1):P, :, NT - 1:NT], 0.0).then_inc(consts, 1)

            wait_emptied(pool, "q")
            for c in range(NCHUNK):
                if c >= 2:
                    pool.wait_ge(scores_ready, c - 1)
                for b in range(KV):
                    rows = slice(b * HD, (b + 1) * HD)
                    pool.tensor_copy(qbd[rows, c % 2, :, b * CHUNK:(b + 1) * CHUNK],
                                     qa[rows, :, c * CHUNK:(c + 1) * CHUNK]).then_inc(qbd_ready, 1)
                    pool.wait_ge(qbd_ready, KV * c + b + 1)

            for t in range(NT):
                if t:
                    rstd(1, t - 1, 1, 1.0 / D, ssq2_ready, rstd2_ready)
                rstd(0, t, BH, 1.0 / BK, osq_ready, ro_ready, osq[:, :], ro[:, :], rows_of(t))
            rstd(1, NT - 1, 1, 1.0 / D, ssq2_ready, rstd2_ready, rows=rows_of(NT - 1))

            pool.wait_ge(out_ready, 2 * NT)
            pool.memset(xg[:, :, :], 0.0).then_inc(xg_clear, 1)
            for par in range(2):
                cols = slice(par * 512, par * 512 + 512)
                pool.dma_start(gf_bc[:, cols], io["gf"][cols].partition_broadcast(P)).then_inc(stored[par], 16)
            pool.wait_ge(xg_clear, 1)
            for t in range(NT):
                pool.wait_ge(h2_stored[t], 16)
            pool.wait_ge(table_ready, 1)

            def gather(s, slot, copies):
                pool.tensor_copy(now_tok[:, slot, :], table_tok[:, bass.ds(s, 1)]).then_inc(col_copied, 1)
                pool.wait_ge(col_copied, copies)
                if not isinstance(s, int):
                    pool.wait_ge(x_turned_b, s - AHEAD + 1)
                    pool.sem_inc(dma_cleared, 1)
                pool.indirect_dma_start(
                    xg[:, slot, :], None, h2_dram, bass.IndirectOffsetOnAxis(ap=now_tok[:, slot, :], axis=0),
                    bounds_check=TOK - 1, oob_is_err=False).then_inc(gathered[slot], 16)

            for s in range(AHEAD):
                gather(s, s, s + 1)
            pool.wait_ge(steer_ready, 1)
            turns = pool.value_load(steer[0:1, 0:1], min_val=NE // UNROLL, max_val=BLOCKS // UNROLL)
            with pool.Fori(0, turns) as i:
                for slot in range(UNROLL):
                    s = UNROLL * i + slot
                    gather(s + AHEAD, (slot + AHEAD) % UNROLL, 2 * s + AHEAD + 1)
                    pool.tensor_copy(now_pair[:, slot, :], table[:, bass.ds(s, 1)]).then_inc(col_copied, 1)
                    pool.wait_ge(col_copied, 2 * s + AHEAD + 2)
                    pool.wait_ge(y_act, s + 3)
                    pool.wait_ge(y_dve, s + 3)
                    pool.sem_inc(dma_cleared, 1)
                    pool.indirect_dma_start(
                        y_dram, bass.IndirectOffsetOnAxis(ap=now_pair[:, slot, :], axis=0),
                        y[:, slot % 2, :], None, bounds_check=PAIRS - 1, oob_is_err=False).then_inc(
                            stored[slot % 2], 16)

            for t in range(NT):
                rstd(2, t, 1, 1.0 / D, ssq3_ready, rstd3_ready, rows=rows_of(t))

        @block.scalar
        def _(act):
            for t in range(NT):
                src = io["x_p"][tok(t), :] if t < PROMPT_TILES else io["x_s"]
                act.dma_start(x[0:rows_of(t), t, :], src).then_inc(x_in[t], 16)
                if t == 0:
                    act.dma_start(g1_bc, io["g1"].partition_broadcast(P)).then_inc(g1_in, 16)
            act.dma_start(lb_t[:, :], io["lower"].rearrange("a k -> (a k)").partition_broadcast(P)).then_inc(lb_in, 16)
            for b in range(KV):
                act.dma_start(sink_bc[b * CHUNK:(b + 1) * CHUNK, :],
                              io["sink"][b * GROUP:(b + 1) * GROUP].partition_broadcast(CHUNK)).then_inc(sink_in, 16)
            act.dma_start(ng_bc[:, :], io["ng"].partition_broadcast(P)).then_inc(ng_in, 16)
            act.dma_start(g2_bc[:, :], io["g2"].partition_broadcast(P)).then_inc(g2_in, 16)
            act.dma_start(w_route[:, :, 0:NG], io["w_rg"].rearrange("(c p) g -> p c g", p=P)).then_inc(route_in, 16)
            for g in range(NG):
                act.dma_start(w_route[:, :, NG + g * EPG:NG + (g + 1) * EPG],
                              io["w_re"][g].rearrange("(c p) e -> p c e", p=P)).then_inc(route_in, 16)
            act.dma_start(b_route[:, 0:NG], io["b_rg"].partition_broadcast(P)).then_inc(route_in, 16)
            act.dma_start(b_route[:, NG:NG + NE], io["b_re"].rearrange("g e -> (g e)").partition_broadcast(P)).then_inc(
                route_in, 16)

            def square_sum(t, which, signal):
                r = rows_of(t)
                if t:
                    act.wait_ge(signal, t)
                act.activation(junk[0:r, :], x[0:r, t, :], ACT.Square,
                               accum_out=stats[0:r, which, t:t + 1]).then_inc(signal, 1)

            def hT_half(t):
                act.wait_ge(turned, t + 1)
                r = rows_of(t)
                act.activation(hT[:, 0:4, tok(t)], bank(2 + 2 * (t % 3)).rearrange("p (c t) -> p c t", c=4)[:, :, 0:r],
                               ACT.Copy).then_inc(hT_act, 1)

            for t in range(2):
                act.wait_ge(x_in[t], 16)
                square_sum(t, 0, ssq_ready)
            act.wait_ge(lb_diff, 1)
            act.activation(lb_t[:, :], lb_t[:, :], ACT.Exp).then_inc(lb_exp, 1)
            for t in range(2, NT):
                act.wait_ge(x_in[t], 16)
                square_sum(t, 0, ssq_ready)
                hT_half(t - 2)
            hT_half(NT - 2)
            hT_half(NT - 1)

            def empty(n):
                kind, t, _ = groups[n]
                act.wait_ge(proj_ready, n + 1)
                b = n % 2
                if kind == "f":
                    ins = act.activation(logf[0:rows_of(t), t, :], ps[0:rows_of(t), b, :], ACT.Sigmoid)
                elif kind == "v":
                    slot = t if t < PROMPT_TILES else 5
                    ins = act.activation(V[0:rows_of(t), slot, :], ps[0:rows_of(t), b, 0:KVW], ACT.Copy)
                elif kind == "q":
                    ins = act.activation(qa[:, t // 2, t % 2 * HALF:(t % 2 + 1) * HALF], bank(b, HALF), ACT.Copy,
                                         scale=float(HD) ** -0.5)
                elif kind == "i":
                    ins = act.activation(vf[0:rows_of(t), t, :], ps[0:rows_of(t), b, :], ACT.Copy)
                else:
                    ins = act.activation(gg[0:rows_of(t), t, :], ps[0:rows_of(t), b, :], ACT.Silu)
                ins.then_inc(proj_act, 1)

            for n in range(first_filler):
                if groups[n][2] == "act":
                    empty(n)
                if groups[n][0] == "k" and groups[n][1] == 1:
                    for t in range(NT):
                        act.wait_ge(f_ready, t + 1)
                        act.activation(logf[0:rows_of(t), t, :], logf[0:rows_of(t), t, :], ACT.Ln).then_inc(logf_ready, 1)

            def exps(c):
                lo, hi, _, _ = window(c)
                par = c % 2
                act.wait_ge(negm_ready, c + 1)
                act.activation(small[:, 3, par, :], small[:, 2, par, :], ACT.Exp)
                for m in range(GROUP):
                    last = act.activation(s_buf[:, par, m, lo:hi], s_buf[:, par, m, lo:hi], ACT.Exp,
                                          bias=small[:, 1, par, m:m + 1], accum_out=small[:, 4, par, m:m + 1])
                last.then_inc(exp_done, 1)

            def pt_before(c):
                act.wait_ge(p_turned, c + 1)
                act.wait_ge(pv_done, c - 1)
                act.activation(pt[:, c % 2, 0, :], bank(4), ACT.Copy).then_inc(pt_act, 1)

            for s, fill in enumerate(slots):
                if s == NCHUNK:
                    wait_emptied(act, "b")
                    act.activation(qf[:, :, :], qf[:, :, :], ACT.Silu).then_inc(qf_ready, 1)
                for n in fill:
                    if groups[n][2] == "act":
                        empty(n)
                if has_before(s - 1) and s - 1 < NCHUNK:
                    pt_before(s - 1)
                if s < NCHUNK:
                    exps(s)

            def cum_exps(t):
                r = rows_of(t)
                act.wait_ge(cum_ready, t + 1)
                if t:
                    act.wait_ge(rec_sum, t)
                cums = ps[:, 2:4, :].rearrange("p b (h w t) -> p (b h) w t", h=2, w=2)
                act.activation(qin[:, :, 0:r], cums[:, :, 0, 0:r], ACT.Exp).then_inc(cum_exp, 1)
                act.activation(kin[:, :, 0:r], cums[:, :, 0, 0:r], ACT.Exp, scale=-1.0).then_inc(cum_exp, 1)
                act.activation(qex[:, :, 0:r], cums[:, :, 1, 0:r], ACT.Exp).then_inc(cum_exp, 1)
                act.activation(kdec[0:r, :, :], ps[0:r, 5, :].rearrange("p (h k) -> p h k", h=BH),
                               ACT.Exp).then_inc(cum_exp, 1)

            def second_norm(t):
                act.wait_ge(x2_ready, 2 * t + 2)
                r = rows_of(t)
                act.activation(qa_flat[0:r, 0:D], x[0:r, t, :], ACT.Square,
                               accum_out=stats[0:r, 1, t:t + 1]).then_inc(ssq2_ready, 1)

            def h2T_half(t):
                act.wait_ge(h2_turned, t + 1)
                act.activation(h2T[:, t % 2, 0:512], bank(2), ACT.Copy).then_inc(h2T_act, 1)

            for t in range(NT):
                r = rows_of(t)
                cum_exps(t)
                if t:
                    second_norm(t - 1)
                act.wait_ge(rec_sum, t + 1)
                for h in range(BH):
                    cols = slice(h * BK, (h + 1) * BK)
                    last = act.activation(logf[0:r, t, cols], ps[0:r, 5, cols], ACT.Square,
                                          accum_out=osq[0:r, h:h + 1])
                last.then_inc(osq_ready, 1)
                act.wait_ge(rec_turned, t + 1)
                act.activation(mixT[:, BH:KC, tok(t)], bank(6).rearrange("p (h t) -> p h t", h=BH)[:, :, 0:r],
                               ACT.Copy).then_inc(rec_taken, 1)
                if t:
                    h2T_half(t - 1)
            second_norm(NT - 1)
            h2T_half(NT - 1)

            for k in range(2):
                act.wait_ge(route_diff, k + 1)
                act.activation(rb[:, :, 0:4] if k == 0 else rb[:, :, 4:5],
                               rb[:, :, 0:4] if k == 0 else rb[:, :, 4:5], ACT.Exp).then_inc(route_exp, 1)

            def x_half(s):
                act.wait_ge(x_turned_a, s + 1)
                act.activation(xT[:, 0:4, :], bank(1).rearrange("p (c t) -> p c t", c=4), ACT.Copy).then_inc(xT_act, 1)

            x_half(0)
            act.sem_inc(y_act, 2)
            act.wait_ge(steer_ready, 1)
            turns = act.value_load(steer[0:1, 0:1], min_val=NE // UNROLL, max_val=BLOCKS // UNROLL)
            with act.Fori(0, turns) as i:
                for slot in range(UNROLL):
                    s = UNROLL * i + slot
                    act.wait_ge(gu_ready, s + 1)
                    act.activation(sg[:, :], ps[:, 0, 0:FE], ACT.Silu).then_inc(silu_ready, 1)
                    x_half(s + 1)
                    act.wait_ge(y_ready, s + 1)
                    act.wait_ge(stored[slot % 2], 16 * (2 * i + slot // 2 + 1))
                    act.activation(y[:, slot % 2, 0:512], bank(4 + 2 * (slot % 2)), ACT.Copy).then_inc(y_act, 1)

            for t in range(NT):
                r = rows_of(t)
                act.wait_ge(sum_ready, 2 * t + 2)
                act.activation(pair[0:r, t, D:2 * D], x[0:r, t, :], ACT.Square,
                               accum_out=stats[0:r, 2, t:t + 1]).then_inc(ssq3_ready, 1)

        @block.vector
        def _(dve):
            done = [0]

            def chain(ins):
                done[0] += 1
                ins.then_inc(dve_chain, 1)
                dve.wait_ge(dve_chain, done[0])

            def h_tile(t):
                dve.wait_ge(rstd_ready, t + 1)
                if t >= 2:
                    dve.wait_ge(turned, t - 1)
                r = rows_of(t)
                dve.scalar_tensor_tensor(hn[0:r, t % 2, :], x[0:r, t, :], stats[0:r, 3, t:t + 1], g1_bc[0:r, :],
                                         ALU.mult, ALU.mult).then_inc(hn_ready, 1)

            def hT_half(t):
                dve.wait_ge(turned, t + 1)
                r = rows_of(t)
                dve.tensor_copy(hT[:, 4:8, tok(t)],
                                bank(3 + 2 * (t % 3)).rearrange("p (c t) -> p c t", c=4)[:, :, 0:r]).then_inc(hT_dve, 1)

            dve.wait_ge(g1_in, 16)
            h_tile(0)
            h_tile(1)
            hT_half(0)
            dve.wait_ge(lb_in, 16)
            l0, l1 = lb_t[:, 0:BW], lb_t[:, BW:2 * BW]
            chain(dve.tensor_tensor(lb, l0, l1, ALU.max))
            chain(dve.tensor_tensor(l0, l0, lb, ALU.subtract))
            dve.tensor_tensor(l1, l1, lb, ALU.subtract).then_inc(lb_diff, 1)
            for t in range(2, NT):
                h_tile(t)
                hT_half(t - 1)
            hT_half(NT - 1)
            dve.wait_ge(lb_exp, 1)
            chain(dve.tensor_tensor(oml, l0, l1, ALU.add))
            chain(dve.reciprocal(oml, oml))
            chain(dve.tensor_tensor(lb, l0, oml, ALU.mult))
            chain(dve.tensor_scalar(oml, lb, -1.0, 1.0, ALU.mult, ALU.add))

            def gate_f(t):
                r = rows_of(t)
                dve.wait_ge(proj_act, t + 1)
                chain(dve.tensor_tensor(logf[0:r, t, :], logf[0:r, t, :], oml[0:r, :], ALU.mult))
                chain(dve.tensor_tensor(logf[0:r, t, :], logf[0:r, t, :], lb[0:r, :], ALU.add))
                dve.tensor_scalar(kf[0:r, t, :], logf[0:r, t, :], -1.0, 1.0, ALU.mult, ALU.add).then_inc(f_ready, 1)

            def empty(n):
                kind, i, _ = groups[n]
                dve.wait_ge(proj_ready, n + 1)
                b = n % 2
                if kind == "k":
                    if i == 0:
                        ins = dve.tensor_copy(kT[:, 0:HALF], bank(b, HALF))
                    else:
                        dve.tensor_copy(kT[:, HALF:SEQ], ps[:, b, 0:SEQ - HALF])
                        ins = dve.tensor_copy(kT[:, SEQ + WINDOW:], ps[:, b, SEQ - HALF:HALF])
                elif kind == "q":
                    ins = dve.tensor_scalar(qa[:, i // 2, i % 2 * HALF:(i % 2 + 1) * HALF], bank(b, HALF),
                                            float(HD) ** -0.5, None, ALU.mult)
                else:
                    ins = dve.tensor_copy(qf[:, i // 2, i % 2 * HALF:(i % 2 + 1) * HALF], bank(b, HALF))
                ins.then_inc(proj_dve, 1)

            for t in range(NT):
                gate_f(t)
            dve.memset(s_buf[:, 1, :, 0:CHUNK], 0.0).then_inc(dve_consts, 1)
            dve.wait_ge(cache_turned, 1)
            dve.tensor_copy(kT[:, SEQ:SEQ + WINDOW], ps[:, 7, 0:P]).then_inc(cache_taken, 1)
            for n in range(first_filler):
                if groups[n][2] == "dve":
                    empty(n)

            def softmax_head(c):
                lo, hi, off, _ = window(c)
                par = c % 2
                dve.wait_ge(scores_ready, c + 1)
                if c == 0:
                    dve.wait_ge(bias_ready, 1)
                    dve.wait_ge(sink_in, 32)
                dve.tensor_tensor(s_buf[:, par, :, lo:hi],
                                  ps[:, 2:4, :].rearrange("p b (m k) -> p (b m) k", m=2)[:, :, lo:hi],
                                  bias[:, :, lo - off:hi - off], ALU.add).then_inc(scores_taken, 1)
                dve.wait_ge(scores_taken, c + 1)
                chain(dve.tensor_reduce(small[:, 0, par, :], s_buf[:, par, :, lo:hi], AX.X, ALU.max))
                chain(dve.tensor_tensor(small[:, 0, par, :], small[:, 0, par, :], sink_bc[:, :], ALU.max))
                chain(dve.tensor_scalar(small[:, 1, par, :], small[:, 0, par, :], -1.0, None, ALU.mult))
                dve.tensor_tensor(small[:, 2, par, :], sink_bc[:, :], small[:, 0, par, :],
                                  ALU.subtract).then_inc(negm_ready, 1)

            def softmax_tail(c):
                lo, hi, _, _ = window(c)
                par = c % 2
                dve.wait_ge(exp_done, c + 1)
                chain(dve.tensor_tensor(small[:, 5, par, :], small[:, 4, par, :], small[:, 3, par, :], ALU.add))
                chain(dve.reciprocal(small[:, 5, par, :], small[:, 5, par, :]))
                for m in range(GROUP):
                    last = dve.tensor_scalar(s_buf[:, par, m, lo:hi], s_buf[:, par, m, lo:hi],
                                             small[:, 5, par, m:m + 1], None, ALU.mult)
                last.then_inc(p_ready, 1)

            def pt_with(c):
                r = P if c % 2 else CHUNK
                dve.wait_ge(p_turned, c + 1)
                if c >= 2:
                    dve.wait_ge(pv_done, c - 1)
                dve.tensor_copy(pt[0:r, c % 2, 1, :], ps[0:r, 5, :]).then_inc(pt_dve, 1)

            def take_o(c):
                dve.wait_ge(pv_done, c + 1)
                dve.tensor_copy(mixT[:, 0:GROUP, c * CHUNK:(c + 1) * CHUNK],
                                ps[:, 6, 0:GROUP * CHUNK].rearrange("p (m q) -> p m q", m=GROUP)).then_inc(o_taken, 1)

            def gain(t):
                r = rows_of(t)
                dve.wait_ge(proj_act, emptied[of_kind["g"][t]][1])
                if t == 0:
                    dve.wait_ge(ng_in, 16)
                dve.tensor_tensor(gg[0:r, t, :], gg[0:r, t, :], ng_bc[0:r, :], ALU.mult).then_inc(gg_ready, 1)

            for s, fill in enumerate(slots):
                if 1 <= s <= NCHUNK:
                    softmax_tail(s - 1)
                for n in fill:
                    if groups[n][2] == "dve":
                        empty(n)
                if s < NCHUNK:
                    softmax_head(s)
                if 1 <= s <= NCHUNK:
                    pt_with(s - 1)
                if 2 <= s < NCHUNK + 2:
                    take_o(s - 2)
            dve.wait_ge(kout_turned, 1)
            chain(dve.tensor_copy(kout[:, 0, :], ps[:, 6, 0:P]))
            dve.tensor_copy(kout[0:DEC, 1, :], ps[0:DEC, 6, P:2 * P]).then_inc(kout_ready, 1)
            for t in range(NT):
                gain(t)
            dve.wait_ge(proj_ready, len(groups))
            chain(dve.memset(aT[:, :, :], 0.0))

            def operands(t):
                r = rows_of(t)
                nch = r // CHUNK
                dve.wait_ge(cum_exp, 4 * t + 1)
                dve.wait_ge(qf_ready, 1)
                dve.tensor_tensor(qin[:, :, 0:r], qin[:, :, 0:r], qf[:, :, tok(t)], ALU.mult).then_inc(hops_ready, 1)
                dve.wait_ge(cum_exp, 4 * t + 2)
                dve.tensor_tensor(kin[:, :, 0:r], kin[:, :, 0:r],
                                  bank(4).rearrange("p (h t) -> p h t", h=BH)[:, :, 0:r],
                                  ALU.mult).then_inc(hops_ready, 1)
                dve.wait_ge(cum_exp, 4 * t + 3)
                chain(dve.tensor_copy(dec[:, :, 0:nch], qex[:, :, CHUNK - 1:r:CHUNK]))
                dve.tensor_tensor(qex[:, :, 0:r], qex[:, :, 0:r], qf[:, :, tok(t)], ALU.mult).then_inc(hops_ready, 1)
                dve.wait_ge(cum_exp, 4 * t + 4)
                dve.tensor_tensor(kdec[0:r, :, :], kdec[0:r, :, :],
                                  kf[0:r, t, :].rearrange("p (h k) -> p h k", h=BH), ALU.mult).then_inc(hops_ready, 1)

            def add_out(t, half):
                r = rows_of(t)
                dve.wait_ge(out_ready, 2 * t + half + 1)
                cols = slice(512 * half, 512 * half + 512)
                dve.tensor_tensor(x[0:r, t, cols], x[0:r, t, cols], ps[0:r, half, :], ALU.add).then_inc(x2_ready, 1)

            def inner_and_states(t):
                r = rows_of(t)
                dve.wait_ge(inner_ready, t + 1)
                dve.copy_predicated(aT[0:r, :, 0:r], causal[0:r, 0:r].bitcast(I32).unsqueeze(1).to_broadcast([r, BH, r]),
                                    ps[0:r, 6, :].rearrange("p (h t) -> p h t", h=BH)[:, :, 0:r]).then_inc(at_ready, 1)
                for c in range(r // CHUNK):
                    n = 2 * t + c
                    before = St[n % 3] if t < PROMPT_TILES else s_sample
                    after = St[(n + 1) % 3] if t < PROMPT_TILES else St[0]
                    ds = bank(7) if c == 0 else bank(4)
                    if c:
                        dve.wait_ge(state_ready, n)
                    if n == 0:
                        last = dve.tensor_copy(after[:, :], ds)
                    else:
                        if t == NT - 1:
                            dve.wait_ge(s_in, 16)
                        for h in range(BH):
                            cols = slice(h * BK, (h + 1) * BK)
                            last = dve.scalar_tensor_tensor(after[:, cols], before[:, cols], dec[:, h, c:c + 1],
                                                            ds[:, cols], ALU.mult, ALU.add)
                    last.then_inc(state_ready, 1)

            def normed(t):
                r = rows_of(t)
                dve.wait_ge(ro_ready, t + 1)
                dve.wait_ge(gg_ready, t + 1)
                if t:
                    dve.wait_ge(rec_turned, t)
                for h in range(BH):
                    cols = slice(h * BK, (h + 1) * BK)
                    last = dve.scalar_tensor_tensor(rec[0:r, cols], ps[0:r, 5, cols], ro[0:r, h:h + 1],
                                                    gg[0:r, t, cols], ALU.mult, ALU.mult)
                last.then_inc(rec_ready, 1)

            def second(t):
                r = rows_of(t)
                dve.wait_ge(rstd2_ready, t + 1)
                if t == 0:
                    dve.wait_ge(g2_in, 16)
                    dve.wait_ge(route_in, 16 * (3 + NG))
                if t >= 2:
                    dve.wait_ge(h2_stored[t - 2], 16)
                    dve.wait_ge(h2_turned, t - 1)
                dve.scalar_tensor_tensor(h2[0:r, t % 2, :], x[0:r, t, :], stats[0:r, 4, t:t + 1], g2_bc[0:r, :],
                                         ALU.mult, ALU.mult).then_inc(h2_ready, 1)
                dve.wait_ge(h2_turned, t + 1)
                dve.tensor_copy(h2T[:, t % 2, 512:1024], bank(3)).then_inc(h2T_dve, 1)
                dve.wait_ge(logits_ready, t + 1)
                dve.tensor_tensor(logits[0:r, t, :], ps[0:r, 7, 0:NG], b_route[0:r, 0:NG], ALU.add)
                dve.tensor_tensor(elogits[0:r, t, :], ps[0:r, 7, NG:NG + NE], b_route[0:r, NG:NG + NE],
                                  ALU.add).then_inc(logits_taken, 1)

            dve.memset(logits[:, :, :], 0.0)
            chain(dve.memset(elogits[:, :, :], 0.0))
            for t in range(NT):
                operands(t)
                if t:
                    add_out(t - 1, 0)
                inner_and_states(t)
                if t:
                    add_out(t - 1, 1)
                normed(t)
                if t:
                    second(t - 1)
            add_out(NT - 1, 0)
            add_out(NT - 1, 1)
            second(NT - 1)

            dve.wait_ge(logits_taken, NT)
            dve.wait_ge(consts, 2)
            rv = rt[:, :, :].rearrange("p a b -> p (a b)")

            def col(i, n=1):
                v = rv[:, i * NT:(i + n) * NT]
                return v if n == 1 else v.rearrange("p (t k) -> p t k", k=n)

            def spread(v, n):
                return v.unsqueeze(2).to_broadcast([P, NT, n])

            def first_max(v, top, hot, scratch):
                chain(dve.tensor_reduce(top, v, AX.X, ALU.max))
                chain(dve.tensor_tensor(scratch, v, spread(top, 4), ALU.is_ge))
                chain(dve.scalar_tensor_tensor(scratch, scratch, -8.0, i4, ALU.mult, ALU.add))
                chain(dve.tensor_reduce(col(3), scratch, AX.X, ALU.min))
                chain(dve.tensor_scalar(col(3), col(3), 8.0, None, ALU.add))
                chain(dve.tensor_tensor(hot, i4, spread(col(3), 4), ALU.is_equal))

            i4 = iota4[:, :].unsqueeze(1).to_broadcast([P, NT, 4])
            group_hot, hot1, hot2, el, scr = (col(a, 4) for a in (8, 12, 16, 20, 24))
            first_max(logits[:, :, :], col(0), group_hot, scr)
            dve.tensor_tensor(rb[:, :, 0:4], logits[:, :, :], spread(col(0), 4), ALU.subtract).then_inc(route_diff, 1)
            picked = picks[:, 0, :, :]
            chain(dve.tensor_tensor(picked.rearrange("p t (g e) -> p (t g) e", g=NG),
                                    elogits[:, :, :].rearrange("p t (g e) -> p (t g) e", g=NG),
                                    group_hot.rearrange("p t g -> p (t g)").unsqueeze(2).to_broadcast(
                                        [P, NT * NG, EPG]), ALU.mult))
            chain(dve.tensor_reduce(el, picked.rearrange("p t (g e) -> p t e g", g=NG), AX.X, ALU.add))
            first_max(el, col(1), hot1, scr)
            chain(dve.scalar_tensor_tensor(el, hot1, -3.0e38, el, ALU.mult, ALU.add))
            first_max(el, col(2), hot2, scr)
            dve.tensor_tensor(rb[:, :, 4:5], spread(col(2), 1), spread(col(1), 1), ALU.subtract).then_inc(route_diff, 1)
            for i, hot in enumerate((hot1, hot2)):
                last = dve.tensor_tensor(picks[:, i, :, :].rearrange("p t (g e) -> p t g e", g=NG),
                                         group_hot.unsqueeze(3).to_broadcast([P, NT, NG, EPG]),
                                         hot.unsqueeze(2).to_broadcast([P, NT, NG, EPG]), ALU.mult)
            chain(last)
            chain(dve.memset(picks[rows_of(NT - 1):P, 0:2, NT - 1, :], 0.0))
            chain(dve.tensor_tensor(picks[:, 2, :, :], picks[:, 0, :, :], picks[:, 1, :, :], ALU.add))
            dve.memset(before[:, 0, :], 0.0)
            chain(dve.tensor_copy(before[:, 1, :], picks[:, 2, 0, :]))
            for t in range(1, NT):
                last = dve.tensor_tensor(before[:, t + 1, :], before[:, t, :], picks[:, 2, t, :], ALU.add)
                if t < NT - 1:
                    chain(last)
            last.then_inc(picks_ready, 1)
            dve.wait_ge(rank_ready, 1)
            chain(dve.tensor_copy(rank_v[:, :, :], ps[:, 0, 0:NT * NE].rearrange("p (t e) -> p t e", e=NE)))
            over, incl, move = (per_expert[:, a, :] for a in range(3))
            rank, expert, j, block = (per_pair[:, a, :, :] for a in range(4))
            limit_e = limits[:, :].unsqueeze(1).to_broadcast([P, NE, TERMS])
            chain(dve.tensor_tensor(compared[:, :, 0:TERMS], ps[:, 1, 0:NE].unsqueeze(2).to_broadcast([P, NE, TERMS]),
                                    limit_e, ALU.is_gt))
            chain(dve.tensor_reduce(over, compared[:, :, 0:TERMS], AX.X, ALU.add))
            chain(dve.tensor_tensor(compared[:, :, :], upto[:, :, :], over.unsqueeze(1).to_broadcast([P, NE, NE]),
                                    ALU.mult))
            chain(dve.tensor_reduce(incl, compared[:, :, :], AX.X, ALU.add))
            chain(dve.scalar_tensor_tensor(move, incl, float(NE - 1), over, ALU.add, ALU.subtract))
            chain(dve.tensor_tensor(move, move, iota16[:, :], ALU.subtract))

            def of_pick(dst, values):
                chain(dve.tensor_tensor(picked_v[:, :, :, :], picks[:, 0:2, :, :], values, ALU.mult))
                chain(dve.tensor_reduce(dst, picked_v[:, :, :, :], AX.X, ALU.add))

            def for_all(v):
                return v.unsqueeze(1).unsqueeze(1).to_broadcast([P, 2, NT, NE])

            of_pick(rank, rank_v[:, :, :].unsqueeze(1).to_broadcast([P, 2, NT, NE]))
            of_pick(expert, for_all(iota16[:, :]))
            of_pick(block, for_all(move))
            compared_j = compared[:, 0:2 * NT, 0:TERMS]
            chain(dve.tensor_tensor(compared_j, rank.rearrange("p i t -> p (i t)").unsqueeze(2).to_broadcast(
                [P, 2 * NT, TERMS]), limits[:, :].unsqueeze(1).to_broadcast([P, 2 * NT, TERMS]), ALU.is_ge))
            chain(dve.tensor_reduce(j.rearrange("p i t -> p (i t)"), compared_j, AX.X, ALU.add))
            chain(dve.tensor_tensor(block, block, j, ALU.add))
            chain(dve.scalar_tensor_tensor(block, j, 0.0, block, ALU.is_gt, ALU.mult))
            chain(dve.tensor_tensor(block, block, expert, ALU.add))
            chain(dve.scalar_tensor_tensor(rank, j, -float(P), rank, ALU.mult, ALU.add))
            pairs = [P, 2 * NT, P]
            dve.tensor_tensor(slot_hot[:, :, :, :].rearrange("p i t s -> p (i t) s"),
                              iota_p[:, :].unsqueeze(1).to_broadcast(pairs),
                              rank.rearrange("p i t -> p (i t)").unsqueeze(2).to_broadcast(pairs), ALU.is_equal)
            pairs = [P, 2 * NT, COLS]
            block_v = block_hot[:, :, :, :].rearrange("p i t s -> p (i t) s")
            chain(dve.tensor_tensor(block_v, iota_p[:, 0:COLS].unsqueeze(1).to_broadcast(pairs),
                                    block.rearrange("p i t -> p (i t)").unsqueeze(2).to_broadcast(pairs),
                                    ALU.is_equal))
            dve.tensor_tensor(block_v, block_v, pair_val[:, :, :].rearrange("p i t -> p (i t)").unsqueeze(
                2).to_broadcast(pairs), ALU.mult).then_inc(hot_ready, 1)
            total = incl[:, NE - 1:NE]
            turn = col(6)[:, 0:1]
            chain(dve.tensor_scalar(turn, total, 0.0, float(NE // UNROLL), ALU.is_gt, ALU.add))
            for k in range(UNROLL, MAX_OVER, UNROLL):
                chain(dve.tensor_scalar(col(6)[:, 1:2], total, float(k), None, ALU.is_gt))
                chain(dve.tensor_tensor(turn, turn, col(6)[:, 1:2], ALU.add))
            chain(dve.tensor_tensor(over_hot[:, :, :], incl.unsqueeze(1).to_broadcast([P, MAX_OVER, NE]),
                                    iota8[:, :].unsqueeze(2).to_broadcast([P, MAX_OVER, NE]), ALU.is_le))
            chain(dve.tensor_reduce(col(7, 2).rearrange("p t k -> p (t k)")[:, 0:MAX_OVER], over_hot[:, :, :],
                                    AX.X, ALU.add))
            chain(dve.tensor_scalar(steer[:, 1:1 + MAX_OVER], col(7, 2).rearrange("p t k -> p (t k)")[:, 0:MAX_OVER],
                                    float(NE - 1), None, ALU.min))
            dve.tensor_copy(steer[:, 0:1], turn).then_inc(steer_ready, 1)
            dve.wait_ge(slots_ready, 1)
            chain(dve.tensor_scalar(table_f[:, :], ps[:, 4, 0:COLS], 0.0, float(NOWHERE), ALU.is_equal, ALU.mult))
            chain(dve.scalar_tensor_tensor(table[:, :], ps[:, 4, 0:COLS], -1.0, table_f[:, :], ALU.add, ALU.add))
            dve.tensor_scalar(table_tok[:, :], table[:, :], 1, None, ALU.logical_shift_right).then_inc(table_ready, 1)
            dve.wait_ge(route_exp, 2)
            chain(dve.tensor_reduce(col(4), rb[:, :, 0:4], AX.X, ALU.add))
            chain(dve.tensor_scalar(col(5), rb[:, :, 4], 1.0, None, ALU.add))
            chain(dve.tensor_tensor(col(4), col(4), col(5), ALU.mult))
            chain(dve.reciprocal(gates[:, 0, :], col(4)))
            chain(dve.tensor_tensor(gates[:, 1, :], gates[:, 0, :], rb[:, :, 4], ALU.mult))

            def x_half(s):
                dve.wait_ge(x_turned_b, s + 1)
                dve.tensor_copy(xT[:, 4:8, :], bank(2).rearrange("p (c t) -> p c t", c=4)).then_inc(xT_dve, 1)

            x_half(0)
            dve.sem_inc(y_dve, 2)
            dve.wait_ge(steer_ready, 1)
            turns = dve.value_load(steer[0:1, 0:1], min_val=NE // UNROLL, max_val=BLOCKS // UNROLL)
            with dve.Fori(0, turns) as i:
                for slot in range(UNROLL):
                    s = UNROLL * i + slot
                    dve.wait_ge(silu_ready, s + 1)
                    dve.tensor_tensor(hh[:, :], sg[:, :], ps[:, 0, FE:2 * FE], ALU.mult).then_inc(hh_ready, 1)
                    dve.wait_ge(hh_turned, s + 1)
                    dve.tensor_copy(hhT[:, :, :], ps[:, 3, 0:2 * P].rearrange("p (c t) -> p c t", c=2)).then_inc(
                        hhT_ready, 1)
                    x_half(s + 1)
                    dve.wait_ge(y_ready, s + 1)
                    dve.wait_ge(stored[slot % 2], 16 * (2 * i + slot // 2 + 1))
                    dve.tensor_copy(y[:, slot % 2, 512:1024], bank(5 + 2 * (slot % 2))).then_inc(y_dve, 1)

            def weigh(t):
                r = rows_of(t)
                dve.wait_ge(pair_in[t], 16)
                for i in range(2):
                    dve.scalar_tensor_tensor(x[0:r, t, :], pair[0:r, t, i * D:(i + 1) * D], gates[0:r, i, t:t + 1],
                                             x[0:r, t, :], ALU.mult, ALU.add).then_inc(sum_ready, 1)
                    dve.wait_ge(sum_ready, 2 * t + i + 1)

            def final(t):
                r = rows_of(t)
                dve.wait_ge(rstd3_ready, t + 1)
                dve.scalar_tensor_tensor(pair[0:r, t, 0:D], x[0:r, t, :], stats[0:r, 5, t:t + 1], gf_bc[0:r, :],
                                         ALU.mult, ALU.mult).then_inc(final_ready, 1)

            weigh(0)
            for t in range(1, NT):
                weigh(t)
                final(t - 1)
            final(NT - 1)

        @block.tensor
        def _(pe):
            def turn_x(t):
                r = rows_of(t)
                pe.wait_ge(hn_ready, t + 1)
                if t >= 3:
                    pe.wait_ge(hT_act, t - 2)
                    pe.wait_ge(hT_dve, t - 2)
                for c in range(KC):
                    b = 2 + 2 * (t % 3) + c // 4
                    last = pe.transpose(ps[:, b, (c % 4) * P:(c % 4) * P + r], hn[0:r, t % 2, c * P:(c + 1) * P],
                                        ident[0:r, 0:r])
                last.then_inc(turned, 1)

            def project(n):
                kind, i, _ = groups[n]
                k = ring_of[kind]
                w = w_slot(k)
                if n >= 2:
                    who, v = emptied[n - 2]
                    pe.wait_ge(proj_act if who == "act" else proj_dve, v)
                if i == 0:
                    pe.wait_ge(w_in[k], 16 * KV * KC if kind == "q" else 16)
                b = n % 2
                for c in range(KC):
                    if kind in "fig":
                        r = rows_of(i)
                        last = pe.matmul(ps[0:r, b, :], hT[:, c, tok(i)], w[:, c, :], start=c == 0, stop=c == KC - 1)
                    elif kind == "v":
                        r = rows_of(i)
                        last = pe.matmul(ps[0:r, b, 0:KVW], hT[:, c, tok(i)], w[:, c, KVW:2 * KVW],
                                         start=c == 0, stop=c == KC - 1)
                    else:
                        m, half = i // 2, i % 2
                        if kind == "k":
                            m, half, lhs = 0, i, w[:, c, 0:KVW]
                        elif kind == "q":
                            lhs = w[:, c, m * P:(m + 1) * P]
                        else:
                            lhs = w[:, c, m * BK:(m + 1) * BK]
                        last = pe.matmul(bank(b, HALF), lhs, hT[:, c, half * HALF:(half + 1) * HALF],
                                         start=c == 0, stop=c == KC - 1)
                last.then_inc(proj_ready, 1)

            pe.wait_ge(consts, 1)
            turn_x(0)
            turn_x(1)
            turn_x(2)
            for t in range(NT):
                pe.wait_ge(hT_act, t + 1)
                pe.wait_ge(hT_dve, t + 1)
                project(t)
                if t + 3 < NT:
                    turn_x(t + 3)
            pe.wait_ge(ck_in, 16)
            pe.wait_ge(hT_dve, NT)
            pe.transpose(ps[:, 7, 0:P], kout[:, 0, :], ident[:, :]).then_inc(cache_turned, 1)
            for n in range(NT, first_filler):
                project(n)

            def scores(c):
                lo, hi, _, start = window(c)
                pe.wait_ge(qbd_ready, KV * (c + 1))
                if c == 0:
                    wait_emptied(pe, "k")
                    pe.wait_ge(cache_taken, 1)
                else:
                    pe.wait_ge(scores_taken, c)
                for m in range(GROUP):
                    last = pe.matmul(ps[:, 2 + m // 2, (m % 2) * 2 * P + lo:(m % 2) * 2 * P + hi], qbd[:, c % 2, m, :],
                                     kT[:, start:start + hi - lo], start=True, stop=True)
                last.then_inc(scores_ready, 1)

            def turn_p(c):
                pe.wait_ge(p_ready, c + 1)
                if c == 1:
                    pe.wait_ge(dve_consts, 1)
                if c >= 1:
                    pe.wait_ge(pt_dve, c)
                if c >= 3:
                    pe.wait_ge(pt_act, c - 2)
                r = P if c % 2 else CHUNK
                for m in range(GROUP):
                    if has_before(c):
                        pe.transpose(ps[:, 4, m * P:(m + 1) * P], s_buf[:, c % 2, m, 0:P], ident[:, :])
                    last = pe.transpose(ps[0:r, 5, m * P:(m + 1) * P], s_buf[:, c % 2, m, P:P + r], ident[:, :])
                last.then_inc(p_turned, 1)

            def attend(c):
                slot_a, slot_b = v_slots(c)
                rows_a = slice(CHUNK, P) if c % 2 else slice(0, P)
                rows_b = slice(0, P if c % 2 else CHUNK)
                if c == 0:
                    wait_emptied(pe, "v")
                if c == NCHUNK - 1:
                    pe.wait_ge(cv_in, 16)
                pe.wait_ge(pt_dve, c + 1)
                if has_before(c):
                    pe.wait_ge(pt_act, c - 1)
                if c:
                    pe.wait_ge(o_taken, c)
                for b in range(KV):
                    def probs(part, rows):
                        return pt[rows, c % 2, part, :].rearrange("p (m b q) -> p m b q", m=GROUP, b=KV)[:, :, b, :]
                    out = ps[b * HD:(b + 1) * HD, 6, 0:GROUP * CHUNK]
                    heads = slice(b * HD, (b + 1) * HD)
                    if has_before(c):
                        pe.matmul(out, V[rows_a, slot_a, heads], probs(0, rows_a), start=True, stop=False)
                    last = pe.matmul(out, V[rows_b, slot_b, heads], probs(1, rows_b), start=not has_before(c),
                                     stop=True)
                last.then_inc(pv_done, 1)

            for s, fill in enumerate(slots):
                for n in fill:
                    project(n)
                if s < NCHUNK:
                    scores(s)
                if 1 <= s <= NCHUNK:
                    turn_p(s - 1)
                if 2 <= s < NCHUNK + 2:
                    attend(s - 2)
            pe.wait_ge(o_taken, NCHUNK)
            pe.transpose(ps[:, 6, 0:P], kT[:, SEQ - P:SEQ], ident[:, :])
            pe.transpose(ps[0:DEC, 6, P:2 * P], kT[:, SEQ + WINDOW:], ident[:, :]).then_inc(kout_turned, 1)

            def decays(t):
                r = rows_of(t)
                pe.wait_ge(logf_ready, t + 1)
                if t >= 2:
                    pe.wait_ge(h2T_act, t - 1)
                    pe.wait_ge(h2T_dve, t - 1)
                if t:
                    pe.wait_ge(state_ready, 2 * t)
                    pe.wait_ge(rec_ready, t)
                for h in range(BH):
                    cols = slice(h * BK, (h + 1) * BK)
                    pe.matmul(ps[:, 2 + h // 2, (h % 2) * 2 * P:(h % 2 + 1) * 2 * P], logf[0:r, t, cols],
                              decay_m[0:r, :, :], start=True, stop=True)
                    pe.transpose(ps[:, 4, h * P:h * P + r], kf[0:r, t, cols], ident[0:r, 0:r])
                pe.matmul(ps[0:r, 5, :], tail_m[0:r, 0:r], logf[0:r, t, :], start=True, stop=True).then_inc(cum_ready, 1)

            def inner(t):
                r = rows_of(t)
                pe.wait_ge(hops_ready, 4 * t + 4)
                if t:
                    pe.wait_ge(rec_taken, t)
                if t >= 2:
                    pe.wait_ge(logits_taken, t - 1)
                for h in range(BH):
                    pe.matmul(ps[0:r, 6, h * P:h * P + r], kin[:, h, 0:r], qin[:, h, 0:r], start=True, stop=True)
                for c in range(r // CHUNK):
                    rows = slice(c * CHUNK, (c + 1) * CHUNK)
                    for h in range(BH):
                        cols = slice(h * BK, (h + 1) * BK)
                        last = pe.matmul(ps[:, 4 if c else 7, cols], kdec[rows, h, :], vf[rows, t, cols],
                                         start=True, stop=True)
                last.then_inc(inner_ready, 1)

            def sums(t):
                r = rows_of(t)
                pe.wait_ge(at_ready, t + 1)
                if t == NT - 1:
                    pe.wait_ge(s_in, 16)
                elif r > CHUNK:
                    pe.wait_ge(state_ready, 2 * t + 1)
                for h in range(BH):
                    cols = slice(h * BK, (h + 1) * BK)
                    terms = []
                    for c in range(r // CHUNK):
                        before = s_sample if t == NT - 1 else St[(2 * t + c) % 3]
                        if 2 * t + c:
                            terms.append((c, before))
                    pe.matmul(ps[0:r, 5, cols], aT[0:r, h, 0:r], vf[0:r, t, cols], start=True, stop=True)
                    for c, before in terms:
                        rows = slice(c * CHUNK, (c + 1) * CHUNK)
                        last = pe.matmul(ps[rows, 5, cols], qex[:, h, rows], before[:, cols], start=False,
                                         stop=True, skip_group_check=True)
                last.then_inc(rec_sum, 1)

            def turn_rec(t):
                r = rows_of(t)
                pe.wait_ge(rec_ready, t + 1)
                for h in range(BH):
                    last = pe.transpose(ps[:, 6, h * P:h * P + r], rec[0:r, h * BK:(h + 1) * BK], ident[0:r, 0:r])
                last.then_inc(rec_turned, 1)

            def out_half(t, half):
                r = rows_of(t)
                k = len(W_GROUPS) + half
                if t == 0:
                    pe.wait_ge(w_in[k], 48)
                    wait_emptied(pe, "g")
                    wait_emptied(pe, "b")
                else:
                    pe.wait_ge(x2_ready, 2 * (t - 1) + half + 1)
                pe.wait_ge(rec_taken, t + 1)
                for c in range(KC):
                    last = pe.matmul(ps[0:r, half, :], mixT[:, c, tok(t)], w_slot(k)[:, c, :], start=c == 0,
                                     stop=c == KC - 1)
                last.then_inc(out_ready, 1)

            def route(t):
                r = rows_of(t)
                pe.wait_ge(h2_ready, t + 1)
                if t + 1 < NT:
                    pe.wait_ge(state_ready, 2 * (t + 1) + 1)
                for c in range(KC):
                    last = pe.transpose(ps[:, 2 + c // 4, (c % 4) * P:(c % 4) * P + r],
                                        h2[0:r, t % 2, c * P:(c + 1) * P], ident[0:r, 0:r])
                last.then_inc(h2_turned, 1)
                pe.wait_ge(h2T_act, t + 1)
                pe.wait_ge(h2T_dve, t + 1)
                for c in range(KC):
                    last = pe.matmul(ps[0:r, 7, 0:NG + NE], h2T[:, t % 2, c * P:c * P + r], w_route[:, c, :],
                                     start=c == 0, stop=c == KC - 1)
                last.then_inc(logits_ready, 1)

            pe.wait_ge(kout_ready, 1)
            for t in range(NT):
                decays(t)
                if t:
                    out_half(t - 1, 0)
                inner(t)
                if t:
                    out_half(t - 1, 1)
                sums(t)
                turn_rec(t)
                if t:
                    route(t - 1)
            out_half(NT - 1, 0)
            out_half(NT - 1, 1)
            route(NT - 1)

            pe.wait_ge(picks_ready, 1)
            pe.wait_ge(x2_ready, 2 * NT)
            pe.matmul(ps[:, 0, 0:NT * NE], ones[:, :], before[:, 0:NT, :].rearrange("p t e -> p (t e)"),
                      start=True, stop=False)
            pe.matmul(ps[:, 0, 0:NT * NE], earlier[:, :], picks[:, 2, :, :].rearrange("p t e -> p (t e)"),
                      start=False, stop=True)
            pe.matmul(ps[:, 1, 0:NE], ones[:, :], before[:, NT, :], start=True, stop=True).then_inc(rank_ready, 1)
            pe.wait_ge(hot_ready, 1)
            for i in range(2):
                for t in range(NT):
                    last = pe.matmul(ps[:, 4, 0:COLS], slot_hot[:, i, t, :], block_hot[:, i, t, :],
                                     start=i + t == 0, stop=i == 1 and t == NT - 1)
            last.then_inc(slots_ready, 1)

            def turn_half(slot, half, signal):
                for c in range(4 * half, 4 * half + 4):
                    last = pe.transpose(ps[:, 1 + half, (c % 4) * P:(c % 4 + 1) * P], xg[:, slot, c:D:KC], ident[:, :])
                last.then_inc(signal, 1)

            pe.wait_ge(steer_ready, 1)
            turns = pe.value_load(steer[0:1, 0:1], min_val=NE // UNROLL, max_val=BLOCKS // UNROLL)
            pe.wait_ge(gathered[0], 16)
            turn_half(0, 0, x_turned_a)
            turn_half(0, 1, x_turned_b)
            with pe.Fori(0, turns) as i:
                for slot in range(UNROLL):
                    s = UNROLL * i + slot
                    following = (slot + 1) % UNROLL
                    pe.wait_ge(expert_in[slot], 48 * (i + 1))
                    pe.wait_ge(xT_act, s + 1)
                    pe.wait_ge(xT_dve, s + 1)
                    for c in range(KC):
                        last = pe.matmul(bank(0), xT[:, c, :], we_gu[slot][:, :, c, :], start=c == 0, stop=c == KC - 1)
                    last.then_inc(gu_ready, 1)
                    pe.wait_ge(gathered[following], 16 * (i + (slot + 1) // UNROLL + 1))
                    turn_half(following, 0, x_turned_a)
                    pe.wait_ge(hh_ready, s + 1)
                    for f in range(2):
                        last = pe.transpose(ps[:, 3, f * P:(f + 1) * P], hh[:, f:FE:2], ident[:, :])
                    last.then_inc(hh_turned, 1)
                    turn_half(following, 1, x_turned_b)
                    pe.wait_ge(hhT_ready, s + 1)
                    pe.wait_ge(y_act, s + 1)
                    pe.wait_ge(y_dve, s + 1)
                    for half in range(2):
                        for f in range(2):
                            last = pe.matmul(bank(4 + 2 * (slot % 2) + half), hhT[:, f, :],
                                             we_d[slot][:, f, 512 * half:512 * half + 512], start=f == 0, stop=f == 1)
                    last.then_inc(y_ready, 1)
    return nc


def kernel(**inputs):
    import numpy as _np
    import concourse.bacc as _bacc
    from concourse import mybir as _mybir
    from concourse.bass_utils import run_bass_kernel_spmd as _run

    nc = _bacc.Bacc("TRN2", target_bir_lowering=False, num_devices=1)
    layout = {
        "x_p": ("x_prompt", (SEQ, D)), "x_s": ("x_sample", (DEC, D)),
        "cache_k": ("cache_k", (WINDOW, KVW)), "cache_v": ("cache_v", (WINDOW, KVW)),
        "state": ("state_hgrn", (BH, BK, BK)), "g1": ("norm1_g", (D,)), "w_in": ("w_in", (D, G0 + BW)),
        "sink": ("attn_sink", (HEADS,)), "lower": ("lower_bounds", (2, BW)), "ng": ("hgrn_norm_g", (BW,)),
        "w_o": ("w_o", (D, D)), "g2": ("norm2_g", (D,)), "w_rg": ("w_router_group", (D, NG)),
        "b_rg": ("b_router_group", (NG,)), "w_re": ("w_router_expert", (NG, D, EPG)),
        "b_re": ("b_router_expert", (NG, EPG)), "w_gate": ("w_gate", (NE, D, FE)), "w_up": ("w_up", (NE, D, FE)),
        "w_down": ("w_down", (NE, FE, D)), "gf": ("final_norm_g", (D,)),
    }
    results = {
        "y_p": ((SEQ, D), (1, SEQ, D)), "y_s": ((DEC, D), (1, DEC, D)),
        "k_win_p": ((WINDOW, KVW), (1, 1, WINDOW, KV, HD)), "v_win_p": ((WINDOW, KVW), (1, 1, WINDOW, KV, HD)),
        "state_p": ((BH, BK, BK), (1, 1, BH, BK, BK)),
        "k_win_s": ((WINDOW, KVW), (1, 1, WINDOW, KV, HD)), "v_win_s": ((WINDOW, KVW), (1, 1, WINDOW, KV, HD)),
        "state_s": ((BH, BK, BK), (1, 1, BH, BK, BK)),
    }
    arrays, io = {}, {}
    for name, (key, shape) in layout.items():
        arrays[f"in_{name}"] = _np.ascontiguousarray(inputs[key]).reshape(shape)
        io[name] = nc.dram_tensor(f"in_{name}", shape, _mybir.dt.float32, kind="ExternalInput").ap()
    for name, (shape, _) in results.items():
        io[name] = nc.dram_tensor(f"out_{name}", shape, _mybir.dt.float32, kind="ExternalOutput").ap()
    program(nc, io)
    r = _run(nc, [arrays], core_ids=[0])
    return tuple(r.results[0][f"out_{name}"].reshape(shape) for name, (_, shape) in results.items())
```

```python
from contextlib import ExitStack

import numpy as np

import concourse.bass as bass
from concourse import mybir

ALU = mybir.AluOpType
ACT = mybir.ActivationFunctionType
AX = mybir.AxisListType
F32 = mybir.dt.float32
F32R = mybir.dt.float32r
I32 = mybir.dt.int32

P = 128
D = 1024
KC = D // P
SEQ, DEC = 512, 64
TOK = SEQ + DEC
NT = (TOK + P - 1) // P
PROMPT_TILES = SEQ // P
CHUNK = 64
NCHUNK = TOK // CHUNK
WINDOW = 128
HEADS, KV, HD = 8, 2, 64
GROUP = HEADS // KV
KVW = KV * HD
BH, BK = 4, 128
BW = BH * BK
EPS = 1e-6
NG, EPG = 4, 4
NE = NG * EPG
FE = 256
PAIRS = 2 * TOK
MAX_OVER = (PAIRS - NE) // P
MAX_OVER = min(MAX_OVER, PAIRS // (P + 1))
UNROLL = 4
BLOCKS = NE + MAX_OVER
AHEAD = UNROLL
COLS = (BLOCKS + AHEAD + 1) // 2 * 2
NOWHERE = 4096
TERMS = (TOK - 1) // P
Q0, K0, V0 = 0, 512, 640
QB0, F0, I0, G0 = 768, 1280, 1792, 2304
W_GROUPS = [(F0, BW), (K0, 2 * KVW), (Q0, BW), (I0, BW), (QB0, BW), (G0, BW)]
RING = 2
HALF = TOK // 2
EARLY = NCHUNK + 2


def rows_of(t):
    return min(P, TOK - t * P)


def window(c):
    odd = c % 2
    sample = c == NCHUNK - 1
    lo = CHUNK * odd if sample or c >= 2 else P
    hi = P + CHUNK + CHUNK * odd
    start = SEQ if sample else (c - 2) * CHUNK + lo - CHUNK * odd
    return lo, hi, CHUNK * odd, start


def has_before(c):
    return c >= 2


def v_slots(c):
    return (4, 5) if c == NCHUNK - 1 else (c // 2 - 1, c // 2)


def program(nc, io):
    ctx = ExitStack()
    with ctx:
        def sem(name):
            return ctx.enter_context(nc.semaphore(name))

        def sems(name, n):
            return [sem(f"{name}{i}") for i in range(n)]

        cursor = [(nc.sbuf_base + 63) // 64 * 64]

        def place(name, shape, dt=F32):
            n = int(np.prod(shape[1:])) * 4
            t = nc.alloc_sbuf_tensor_at(name, shape, dt, offset=cursor[0])
            cursor[0] += (n + 31) // 32 * 32
            return t

        ident = place("ident", [P, P])
        ones = place("ones", [P, P])
        earlier = place("earlier", [P, P])
        decay_m = place("decay_m", [P, 2, P])
        tail_m = place("tail_m", [P, P])
        causal = place("causal", [P, P])
        neghalf = place("neghalf", [P, 8])
        iota4 = place("iota4", [P, 4])
        iota16 = place("iota16", [P, NE])
        iota8 = place("iota8", [P, MAX_OVER])
        iota_p = place("iota_p", [P, P])
        limits = place("limits", [P, TERMS])
        upto = place("upto", [P, NE, NE])
        pair_val = place("pair_val", [P, 2, NT])
        g2_bc = place("g2_bc", [P, D])
        ng_bc = place("ng_bc", [P, BW])
        w_route = place("w_route", [P, KC, NG + NE])
        b_route = place("b_route", [P, NG + NE])
        sink_bc = place("sink_bc", [P, GROUP])
        stats = place("stats", [P, 6, 8])
        ms = place("ms", [P, 3 * NT + BH * NT])
        ro = place("ro", [P, BH])
        osq = place("osq", [P, BH])
        small = place("small", [P, 8, 2, GROUP])
        logits = place("logits", [P, NT, NG])
        elogits = place("elogits", [P, NT, NE])
        gates = place("gates", [P, 2, NT])
        rt = place("rt", [P, 12, NE])
        steer = place("steer", [P, 2 + MAX_OVER], I32)
        table = place("table", [P, COLS], I32)
        table_tok = place("table_tok", [P, COLS], I32)
        now_tok = place("now_tok", [P, UNROLL, 1], I32)
        now_pair = place("now_pair", [P, UNROLL, 1], I32)
        dec = place("dec", [P, BH, 2])
        kout = place("kout", [P, 2, KVW])

        x_at = cursor[0]
        w_hi = [place(f"w_hi{i}", [P, KC, 512], F32R) for i in range(RING)]
        raw_at = cursor[0]
        ring = place("ring", [P, RING, KC, 512])
        mix_at = cursor[0]
        mixT = place("mixT", [P, KC, TOK])
        end_small = cursor[0]

        after_weights = cursor[0]
        hT_at = cursor[0]
        hT_hi = place("hT_hi", [P, KC, TOK], F32R)
        hT_lo_a = place("hT_lo_a", [P, KC // 2, TOK], F32R)
        kf = place("kf", [P, NT, BW])
        logf = place("logf", [P, NT, BW])
        x_first_at = cursor[0]
        vf = place("vf", [P, NT, BW])
        qf = place("qf", [P, BH, TOK])
        gg_at = cursor[0]
        gg = place("gg", [P, NT, BW])
        kT = place("kT", [P, SEQ + WINDOW + DEC])
        V = place("V", [P, 6, KVW])
        bias = place("bias", [P, GROUP, WINDOW + CHUNK])
        qbd_at = cursor[0]
        qbd = place("qbd", [P, 2, GROUP, P])
        s_buf = place("s_buf", [P, 2, GROUP, 2 * P])
        pt_at = cursor[0]
        pt = place("pt", [P, 2, 2, GROUP * P])
        wo_hi_top = place("wo_hi_top", [P, 2, 512], F32R)
        assert cursor[0] <= nc.sbuf_usable_end

        def at(name, shape, dt, offset):
            return nc.alloc_sbuf_tensor_at(name, shape, dt, offset=offset)

        x = at("x", [P, NT, D], F32, x_at)
        after_small = x_at + NT * D * 4
        assert after_small <= raw_at
        w_lo = [at(f"w_lo{i}", [P, KC, 512], F32R, raw_at + i * KC * 512 * 4) for i in range(RING)]
        hT_lo_b = at("hT_lo_b", [P, KC // 2, TOK], F32R, mix_at + KC // 2 * TOK * 4)
        hT_f = at("hT_f", [P, KC, TOK], F32, hT_at)
        x_first = at("x_first", [P, NT, D], F32, x_first_at)
        qa = at("qa", [P, GROUP, TOK], F32, gg_at)
        wo_hi = [(wo_hi_top, 2),
                 (at("wo_hi_q", [P, 2, 512], F32R, qbd_at), 2),
                 (at("wo_hi_p", [P, 2, 512], F32R, pt_at + 2 * GROUP * P * 4), 2),
                 (at("wo_hi_h", [P, 4, 512], F32R, hT_at + KC * TOK * 4), 4),
                 (at("wo_hi_w", [P, 6, 512], F32R, after_small), 6)]
        wo_chunks = [part[:, j, :] for part, many in wo_hi for j in range(many)]
        assert len(wo_chunks) == 2 * KC and after_small + 6 * 512 * 4 <= raw_at
        mix_hi = at("mix_hi", [P, KC, P], F32R, mix_at + KC // 2 * TOK * 4)
        mix_lo = at("mix_lo", [P, KC, P], F32R, mix_at + KC // 2 * TOK * 4 + KC * P * 4)
        assert 2 * P <= TOK // 2
        hn = s_buf[:, :, :, :].rearrange("p a m k -> p a (m k)")
        h2 = hn
        h2T = pt[:, 0, :, :].rearrange("p b k -> p (b k)")
        gf_bc = g2_bc
        g1_bc = pt[:, 0, :, :].rearrange("p b k -> p (b k)")
        mix_flat = mixT[:, :, :].rearrange("p k t -> p (k t)")
        lb_bc = mix_flat[:, 0:2 * BW]
        lb = lb_bc[:, 0:BW]
        oml = lb_bc[:, BW:2 * BW]
        kf_flat = kf[:, :, :].rearrange("p t k -> p (t k)")
        lb_t = kf_flat[:, 2 * BW:4 * BW]
        junk = kf_flat[:, 0:D]
        hT_flat = hT_f[:, :, :].rearrange("p k t -> p (k t)")
        s_flat = s_buf[:, :, :, :].rearrange("p a m k -> p (a m k)")
        pt_flat = pt[:, 0, :, :].rearrange("p b k -> p (b k)")

        def hgrn_buffers(t):
            places = [s_flat[:, i * BW:(i + 1) * BW] for i in range(3)] + [pt_flat[:, 0:BW], s_flat[:, 3 * BW:4 * BW],
                                                                          pt_flat[:, BW:2 * BW]]
            if t:
                places = [hT_flat[:, i * BW:(i + 1) * BW] for i in range(6)]
            return [v.rearrange("p (h t) -> p h t", h=BH) for v in places[0:5]] + [places[5]]

        St = [hT_flat[:, 6 * BW:7 * BW], kT[:, 0:BW], hT_flat[:, 8 * BW:9 * BW]]
        s_sample = bias[:, :, :].rearrange("p m k -> p (m k)")[:, 0:BW]

        cursor[0] = after_small
        xg = place("xg", [P, UNROLL, D])
        xT_hi = place("xT_hi", [P, KC, P], F32R)
        xT_lo = place("xT_lo", [P, KC, P], F32R)
        sg = place("sg", [P, FE])
        hh = place("hh", [P, FE])
        hhT = place("hhT", [P, 2, 2, P])
        gu_hi = [place("gu_hi0", [P, 2, KC, FE], F32R)]
        routing_at = cursor[0]
        y = place("y", [P, 2, D])
        y_end = cursor[0]
        cursor[0] = routing_at
        picks = place("picks", [P, 3, NT, NE])
        before = place("before", [P, NT + 1, NE])
        rank_v = place("rank_v", [P, NT, NE])
        picked_v = place("picked_v", [P, 2, NT, NE])
        rb = place("rb", [P, NT, 5])
        compared = place("compared", [P, NE, NE])
        per_pair = place("per_pair", [P, 4, 2, NT])
        per_expert = place("per_expert", [P, 3, NE])
        over_hot = place("over_hot", [P, MAX_OVER, NE])
        table_f = place("table_f", [P, COLS])
        slot_hot = place("slot_hot", [P, 2, NT, P], F32R)
        block_hot = place("block_hot", [P, 2, NT, COLS], F32R)
        assert PAIRS < 2 ** 12
        assert cursor[0] <= end_small
        cursor[0] = after_weights - 2048
        assert cursor[0] >= y_end
        experts_at = cursor[0]
        gu_lo = [at(f"gu_lo{i}", [P, 2, KC, FE], F32R, experts_at + i * 2 * KC * FE * 4) for i in range(UNROLL)]
        we_gu = [place(f"we_gu{i}", [P, 2, KC, FE]) for i in range(UNROLL)]
        we_d = [place(f"we_d{i}", [P, 2, D]) for i in range(UNROLL)]
        gu_hi.append(place("gu_hi1", [P, 2, KC, FE], F32R))
        assert cursor[0] <= nc.sbuf_usable_end
        cursor[0] = after_weights
        pair = place("pair", [P, NT, 2 * D])
        assert cursor[0] <= nc.sbuf_usable_end

        ps = ctx.enter_context(nc.psum_tensor("ps", [P, 8, 512], F32))

        h2_dram = nc.dram_tensor("h2_rows", (TOK, D), F32, kind="Internal").ap()
        y_dram = nc.dram_tensor("y_pairs", (PAIRS, D), F32, kind="Internal").ap()

        x_in, x_again = sems("x_in", NT), sems("x_again", NT)
        w_first = sems("w_first", 2)
        mix_hi_done = sem("mix_hi_done")
        w_hi_done, w_lo_done = sem("w_hi_done"), sem("w_lo_done")
        g1_in, lb_in, ng_in, sink_in, route_in = (sem(n) for n in ("g1_in", "lb_in", "ng_in", "sink_in", "route_in"))
        g2_in, ck_in, cv_in, s_in = (sem(n) for n in ("g2_in", "ck_in", "cv_in", "s_in"))
        w_in = sems("w_in", len(W_GROUPS) + 2)
        consts, bias_ready = sem("consts"), sem("bias_ready")
        dve_chain, pool_chain, dve_consts = sem("dve_chain"), sem("pool_chain"), sem("dve_consts")
        ssq_ready, rstd_ready, hn_ready, turned, hT_act, hT_dve = (
            sem(n) for n in ("ssq_ready", "rstd_ready", "hn_ready", "turned", "hT_act", "hT_dve"))
        proj_ready, proj_act, proj_dve = (sem(n) for n in ("proj_ready", "proj_act", "proj_dve"))
        f_ready, logf_ready = sem("f_ready"), sem("logf_ready")
        lb_exp, lb_diff = sem("lb_exp"), sem("lb_diff")
        cache_turned, cache_taken, qf_ready, gg_ready = (
            sem(n) for n in ("cache_turned", "cache_taken", "qf_ready", "gg_ready"))
        qbd_ready, scores_ready, scores_taken, negm_ready, exp_done, p_ready = (
            sem(n) for n in ("qbd_ready", "scores_ready", "scores_taken", "negm_ready", "exp_done", "p_ready"))
        p_turned, pt_act, pt_dve, pv_done, o_taken = (
            sem(n) for n in ("p_turned", "pt_act", "pt_dve", "pv_done", "o_taken"))
        kout_turned, kout_ready = sem("kout_turned"), sem("kout_ready")
        cum_ready, cum_exp, hops_ready, inner_ready, at_ready, state_ready = (
            sem(n) for n in ("cum_ready", "cum_exp", "hops_ready", "inner_ready", "at_ready", "state_ready"))
        rec_sum, osq_ready, ro_ready, rec_ready, rec_turned, rec_taken = (
            sem(n) for n in ("rec_sum", "osq_ready", "ro_ready", "rec_ready", "rec_turned", "rec_taken"))
        out_ready, x2_ready, ssq2_ready, rstd2_ready, h2_ready = (
            sem(n) for n in ("out_ready", "x2_ready", "ssq2_ready", "rstd2_ready", "h2_ready"))
        h2_stored = sems("h2_stored", NT)
        h2_turned, h2T_act, h2T_dve, logits_ready, logits_taken = (
            sem(n) for n in ("h2_turned", "h2T_act", "h2T_dve", "logits_ready", "logits_taken"))
        route_diff, route_exp, picks_ready, rank_ready, hot_ready, slots_ready = (
            sem(n) for n in ("route_diff", "route_exp", "picks_ready", "rank_ready", "hot_ready", "slots_ready"))
        table_ready, steer_ready, xg_clear = sem("table_ready"), sem("steer_ready"), sem("xg_clear")
        expert_in = sems("expert_in", UNROLL)
        gathered, stored = sems("gathered", UNROLL), sems("stored", 2)
        col_copied, dma_cleared = sem("col_copied"), sem("dma_cleared")
        x_turned_a, x_turned_b, xT_act, xT_dve, gu_ready, silu_ready, hh_ready = (
            sem(n) for n in ("x_turned_a", "x_turned_b", "xT_act", "xT_dve", "gu_ready", "silu_ready", "hh_ready"))
        hh_turned, hhT_ready, y_ready, y_act, y_dve = (
            sem(n) for n in ("hh_turned", "hhT_ready", "y_ready", "y_act", "y_dve"))
        gu_hi_done, gu_lo_done, gates_ready = sem("gu_hi_done"), sem("gu_lo_done"), sem("gates_ready")
        pair_in = sems("pair_in", NT)
        sum_ready, ssq3_ready, rstd3_ready, final_ready = (
            sem(n) for n in ("sum_ready", "ssq3_ready", "rstd3_ready", "final_ready"))
        out_stored = sem("out_stored")

        groups = []
        for t in range(NT):
            groups.append(("f", t, "act"))
        groups += [("k", 0, "dve"), ("k", 1, "dve")]
        groups += [("v", t, "act") for t in range(NT)]
        groups += [("q", i, "act" if i % 2 else "dve") for i in range(2 * GROUP)]
        first_filler = len(groups)
        groups += [("i", t, "act") for t in range(NT)]
        groups += [("b", i, "dve") for i in range(2 * BH)]
        groups += [("g", t, "act") for t in range(NT)]
        ring_of = {"f": 0, "k": 1, "v": 1, "q": 2, "i": 3, "b": 4, "g": 5}
        emptied = {}
        count = {"act": 0, "dve": 0}
        for n, (_, _, who) in enumerate(groups):
            count[who] += 1
            emptied[n] = (who, count[who])
        last_of = {}
        for n, (kind, _, _) in enumerate(groups):
            last_of[ring_of[kind]] = n
        of_kind = {kind: [n for n, g in enumerate(groups) if g[0] == kind] for kind in ring_of}

        def wait_emptied(eng, kinds):
            for who, s in (("act", proj_act), ("dve", proj_dve)):
                last = [emptied[n][1] for k in kinds for n in of_kind[k] if emptied[n][0] == who]
                if last:
                    eng.wait_ge(s, max(last))

        slots = [[n] for n in of_kind["i"]] + [of_kind["b"][2 * m:2 * m + 2] for m in range(BH)] + \
                [[n] for n in of_kind["g"]]
        assert len(slots) >= NCHUNK + 2

        def w_slot(k):
            return ring[:, k % RING, :, :]

        def w_loaded(k):
            if k >= len(W_GROUPS):
                return 48
            return 16 * KV * KC if W_GROUPS[k][0] == Q0 else 16

        def w_columns(k):
            return W_GROUPS[k][1] if k < len(W_GROUPS) else 512

        def w_high(k, c):
            if k >= len(W_GROUPS):
                return wo_chunks[(k - len(W_GROUPS)) * KC + c]
            return w_hi[k % RING][:, c, 0:w_columns(k)]

        def h_lo(c):
            return (hT_lo_a, hT_lo_b)[c // (KC // 2)][:, c % (KC // 2), :]

        splits = {1: (4, 0, 4), 2: (4, 4, KC), 6: (5, 0, 4), 7: (5, 4, KC),
                  EARLY: (len(W_GROUPS), 0, 3), EARLY + 1: (len(W_GROUPS), 3, 6)}

        def bank(b, n=512):
            return ps[:, b, 0:n]

        def turned_bank(t):
            return 2 if t == NT - 2 else 0

        def tok(t):
            return slice(t * P, t * P + rows_of(t))

        block = ctx.enter_context(nc.Block())

        @block.sync
        def _(sp):
            def store_out(t):
                sp.wait_ge(final_ready, t + 1)
                dst = io["y_p"][tok(t), :] if t < PROMPT_TILES else io["y_s"]
                sp.dma_start(dst, pair[0:rows_of(t), t, 0:D]).then_inc(out_stored, 16)

            def w_group(k):
                if k < len(W_GROUPS) and W_GROUPS[k][0] == Q0:
                    src = io["w_in"][:, Q0:Q0 + BW].rearrange("(c p) (b m d) -> p b c m d", p=P, b=KV, m=GROUP)
                    dst = w_slot(k)[:, :, :].rearrange("p c (m b d) -> p b c m d", b=KV, m=GROUP)
                    for b in range(KV):
                        for c in range(KC):
                            sp.dma_start(dst[:, b, c, :, :], src[:, b, c, :, :]).then_inc(w_in[k], 16)
                elif k < len(W_GROUPS):
                    a, n = W_GROUPS[k]
                    sp.dma_start(w_slot(k)[:, :, 0:n],
                                 io["w_in"][:, a:a + n].rearrange("(c p) n -> p c n", p=P)).then_inc(w_in[k], 16)
                else:
                    cols = slice(512 * (k - len(W_GROUPS)), 512 * (k - len(W_GROUPS)) + 512)
                    att = io["w_o"][0:HEADS * HD, cols].rearrange("(b m d) n -> b d m n", b=KV, m=GROUP)
                    for b in range(KV):
                        sp.dma_start(w_slot(k)[b * HD:(b + 1) * HD, 0:GROUP, :], att[b]).then_inc(w_in[k], 16)
                    sp.dma_start(w_slot(k)[:, GROUP:KC, :],
                                 io["w_o"][HEADS * HD:, cols].rearrange("(h p) n -> p h n", p=P)).then_inc(w_in[k], 16)

            for t in range(NT):
                src = io["x_p"][tok(t), :] if t < PROMPT_TILES else io["x_s"]
                sp.dma_start(x_first[0:rows_of(t), t, :], src).then_inc(x_in[t], 16)
                if t == 0:
                    sp.dma_start(g1_bc, io["g1"].partition_broadcast(P)).then_inc(g1_in, 16)
                    for part in range(2):
                        rows = slice(part * KC // 2, (part + 1) * KC // 2)
                        sp.dma_start(w_slot(0)[:, rows, :], io["w_in"][:, F0:F0 + BW].rearrange(
                            "(c p) n -> p c n", p=P)[:, rows, :]).then_inc(w_first[part], 16)
                if t == 1:
                    sp.dma_start(lb_t[:, :], io["lower"].rearrange("a k -> (a k)").partition_broadcast(P)).then_inc(
                        lb_in, 16)
            w_group(1)
            for b in range(KV):
                sp.dma_start(sink_bc[b * CHUNK:(b + 1) * CHUNK, :],
                              io["sink"][b * GROUP:(b + 1) * GROUP].partition_broadcast(CHUNK)).then_inc(sink_in, 16)
            sp.dma_start(ng_bc[:, :], io["ng"].partition_broadcast(P)).then_inc(ng_in, 16)
            sp.dma_start(g2_bc[:, :], io["g2"].partition_broadcast(P)).then_inc(g2_in, 16)
            sp.dma_start(w_route[:, :, 0:NG], io["w_rg"].rearrange("(c p) g -> p c g", p=P)).then_inc(route_in, 16)
            for g in range(NG):
                sp.dma_start(w_route[:, :, NG + g * EPG:NG + (g + 1) * EPG],
                              io["w_re"][g].rearrange("(c p) e -> p c e", p=P)).then_inc(route_in, 16)
            sp.dma_start(b_route[:, 0:NG], io["b_rg"].partition_broadcast(P)).then_inc(route_in, 16)
            sp.dma_start(b_route[:, NG:NG + NE], io["b_re"].rearrange("g e -> (g e)").partition_broadcast(P)).then_inc(
                route_in, 16)
            sp.dma_start(kout[:, 0, :], io["cache_k"]).then_inc(ck_in, 16)
            sp.dma_start(V[:, 4, :], io["cache_v"]).then_inc(cv_in, 16)
            sp.dma_start(io["k_win_s"][0:CHUNK, :], io["cache_k"][CHUNK:WINDOW, :]).then_inc(out_stored, 16)
            sp.dma_start(io["v_win_s"][0:CHUNK, :], io["cache_v"][CHUNK:WINDOW, :]).then_inc(out_stored, 16)
            for k in range(RING, len(W_GROUPS) + 2):
                sp.wait_ge(proj_ready, last_of[k - RING] + 1)
                w_group(k)
                if k == 3:
                    wait_emptied(sp, "v")
                    sp.dma_start(io["v_win_p"], V[:, PROMPT_TILES - 1, :]).then_inc(out_stored, 16)
                    sp.dma_start(io["v_win_s"][CHUNK:WINDOW, :], V[0:DEC, 5, :]).then_inc(out_stored, 16)
            for t in range(NT):
                src = io["x_p"][tok(t), :] if t < PROMPT_TILES else io["x_s"]
                sp.dma_start(x[0:rows_of(t), t, :], src).then_inc(x_again[t], 16)
            sp.wait_ge(kout_ready, 1)
            sp.dma_start(io["k_win_p"], kout[:, 0, :]).then_inc(out_stored, 16)
            sp.dma_start(io["k_win_s"][CHUNK:WINDOW, :], kout[0:DEC, 1, :]).then_inc(out_stored, 16)
            sp.dma_start(s_sample[:, :].rearrange("k (h v) -> k h v", h=BH),
                         io["state"].rearrange("h k v -> k h v")).then_inc(s_in, 16)
            def store_h2(t):
                sp.wait_ge(h2_ready, t + 1)
                sp.dma_start(h2_dram[tok(t), :], h2[0:rows_of(t), t % 2, :]).then_inc(h2_stored[t], 16)

            def expert_parts(slot, e):
                gate, up = (we_gu[slot][:, i, :, :] for i in range(2))
                for dst, src in ((gate, io["w_gate"]), (up, io["w_up"]), (we_d[slot][:, :, :], io["w_down"])):
                    v = src[bass.ds(e, 1), :, :] if not isinstance(e, int) else src[e:e + 1, :, :]
                    yield dst, v.rearrange("e (p c) n -> p (e c) n", p=P)

            def expert(slot, e, first=0, last=3):
                for dst, src in list(expert_parts(slot, e))[first:last]:
                    sp.dma_start(dst, src).then_inc(expert_in[slot], 16)

            for t in range(PROMPT_TILES - 1):
                store_h2(t)
            sp.wait_ge(state_ready, 2 * PROMPT_TILES)
            sp.dma_start(io["state_p"].rearrange("h k v -> k h v"),
                         St[2 * PROMPT_TILES % 3].rearrange("k (h v) -> k h v", h=BH)).then_inc(out_stored, 16)
            store_h2(PROMPT_TILES - 1)
            sp.wait_ge(state_ready, 2 * PROMPT_TILES + 1)
            sp.dma_start(io["state_s"].rearrange("h k v -> k h v"),
                         St[0].rearrange("k (h v) -> k h v", h=BH)).then_inc(out_stored, 16)
            sp.wait_ge(out_stored, 16 * 8)
            sp.wait_ge(rec_taken, NT)
            expert(2, 2, 0, 2)
            expert(3, 3, 0, 2)
            expert(0, 0, 2, 3)
            expert(1, 1, 2, 3)
            store_h2(NT - 1)
            sp.wait_ge(h2T_act, NT)
            sp.wait_ge(h2T_dve, NT)
            for t in range(NT):
                sp.wait_ge(h2_stored[t], 16)
            expert(0, 0, 0, 2)
            expert(1, 1, 0, 2)
            sp.wait_ge(gathered[0], 16)
            expert(2, 2, 2, 3)
            expert(3, 3, 2, 3)
            with sp.Fori(1, NE // UNROLL) as i:
                for slot in range(UNROLL):
                    sp.wait_ge(gu_ready, UNROLL * (i - 1) + slot + 1)
                    expert(slot, UNROLL * i + slot, 0, 2)
                    for used in ((), (0,), (1,), (2, 3))[slot]:
                        sp.wait_ge(y_ready, UNROLL * (i - 1) + used + 1)
                        expert(used, UNROLL * i + used, 2, 3)
            sp.wait_ge(steer_ready, 1)
            turns = sp.value_load(steer[0:1, 0:1], min_val=NE // UNROLL, max_val=BLOCKS // UNROLL)
            with sp.If(turns > NE // UNROLL):
                with sp.Fori(0, turns - NE // UNROLL) as i:
                    for slot in range(UNROLL):
                        sp.wait_ge(y_ready, NE - UNROLL + UNROLL * i + slot + 1)
                        e = sp.value_load(steer[0:1, bass.ds(UNROLL * i + slot + 1, 1)], min_val=0, max_val=NE - 1)
                        expert(slot, e)
            for par in range(2):
                sp.wait_ge(stored[par], 8 * UNROLL * turns + 16)
            pairs = y_dram.rearrange("(t a) d -> t (a d)", a=2)
            for t in range(NT):
                sp.dma_start(pair[0:rows_of(t), t, :], pairs[tok(t), :]).then_inc(pair_in[t], 16)
            for t in range(NT):
                store_out(t)
            sp.wait_ge(out_stored, 16 * (8 + NT))

        @block.gpsimd
        def _(pool):
            done = [0]

            def chain(ins):
                done[0] += 1
                ins.then_inc(pool_chain, 1)
                pool.wait_ge(pool_chain, done[0])

            used = [0]
            chain(pool.memset(neghalf[:, :], -0.5))
            chain(pool.memset(ident[:, :], 0.0))
            pool.affine_select(out=ident[:, :], in_=ident[:, :], compare_op=ALU.not_equal, fill=1.0, base=0,
                               pattern=[[-1, P]], channel_multiplier=1).then_inc(consts, 1)

            def rstd(which, t, n, scale, waited, signal, src=None, dst=None, rows=P):
                pool.wait_ge(waited, t + 1)
                src = stats[:, which, t:t + 1] if src is None else src
                dst = stats[:, which + 3, t:t + 1] if dst is None else dst
                at = used[0]
                used[0] += n
                chain(pool.tensor_scalar(ms[0:rows, at:at + n], src[0:rows], scale, EPS, ALU.mult, ALU.add))
                pool.tensor_tensor(dst[0:rows], ms[0:rows, at:at + n], neghalf[0:rows, 0:n], ALU.pow).then_inc(signal, 1)

            rstd(0, 0, 1, 1.0 / D, ssq_ready, rstd_ready)
            chain(pool.memset(causal[:, :], 1.0))
            chain(pool.affine_select(out=causal[:, :], in_=causal[:, :], compare_op=ALU.is_ge, fill=0.0,
                                     base=0, pattern=[[1, P]], channel_multiplier=-1))
            chain(pool.memset(causal[0:CHUNK, CHUNK:P], 0.0))
            chain(pool.memset(decay_m[:, 0, :], 0.0))
            for c in range(2):
                part = decay_m[c * CHUNK:(c + 1) * CHUNK, 0, c * CHUNK:(c + 1) * CHUNK]
                chain(pool.memset(part, 1.0))
                chain(pool.affine_select(out=part, in_=part, compare_op=ALU.is_ge, fill=0.0, base=CHUNK // 2,
                                         pattern=[[0, CHUNK]], channel_multiplier=-1))
            chain(pool.tensor_tensor(decay_m[:, 0, :], causal[:, :], decay_m[:, 0, :], ALU.subtract))
            chain(pool.tensor_copy(decay_m[:, 1, :], causal[:, :]))
            chain(pool.memset(tail_m[:, :], 1.0))
            chain(pool.affine_select(out=tail_m[:, :], in_=tail_m[:, :], compare_op=ALU.is_ge, fill=0.0, base=-1,
                                     pattern=[[-1, P]], channel_multiplier=1))
            chain(pool.memset(tail_m[CHUNK:P, 0:CHUNK], 0.0))
            chain(pool.memset(ones[:, :], 1.0))
            chain(pool.affine_select(out=earlier[:, :], in_=ones[:, :], compare_op=ALU.is_ge, fill=0.0, base=-1,
                                     pattern=[[1, P]], channel_multiplier=-1))
            chain(pool.memset(qbd[:, :, :, :], 0.0))
            for t in range(1, NT):
                rstd(0, t, 1, 1.0 / D, ssq_ready, rstd_ready, rows=rows_of(t))
            base = rt[:, :, :].rearrange("p a b -> p (a b)")[:, 0:WINDOW + CHUNK]
            for b in range(KV):
                chain(pool.iota(base[b * CHUNK:(b + 1) * CHUNK, :], pattern=[[-1, WINDOW + CHUNK]], base=WINDOW,
                                channel_multiplier=1, allow_small_or_imprecise_dtypes=True))
            chain(pool.tensor_scalar(bias[:, 0, :], base, 0.0, None, ALU.min))
            chain(pool.tensor_scalar(base, base, 0.0, None, ALU.max))
            chain(pool.tensor_tensor(base, base, bias[:, 0, :], ALU.subtract))
            for b in range(KV):
                for m in range(GROUP):
                    slope = 2.0 ** (-8.0 * (m + GROUP * b + 1) / HEADS)
                    rows = slice(b * CHUNK, (b + 1) * CHUNK)
                    chain(pool.tensor_scalar(bias[rows, m, :], base[rows, :], -slope, None, ALU.mult))
            pool.sem_inc(bias_ready, 1)
            for out, n, first, step in ((iota4, 4, 0, 1), (iota16, NE, 0, 1), (iota8, MAX_OVER, 0, 1),
                                        (iota_p, P, 0, 1), (limits, TERMS, P, P)):
                chain(pool.iota(out[:, :], pattern=[[step, n]], base=first, channel_multiplier=0,
                                allow_small_or_imprecise_dtypes=True))
            chain(pool.memset(upto[:, :, :], 1.0))
            chain(pool.affine_select(out=upto[:, :, :], in_=upto[:, :, :], compare_op=ALU.is_ge, fill=0.0, base=0,
                                     pattern=[[1, NE], [-1, NE]], channel_multiplier=0))
            chain(pool.iota(pair_val[:, :, :], pattern=[[1, 2], [2 * P, NT]], base=1, channel_multiplier=2,
                            allow_small_or_imprecise_dtypes=True))
            pool.memset(pair_val[rows_of(NT - 1):P, :, NT - 1:NT], 0.0).then_inc(consts, 1)

            wait_emptied(pool, "q")
            for c in range(NCHUNK):
                if c >= 2:
                    pool.wait_ge(scores_ready, c - 1)
                for b in range(KV):
                    rows = slice(b * HD, (b + 1) * HD)
                    pool.tensor_copy(qbd[rows, c % 2, :, b * CHUNK:(b + 1) * CHUNK],
                                     qa[rows, :, c * CHUNK:(c + 1) * CHUNK]).then_inc(qbd_ready, 1)
                    pool.wait_ge(qbd_ready, KV * c + b + 1)

            for t in range(NT):
                rstd(0, t, BH, 1.0 / BK, osq_ready, ro_ready, osq[:, :], ro[:, :], rows_of(t))
                if t:
                    rstd(1, t - 1, 1, 1.0 / D, ssq2_ready, rstd2_ready)
            rstd(1, NT - 1, 1, 1.0 / D, ssq2_ready, rstd2_ready, rows=rows_of(NT - 1))

            pool.wait_ge(out_ready, 2 * NT)
            pool.memset(xg[:, :, :], 0.0).then_inc(xg_clear, 1)
            pool.wait_ge(h2_ready, NT)
            for par in range(2):
                cols = slice(par * 512, par * 512 + 512)
                pool.dma_start(gf_bc[:, cols], io["gf"][cols].partition_broadcast(P)).then_inc(stored[par], 16)
            pool.wait_ge(xg_clear, 1)
            for t in range(NT):
                pool.wait_ge(h2_stored[t], 16)
            pool.wait_ge(table_ready, 1)

            def gather(s, slot, copies):
                if not isinstance(s, int):
                    pool.wait_ge(x_turned_b, s - AHEAD + 1)
                pool.tensor_copy(now_tok[:, slot, :], table_tok[:, bass.ds(s, 1)]).then_inc(col_copied, 1)
                pool.wait_ge(col_copied, copies)
                if not isinstance(s, int):
                    pool.sem_inc(dma_cleared, 1)
                pool.indirect_dma_start(
                    xg[:, slot, :], None, h2_dram, bass.IndirectOffsetOnAxis(ap=now_tok[:, slot, :], axis=0),
                    bounds_check=TOK - 1, oob_is_err=False).then_inc(gathered[slot], 16)

            for s in range(AHEAD):
                gather(s, s, s + 1)
            pool.wait_ge(steer_ready, 1)
            turns = pool.value_load(steer[0:1, 0:1], min_val=NE // UNROLL, max_val=BLOCKS // UNROLL)
            with pool.Fori(0, turns) as i:
                for slot in range(UNROLL):
                    s = UNROLL * i + slot
                    gather(s + AHEAD, (slot + AHEAD) % UNROLL, 2 * s + AHEAD + 1)
                    pool.tensor_copy(now_pair[:, slot, :], table[:, bass.ds(s, 1)]).then_inc(col_copied, 1)
                    pool.wait_ge(col_copied, 2 * s + AHEAD + 2)
                    pool.wait_ge(y_act, s + 3)
                    pool.wait_ge(y_dve, s + 3)
                    pool.sem_inc(dma_cleared, 1)
                    pool.indirect_dma_start(
                        y_dram, bass.IndirectOffsetOnAxis(ap=now_pair[:, slot, :], axis=0),
                        y[:, slot % 2, :], None, bounds_check=PAIRS - 1, oob_is_err=False).then_inc(
                            stored[slot % 2], 16)
            for slot in range(AHEAD):
                pool.wait_ge(gathered[slot], turns * 16 + 16)
            pool.sem_inc(dma_cleared, 1)

            for t in range(NT):
                rstd(2, t, 1, 1.0 / D, ssq3_ready, rstd3_ready, rows=rows_of(t))

        @block.scalar
        def _(act):
            def square_sum(t, which, signal):
                r = rows_of(t)
                if t:
                    act.wait_ge(signal, t)
                act.activation(junk[0:r, :], x_first[0:r, t, :], ACT.Square,
                               accum_out=stats[0:r, which, t:t + 1]).then_inc(signal, 1)

            def h_high(t):
                act.wait_ge(turned, t + 1)
                r = rows_of(t)
                for half in range(2):
                    act.activation(hT_hi[:, 4 * half:4 * half + 4, tok(t)],
                                   bank(2 + 2 * (t % 3) + half).rearrange("p (c t) -> p c t", c=4)[:, :, 0:r],
                                   ACT.Copy).then_inc(hT_act, 1)

            def high(k, first, last):
                if k:
                    act.wait_ge(w_in[k], w_loaded(k))
                else:
                    act.wait_ge(w_first[first * 2 // KC], 16)
                for c in range(first, last):
                    act.activation(w_high(k, c), w_slot(k)[:, c, 0:w_columns(k)], ACT.Copy).then_inc(w_hi_done, 1)

            def first_squares(t):
                act.wait_ge(x_in[t], 16)
                square_sum(t, 0, ssq_ready)

            def empty(n):
                kind, t, _ = groups[n]
                act.wait_ge(proj_ready, n + 1)
                b = n % 2
                if kind == "f":
                    ins = act.activation(logf[0:rows_of(t), t, :], ps[0:rows_of(t), b, :], ACT.Sigmoid)
                elif kind == "v":
                    slot = t if t < PROMPT_TILES else 5
                    ins = act.activation(V[0:rows_of(t), slot, :], ps[0:rows_of(t), b, 0:KVW], ACT.Copy)
                elif kind == "q":
                    ins = act.activation(qa[:, t // 2, t % 2 * HALF:(t % 2 + 1) * HALF], bank(b, HALF), ACT.Copy,
                                         scale=float(HD) ** -0.5)
                elif kind == "i":
                    ins = act.activation(vf[0:rows_of(t), t, :], ps[0:rows_of(t), b, :], ACT.Copy)
                else:
                    ins = act.activation(gg[0:rows_of(t), t, :], ps[0:rows_of(t), b, :], ACT.Silu)
                ins.then_inc(proj_act, 1)

            first_squares(0)
            h_high(0)
            high(0, 0, 4)
            high(0, 4, KC)
            first_squares(1)
            first_squares(2)
            first_squares(3)
            h_high(1)
            act.wait_ge(lb_diff, 1)
            act.activation(lb_t[:, :], lb_t[:, :], ACT.Exp).then_inc(lb_exp, 1)
            h_high(2)
            first_squares(4)
            for n in range(first_filler):
                if groups[n][2] == "act":
                    empty(n)
                kind, index, _ = groups[n]
                if kind == "f" and index < 2:
                    h_high(3 + index)
                if (kind, index) == ("f", 2):
                    high(1, 0, KC)
                if kind == "v" and index >= 2:
                    high(2, *((0, 4), (4, 6), (6, KC))[index - 2])
                if (kind, index) == ("q", 5):
                    high(3, 0, KC)
                if groups[n][0] == "k" and groups[n][1] == 1:
                    for t in range(NT):
                        act.wait_ge(f_ready, t + 1)
                        act.activation(logf[0:rows_of(t), t, :], logf[0:rows_of(t), t, :], ACT.Ln).then_inc(logf_ready, 1)

            def exps(c):
                lo, hi, _, _ = window(c)
                par = c % 2
                act.wait_ge(negm_ready, c + 1)
                act.activation(small[:, 3, par, :], small[:, 2, par, :], ACT.Exp)
                for m in range(GROUP):
                    last = act.activation(s_buf[:, par, m, lo:hi], s_buf[:, par, m, lo:hi], ACT.Exp,
                                          bias=small[:, 1, par, m:m + 1], accum_out=small[:, 4, par, m:m + 1])
                last.then_inc(exp_done, 1)

            def pt_before(c):
                act.wait_ge(p_turned, c + 1)
                act.wait_ge(pv_done, c - 1)
                act.activation(pt[:, c % 2, 0, :], bank(4), ACT.Copy).then_inc(pt_act, 1)

            def cum_exps(t):
                r = rows_of(t)
                qin, kin, qex, _, kdec, _ = hgrn_buffers(t)
                act.wait_ge(cum_ready, t + 1)
                if t:
                    act.wait_ge(rec_sum, t)
                cums = ps[:, 2:4, :].rearrange("p b (h w t) -> p (b h) w t", h=2, w=2)
                act.activation(qin[:, :, 0:r], cums[:, :, 0, 0:r], ACT.Exp).then_inc(cum_exp, 1)
                act.activation(kin[:, :, 0:r], cums[:, :, 0, 0:r], ACT.Exp, scale=-1.0).then_inc(cum_exp, 1)
                act.activation(qex[:, :, 0:r], cums[:, :, 1, 0:r], ACT.Exp).then_inc(cum_exp, 1)
                act.activation(kdec[0:r, :, :], ps[0:r, 5, :].rearrange("p (h k) -> p h k", h=BH),
                               ACT.Exp).then_inc(cum_exp, 1)

            for s, fill in enumerate(slots):
                if s == NCHUNK:
                    wait_emptied(act, "b")
                    act.activation(qf[:, :, :], qf[:, :, :], ACT.Silu).then_inc(qf_ready, 1)
                if s == EARLY:
                    cum_exps(0)
                for n in fill:
                    if groups[n][2] == "act":
                        empty(n)
                if has_before(s - 1) and s - 1 < NCHUNK:
                    pt_before(s - 1)
                if s < NCHUNK:
                    exps(s)
                if s in splits:
                    high(*splits[s])

            def second_norm(t):
                act.wait_ge(x2_ready, 2 * t + 2)
                r = rows_of(t)
                if t >= 2:
                    act.wait_ge(h2_stored[t - 2], 16)
                    act.wait_ge(h2_turned, t - 1)
                act.activation(h2[0:r, t % 2, :], x[0:r, t, :], ACT.Square,
                               accum_out=stats[0:r, 1, t:t + 1]).then_inc(ssq2_ready, 1)

            def h2T_half(t):
                act.wait_ge(h2_turned, t + 1)
                act.activation(h2T[:, 0:512], bank(turned_bank(t)), ACT.Copy).then_inc(h2T_act, 1)

            for t in range(NT):
                r = rows_of(t)
                if t == 0:
                    act.wait_ge(proj_ready, len(groups))
                    high(len(W_GROUPS), 6, KC)
                else:
                    cum_exps(t)
                if t >= 2:
                    h2T_half(t - 2)
                act.wait_ge(rec_sum, t + 1)
                for h in range(BH):
                    cols = slice(h * BK, (h + 1) * BK)
                    last = act.activation(logf[0:r, t, cols], ps[0:r, 5, cols], ACT.Square,
                                          accum_out=osq[0:r, h:h + 1])
                last.then_inc(osq_ready, 1)
                if t == 0:
                    high(len(W_GROUPS) + 1, 0, 4)
                if 0 < t < NT - 1:
                    second_norm(t - 1)
                act.wait_ge(rec_turned, t + 1)
                act.activation(mix_hi[:, BH:KC, 0:r], bank(6).rearrange("p (h t) -> p h t", h=BH)[:, :, 0:r],
                               ACT.Copy).then_inc(mix_hi_done, 1)
                act.activation(mix_hi[:, 0:BH, 0:r], mixT[:, 0:BH, tok(t)], ACT.Copy).then_inc(mix_hi_done, 1)
                if t == 0:
                    high(len(W_GROUPS) + 1, 4, KC)
            second_norm(NT - 2)
            h2T_half(NT - 2)
            second_norm(NT - 1)
            h2T_half(NT - 1)

            for k in range(2):
                act.wait_ge(route_diff, k + 1)
                act.activation(rb[:, :, 0:4] if k == 0 else rb[:, :, 4:5],
                               rb[:, :, 0:4] if k == 0 else rb[:, :, 4:5], ACT.Exp).then_inc(route_exp, 1)

            def x_high(s, half):
                act.wait_ge((x_turned_a, x_turned_b)[half], s + 1)
                act.activation(xT_hi[:, 4 * half:4 * half + 4, :], bank(1 + half).rearrange("p (c t) -> p c t", c=4),
                               ACT.Copy).then_inc(xT_act, 1)

            def gu_high(slot, first, last):
                for q in range(first, last):
                    act.activation(gu_hi[slot % 2][:, :, 2 * q:2 * q + 2, :], we_gu[slot][:, :, 2 * q:2 * q + 2, :],
                                   ACT.Copy).then_inc(gu_hi_done, 1)

            act.wait_ge(expert_in[0], 48)
            gu_high(0, 0, KC // 2)
            x_high(0, 0)
            x_high(0, 1)
            act.wait_ge(expert_in[1], 48)
            gu_high(1, 0, KC // 2)
            act.sem_inc(y_act, 2)
            act.wait_ge(gates_ready, 1)
            act.wait_ge(steer_ready, 1)
            turns = act.value_load(steer[0:1, 0:1], min_val=NE // UNROLL, max_val=BLOCKS // UNROLL)

            def split_ahead(slot, i, half):
                if slot in (1, 2):
                    if half == 0:
                        act.wait_ge(expert_in[slot + 1], 48 * (i + 1))
                    gu_high(slot + 1, 2 * half, 2 * half + 2)
                elif slot == UNROLL - 1:
                    with act.If(i < turns - 1):
                        if half == 0:
                            act.wait_ge(expert_in[0], 48 * (i + 2))
                        gu_high(0, 2 * half, 2 * half + 2)
                        if half == 1:
                            act.wait_ge(expert_in[1], 48 * (i + 2))
                            gu_high(1, 0, KC // 2)

            def take_y(i, slot):
                act.wait_ge(y_ready, UNROLL * i + slot + 1)
                act.wait_ge(stored[slot % 2], 16 * (2 * i + slot // 2 + 1))
                act.activation(y[:, slot % 2, 0:512], bank(4 + 2 * (slot % 2)), ACT.Copy).then_inc(y_act, 1)

            with act.Fori(0, turns) as i:
                for slot in range(UNROLL):
                    s = UNROLL * i + slot
                    split_ahead(slot, i, 0)
                    act.wait_ge(gu_ready, s + 1)
                    act.activation(sg[:, :], ps[:, 0, 0:FE], ACT.Silu).then_inc(silu_ready, 1)
                    x_high(s + 1, 0)
                    x_high(s + 1, 1)
                    split_ahead(slot, i, 1)
                    if slot:
                        take_y(i, slot - 1)
                take_y(i, UNROLL - 1)

            for t in range(NT):
                r = rows_of(t)
                act.wait_ge(sum_ready, 2 * t + 2)
                act.activation(pair[0:r, t, D:2 * D], x[0:r, t, :], ACT.Square,
                               accum_out=stats[0:r, 2, t:t + 1]).then_inc(ssq3_ready, 1)

        @block.vector
        def _(dve):
            done = [0]

            def chain(ins):
                done[0] += 1
                ins.then_inc(dve_chain, 1)
                dve.wait_ge(dve_chain, done[0])

            def h_tile(t):
                dve.wait_ge(rstd_ready, t + 1)
                if t >= 2:
                    dve.wait_ge(turned, t - 1)
                r = rows_of(t)
                dve.scalar_tensor_tensor(hn[0:r, t % 2, :], x_first[0:r, t, :], stats[0:r, 3, t:t + 1], g1_bc[0:r, :],
                                         ALU.mult, ALU.mult).then_inc(hn_ready, 1)

            def h_low(t):
                r = rows_of(t)
                for half in range(2):
                    dve.wait_ge(hT_act, 2 * t + half + 1)
                    last = dve.tensor_tensor(
                        (hT_lo_a, hT_lo_b)[half][:, :, tok(t)],
                        bank(2 + 2 * (t % 3) + half).rearrange("p (c t) -> p c t", c=4)[:, :, 0:r],
                        hT_hi[:, 4 * half:4 * half + 4, tok(t)].bitcast(F32), ALU.subtract)
                last.then_inc(hT_dve, 1)

            def low(k, first, last):
                n = w_columns(k)
                for c in range(first, last):
                    dve.wait_ge(w_hi_done, KC * k + c + 1)
                    dve.tensor_tensor(w_lo[k % RING][:, c, 0:n], w_slot(k)[:, c, 0:n],
                                      w_high(k, c).bitcast(F32), ALU.subtract).then_inc(w_lo_done, 1)

            dve.wait_ge(g1_in, 16)
            h_tile(0)
            h_low(0)
            low(0, 0, KC)
            h_tile(1)
            h_tile(2)
            dve.wait_ge(lb_in, 16)
            l0, l1 = lb_t[:, 0:BW], lb_t[:, BW:2 * BW]
            chain(dve.tensor_tensor(lb, l0, l1, ALU.max))
            chain(dve.tensor_tensor(l0, l0, lb, ALU.subtract))
            dve.tensor_tensor(l1, l1, lb, ALU.subtract).then_inc(lb_diff, 1)
            h_low(1)
            h_tile(3)
            h_low(2)
            def gate_f(t):
                r = rows_of(t)
                dve.wait_ge(proj_act, t + 1)
                chain(dve.tensor_tensor(logf[0:r, t, :], logf[0:r, t, :], oml[0:r, :], ALU.mult))
                chain(dve.tensor_tensor(logf[0:r, t, :], logf[0:r, t, :], lb[0:r, :], ALU.add))
                dve.tensor_scalar(kf[0:r, t, :], logf[0:r, t, :], -1.0, 1.0, ALU.mult, ALU.add).then_inc(f_ready, 1)

            h_tile(4)
            dve.wait_ge(lb_exp, 1)
            chain(dve.tensor_tensor(oml, l0, l1, ALU.add))
            chain(dve.reciprocal(oml, oml))
            chain(dve.tensor_tensor(lb, l0, oml, ALU.mult))
            chain(dve.tensor_scalar(oml, lb, -1.0, 1.0, ALU.mult, ALU.add))
            h_low(3)
            gate_f(0)
            h_low(4)
            gate_f(1)
            low(1, 0, KC)
            gate_f(2)
            gate_f(3)

            def empty(n):
                kind, i, _ = groups[n]
                dve.wait_ge(proj_ready, n + 1)
                b = n % 2
                if kind == "k":
                    if i == 0:
                        ins = dve.tensor_copy(kT[:, 0:HALF], bank(b, HALF))
                    else:
                        dve.tensor_copy(kT[:, HALF:SEQ], ps[:, b, 0:SEQ - HALF])
                        ins = dve.tensor_copy(kT[:, SEQ + WINDOW:], ps[:, b, SEQ - HALF:HALF])
                elif kind == "q":
                    ins = dve.tensor_scalar(qa[:, i // 2, i % 2 * HALF:(i % 2 + 1) * HALF], bank(b, HALF),
                                            float(HD) ** -0.5, None, ALU.mult)
                else:
                    ins = dve.tensor_copy(qf[:, i // 2, i % 2 * HALF:(i % 2 + 1) * HALF], bank(b, HALF))
                ins.then_inc(proj_dve, 1)

            dve.memset(s_buf[:, 1, :, 0:CHUNK], 0.0).then_inc(dve_consts, 1)
            dve.wait_ge(cache_turned, 1)
            dve.tensor_copy(kT[:, SEQ:SEQ + WINDOW], ps[:, 7, 0:P]).then_inc(cache_taken, 1)
            for n in range(first_filler):
                if groups[n][2] == "dve":
                    empty(n)
                if groups[n][:2] == ("k", 1):
                    gate_f(NT - 1)
                    low(2, 0, KC)
                if groups[n][:2] == ("q", 6):
                    low(3, 0, KC)

            def softmax_head(c):
                lo, hi, off, _ = window(c)
                par = c % 2
                dve.wait_ge(scores_ready, c + 1)
                if c == 0:
                    dve.wait_ge(bias_ready, 1)
                    dve.wait_ge(sink_in, 32)
                dve.tensor_tensor(s_buf[:, par, :, lo:hi],
                                  ps[:, 2:4, :].rearrange("p b (m k) -> p (b m) k", m=2)[:, :, lo:hi],
                                  bias[:, :, lo - off:hi - off], ALU.add).then_inc(scores_taken, 1)
                dve.wait_ge(scores_taken, c + 1)
                chain(dve.tensor_reduce(small[:, 0, par, :], s_buf[:, par, :, lo:hi], AX.X, ALU.max))
                chain(dve.tensor_tensor(small[:, 0, par, :], small[:, 0, par, :], sink_bc[:, :], ALU.max))
                chain(dve.tensor_scalar(small[:, 1, par, :], small[:, 0, par, :], -1.0, None, ALU.mult))
                dve.tensor_tensor(small[:, 2, par, :], sink_bc[:, :], small[:, 0, par, :],
                                  ALU.subtract).then_inc(negm_ready, 1)

            def softmax_tail(c):
                lo, hi, _, _ = window(c)
                par = c % 2
                dve.wait_ge(exp_done, c + 1)
                chain(dve.tensor_tensor(small[:, 5, par, :], small[:, 4, par, :], small[:, 3, par, :], ALU.add))
                chain(dve.reciprocal(small[:, 5, par, :], small[:, 5, par, :]))
                for m in range(GROUP):
                    last = dve.tensor_scalar(s_buf[:, par, m, lo:hi], s_buf[:, par, m, lo:hi],
                                             small[:, 5, par, m:m + 1], None, ALU.mult)
                last.then_inc(p_ready, 1)

            def pt_with(c):
                r = P if c % 2 else CHUNK
                dve.wait_ge(p_turned, c + 1)
                if c >= 2:
                    dve.wait_ge(pv_done, c - 1)
                dve.tensor_copy(pt[0:r, c % 2, 1, :], ps[0:r, 5, :]).then_inc(pt_dve, 1)

            def take_o(c):
                dve.wait_ge(pv_done, c + 1)
                dve.tensor_copy(mixT[:, 0:GROUP, c * CHUNK:(c + 1) * CHUNK],
                                ps[:, 6, 0:GROUP * CHUNK].rearrange("p (m q) -> p m q", m=GROUP)).then_inc(o_taken, 1)

            def gain(t):
                r = rows_of(t)
                dve.wait_ge(proj_act, emptied[of_kind["g"][t]][1])
                if t == 0:
                    dve.wait_ge(ng_in, 16)
                dve.tensor_tensor(gg[0:r, t, :], gg[0:r, t, :], ng_bc[0:r, :], ALU.mult).then_inc(gg_ready, 1)

            def operands(t):
                r = rows_of(t)
                qin, kin, qex, _, kdec, _ = hgrn_buffers(t)
                nch = r // CHUNK
                dve.wait_ge(cum_exp, 4 * t + 1)
                dve.wait_ge(qf_ready, 1)
                dve.tensor_tensor(qin[:, :, 0:r], qin[:, :, 0:r], qf[:, :, tok(t)], ALU.mult).then_inc(hops_ready, 1)
                dve.wait_ge(cum_exp, 4 * t + 2)
                dve.tensor_tensor(kin[:, :, 0:r], kin[:, :, 0:r],
                                  bank(4).rearrange("p (h t) -> p h t", h=BH)[:, :, 0:r],
                                  ALU.mult).then_inc(hops_ready, 1)
                dve.wait_ge(cum_exp, 4 * t + 3)
                chain(dve.tensor_copy(dec[:, :, 0:nch], qex[:, :, CHUNK - 1:r:CHUNK]))
                dve.tensor_tensor(qex[:, :, 0:r], qex[:, :, 0:r], qf[:, :, tok(t)], ALU.mult).then_inc(hops_ready, 1)
                dve.wait_ge(cum_exp, 4 * t + 4)
                dve.tensor_tensor(kdec[0:r, :, :], kdec[0:r, :, :],
                                  kf[0:r, t, :].rearrange("p (h k) -> p h k", h=BH), ALU.mult).then_inc(hops_ready, 1)

            def add_out(t, half):
                r = rows_of(t)
                dve.wait_ge(out_ready, 2 * t + half + 1)
                if half == 0:
                    dve.wait_ge(x_again[t], 16)
                cols = slice(512 * half, 512 * half + 512)
                dve.tensor_tensor(x[0:r, t, cols], x[0:r, t, cols], ps[0:r, half, :], ALU.add).then_inc(x2_ready, 1)

            def inner_and_states(t):
                r = rows_of(t)
                aT = hgrn_buffers(t)[3]
                dve.wait_ge(inner_ready, t + 1)
                dve.copy_predicated(aT[0:r, :, 0:r], causal[0:r, 0:r].bitcast(I32).unsqueeze(1).to_broadcast([r, BH, r]),
                                    ps[0:r, 6, :].rearrange("p (h t) -> p h t", h=BH)[:, :, 0:r]).then_inc(at_ready, 1)
                for c in range(r // CHUNK):
                    n = 2 * t + c
                    before = St[n % 3] if t < PROMPT_TILES else s_sample
                    after = St[(n + 1) % 3] if t < PROMPT_TILES else St[0]
                    ds = bank(7) if c == 0 else bank(4)
                    if c:
                        dve.wait_ge(state_ready, n)
                    if n == 1:
                        dve.wait_ge(proj_ready, len(groups))
                    if n == 0:
                        last = dve.tensor_copy(after[:, :], ds)
                    else:
                        if t == NT - 1:
                            dve.wait_ge(s_in, 16)
                        for h in range(BH):
                            cols = slice(h * BK, (h + 1) * BK)
                            last = dve.scalar_tensor_tensor(after[:, cols], before[:, cols], dec[:, h, c:c + 1],
                                                            ds[:, cols], ALU.mult, ALU.add)
                    last.then_inc(state_ready, 1)

            def normed(t):
                r = rows_of(t)
                rec = hgrn_buffers(t)[5]
                dve.wait_ge(ro_ready, t + 1)
                dve.wait_ge(gg_ready, t + 1)
                if t:
                    dve.wait_ge(rec_turned, t)
                for h in range(BH):
                    cols = slice(h * BK, (h + 1) * BK)
                    last = dve.scalar_tensor_tensor(rec[0:r, cols], ps[0:r, 5, cols], ro[0:r, h:h + 1],
                                                    gg[0:r, t, cols], ALU.mult, ALU.mult)
                last.then_inc(rec_ready, 1)

            def make_h2(t):
                r = rows_of(t)
                dve.wait_ge(rstd2_ready, t + 1)
                if t == 0:
                    dve.wait_ge(g2_in, 16)
                if t >= 2:
                    dve.wait_ge(h2_stored[t - 2], 16)
                    dve.wait_ge(h2_turned, t - 1)
                dve.scalar_tensor_tensor(h2[0:r, t % 2, :], x[0:r, t, :], stats[0:r, 4, t:t + 1], g2_bc[0:r, :],
                                         ALU.mult, ALU.mult).then_inc(h2_ready, 1)

            def h2T_half(t):
                dve.wait_ge(h2_turned, t + 1)
                dve.tensor_copy(h2T[:, 512:1024], bank(turned_bank(t) + 1)).then_inc(h2T_dve, 1)

            def take_logits(t):
                r = rows_of(t)
                dve.wait_ge(logits_ready, t + 1)
                if t == 0:
                    dve.wait_ge(route_in, 16 * (3 + NG))
                dve.tensor_tensor(logits[0:r, t, :], ps[0:r, 7, 0:NG], b_route[0:r, 0:NG], ALU.add)
                dve.tensor_tensor(elogits[0:r, t, :], ps[0:r, 7, NG:NG + NE], b_route[0:r, NG:NG + NE],
                                  ALU.add).then_inc(logits_taken, 1)

            for s, fill in enumerate(slots):
                if 1 <= s <= NCHUNK:
                    softmax_tail(s - 1)
                for n in fill:
                    if groups[n][2] == "dve":
                        empty(n)
                if s < NCHUNK:
                    softmax_head(s)
                if 1 <= s <= NCHUNK:
                    pt_with(s - 1)
                if 2 <= s < NCHUNK + 2:
                    take_o(s - 2)
                if s == EARLY:
                    chain(dve.memset(hgrn_buffers(0)[3], 0.0))
                    dve.wait_ge(kout_turned, 1)
                    chain(dve.tensor_copy(kout[:, 0, :], ps[:, 6, 0:P]))
                    dve.tensor_copy(kout[0:DEC, 1, :], ps[0:DEC, 6, P:2 * P]).then_inc(kout_ready, 1)
                    operands(0)
                    gain(0)
                    gain(1)
                if s in splits:
                    low(*splits[s])
            inner_and_states(0)
            chain(dve.memset(hgrn_buffers(1)[3], 0.0))

            dve.memset(logits[:, :, :], 0.0)
            chain(dve.memset(elogits[:, :, :], 0.0))
            def mix_low(t):
                r = rows_of(t)
                dve.wait_ge(mix_hi_done, 2 * t + 1)
                dve.tensor_tensor(mix_lo[:, BH:KC, 0:r], bank(6).rearrange("p (h t) -> p h t", h=BH)[:, :, 0:r],
                                  mix_hi[:, BH:KC, 0:r].bitcast(F32), ALU.subtract)
                dve.wait_ge(mix_hi_done, 2 * t + 2)
                dve.tensor_tensor(mix_lo[:, 0:BH, 0:r], mixT[:, 0:BH, tok(t)], mix_hi[:, 0:BH, 0:r].bitcast(F32),
                                  ALU.subtract).then_inc(rec_taken, 1)

            for t in range(NT):
                if t >= 2:
                    h2T_half(t - 2)
                if t:
                    operands(t)
                if t >= 2:
                    take_logits(t - 2)
                if t:
                    inner_and_states(t)
                    add_out(t - 1, 0)
                else:
                    low(len(W_GROUPS), 6, KC)
                normed(t)
                if t:
                    add_out(t - 1, 1)
                else:
                    low(len(W_GROUPS) + 1, 0, 4)
                if 0 < t < NT - 1:
                    make_h2(t - 1)
                mix_low(t)
                if t == 0:
                    low(len(W_GROUPS) + 1, 4, KC)
                elif t < NT - 1:
                    gain(t + 1)
            make_h2(NT - 2)
            add_out(NT - 1, 0)
            h2T_half(NT - 2)
            add_out(NT - 1, 1)
            take_logits(NT - 2)
            make_h2(NT - 1)
            h2T_half(NT - 1)
            take_logits(NT - 1)

            dve.wait_ge(logits_taken, NT)
            dve.wait_ge(consts, 2)
            rv = rt[:, :, :].rearrange("p a b -> p (a b)")

            def col(i, n=1):
                v = rv[:, i * NT:(i + n) * NT]
                return v if n == 1 else v.rearrange("p (t k) -> p t k", k=n)

            def spread(v, n):
                return v.unsqueeze(2).to_broadcast([P, NT, n])

            def first_max(v, top, hot, scratch):
                chain(dve.tensor_reduce(top, v, AX.X, ALU.max))
                chain(dve.tensor_tensor(scratch, v, spread(top, 4), ALU.is_ge))
                chain(dve.scalar_tensor_tensor(scratch, scratch, -8.0, i4, ALU.mult, ALU.add))
                chain(dve.tensor_reduce(col(3), scratch, AX.X, ALU.min))
                chain(dve.tensor_scalar(col(3), col(3), 8.0, None, ALU.add))
                chain(dve.tensor_tensor(hot, i4, spread(col(3), 4), ALU.is_equal))

            i4 = iota4[:, :].unsqueeze(1).to_broadcast([P, NT, 4])
            group_hot, hot1, hot2, el, scr = (col(a, 4) for a in (8, 12, 16, 20, 24))
            first_max(logits[:, :, :], col(0), group_hot, scr)
            dve.tensor_tensor(rb[:, :, 0:4], logits[:, :, :], spread(col(0), 4), ALU.subtract).then_inc(route_diff, 1)
            picked = picks[:, 0, :, :]
            chain(dve.tensor_tensor(picked.rearrange("p t (g e) -> p (t g) e", g=NG),
                                    elogits[:, :, :].rearrange("p t (g e) -> p (t g) e", g=NG),
                                    group_hot.rearrange("p t g -> p (t g)").unsqueeze(2).to_broadcast(
                                        [P, NT * NG, EPG]), ALU.mult))
            chain(dve.tensor_reduce(el, picked.rearrange("p t (g e) -> p t e g", g=NG), AX.X, ALU.add))
            first_max(el, col(1), hot1, scr)
            chain(dve.scalar_tensor_tensor(el, hot1, -3.0e38, el, ALU.mult, ALU.add))
            first_max(el, col(2), hot2, scr)
            dve.tensor_tensor(rb[:, :, 4:5], spread(col(2), 1), spread(col(1), 1), ALU.subtract).then_inc(route_diff, 1)
            for i, hot in enumerate((hot1, hot2)):
                last = dve.tensor_tensor(picks[:, i, :, :].rearrange("p t (g e) -> p t g e", g=NG),
                                         group_hot.unsqueeze(3).to_broadcast([P, NT, NG, EPG]),
                                         hot.unsqueeze(2).to_broadcast([P, NT, NG, EPG]), ALU.mult)
            chain(last)
            chain(dve.memset(picks[rows_of(NT - 1):P, 0:2, NT - 1, :], 0.0))
            chain(dve.tensor_tensor(picks[:, 2, :, :], picks[:, 0, :, :], picks[:, 1, :, :], ALU.add))
            dve.memset(before[:, 0, :], 0.0)
            chain(dve.tensor_copy(before[:, 1, :], picks[:, 2, 0, :]))
            for t in range(1, NT):
                last = dve.tensor_tensor(before[:, t + 1, :], before[:, t, :], picks[:, 2, t, :], ALU.add)
                if t < NT - 1:
                    chain(last)
            last.then_inc(picks_ready, 1)
            dve.wait_ge(rank_ready, 1)
            chain(dve.tensor_copy(rank_v[:, :, :], ps[:, 0, 0:NT * NE].rearrange("p (t e) -> p t e", e=NE)))
            over, incl, move = (per_expert[:, a, :] for a in range(3))
            rank, expert, j, block = (per_pair[:, a, :, :] for a in range(4))
            limit_e = limits[:, :].unsqueeze(1).to_broadcast([P, NE, TERMS])
            chain(dve.tensor_tensor(compared[:, :, 0:TERMS], ps[:, 1, 0:NE].unsqueeze(2).to_broadcast([P, NE, TERMS]),
                                    limit_e, ALU.is_gt))
            chain(dve.tensor_reduce(over, compared[:, :, 0:TERMS], AX.X, ALU.add))
            chain(dve.tensor_tensor(compared[:, :, :], upto[:, :, :], over.unsqueeze(1).to_broadcast([P, NE, NE]),
                                    ALU.mult))
            chain(dve.tensor_reduce(incl, compared[:, :, :], AX.X, ALU.add))
            chain(dve.scalar_tensor_tensor(move, incl, float(NE - 1), over, ALU.add, ALU.subtract))
            chain(dve.tensor_tensor(move, move, iota16[:, :], ALU.subtract))

            def of_pick(dst, values):
                chain(dve.tensor_tensor(picked_v[:, :, :, :], picks[:, 0:2, :, :], values, ALU.mult))
                chain(dve.tensor_reduce(dst, picked_v[:, :, :, :], AX.X, ALU.add))

            def for_all(v):
                return v.unsqueeze(1).unsqueeze(1).to_broadcast([P, 2, NT, NE])

            of_pick(rank, rank_v[:, :, :].unsqueeze(1).to_broadcast([P, 2, NT, NE]))
            of_pick(expert, for_all(iota16[:, :]))
            of_pick(block, for_all(move))
            compared_j = compared[:, 0:2 * NT, 0:TERMS]
            chain(dve.tensor_tensor(compared_j, rank.rearrange("p i t -> p (i t)").unsqueeze(2).to_broadcast(
                [P, 2 * NT, TERMS]), limits[:, :].unsqueeze(1).to_broadcast([P, 2 * NT, TERMS]), ALU.is_ge))
            chain(dve.tensor_reduce(j.rearrange("p i t -> p (i t)"), compared_j, AX.X, ALU.add))
            chain(dve.tensor_tensor(block, block, j, ALU.add))
            chain(dve.scalar_tensor_tensor(block, j, 0.0, block, ALU.is_gt, ALU.mult))
            chain(dve.tensor_tensor(block, block, expert, ALU.add))
            chain(dve.scalar_tensor_tensor(rank, j, -float(P), rank, ALU.mult, ALU.add))
            pairs = [P, 2 * NT, P]
            dve.tensor_tensor(slot_hot[:, :, :, :].rearrange("p i t s -> p (i t) s"),
                              iota_p[:, :].unsqueeze(1).to_broadcast(pairs),
                              rank.rearrange("p i t -> p (i t)").unsqueeze(2).to_broadcast(pairs), ALU.is_equal)
            pairs = [P, 2 * NT, COLS]
            block_v = block_hot[:, :, :, :].rearrange("p i t s -> p (i t) s")
            chain(dve.tensor_tensor(block_v, iota_p[:, 0:COLS].unsqueeze(1).to_broadcast(pairs),
                                    block.rearrange("p i t -> p (i t)").unsqueeze(2).to_broadcast(pairs),
                                    ALU.is_equal))
            dve.tensor_tensor(block_v, block_v.bitcast(F32), pair_val[:, :, :].rearrange("p i t -> p (i t)").unsqueeze(
                2).to_broadcast(pairs), ALU.mult).then_inc(hot_ready, 1)
            total = incl[:, NE - 1:NE]
            turn = col(6)[:, 0:1]
            chain(dve.tensor_scalar(turn, total, 0.0, float(NE // UNROLL), ALU.is_gt, ALU.add))
            for k in range(UNROLL, MAX_OVER, UNROLL):
                chain(dve.tensor_scalar(col(6)[:, 1:2], total, float(k), None, ALU.is_gt))
                chain(dve.tensor_tensor(turn, turn, col(6)[:, 1:2], ALU.add))
            chain(dve.tensor_tensor(over_hot[:, :, :], incl.unsqueeze(1).to_broadcast([P, MAX_OVER, NE]),
                                    iota8[:, :].unsqueeze(2).to_broadcast([P, MAX_OVER, NE]), ALU.is_le))
            chain(dve.tensor_reduce(col(7, 2).rearrange("p t k -> p (t k)")[:, 0:MAX_OVER], over_hot[:, :, :],
                                    AX.X, ALU.add))
            chain(dve.tensor_scalar(steer[:, 1:1 + MAX_OVER], col(7, 2).rearrange("p t k -> p (t k)")[:, 0:MAX_OVER],
                                    float(NE - 1), None, ALU.min))
            dve.tensor_copy(steer[:, 0:1], turn).then_inc(steer_ready, 1)
            dve.wait_ge(slots_ready, 1)
            chain(dve.tensor_scalar(table_f[:, :], ps[:, 4, 0:COLS], 0.0, float(NOWHERE), ALU.is_equal, ALU.mult))
            chain(dve.scalar_tensor_tensor(table[:, :], ps[:, 4, 0:COLS], -1.0, table_f[:, :], ALU.add, ALU.add))
            dve.tensor_scalar(table_tok[:, :], table[:, :], 1, None, ALU.logical_shift_right).then_inc(table_ready, 1)
            dve.wait_ge(route_exp, 2)
            chain(dve.tensor_reduce(col(4), rb[:, :, 0:4], AX.X, ALU.add))
            chain(dve.tensor_scalar(col(5), rb[:, :, 4], 1.0, None, ALU.add))
            chain(dve.tensor_tensor(col(4), col(4), col(5), ALU.mult))
            chain(dve.reciprocal(gates[:, 0, :], col(4)))
            dve.tensor_tensor(gates[:, 1, :], gates[:, 0, :], rb[:, :, 4], ALU.mult).then_inc(gates_ready, 1)
            dve.wait_ge(gates_ready, 1)

            def x_low(s, half):
                dve.wait_ge(xT_act, 2 * s + half + 1)
                dve.tensor_tensor(xT_lo[:, 4 * half:4 * half + 4, :], bank(1 + half).rearrange("p (c t) -> p c t", c=4),
                                  xT_hi[:, 4 * half:4 * half + 4, :].bitcast(F32), ALU.subtract).then_inc(xT_dve, 1)

            def gu_low(slot, block, first, last):
                for q in range(first, last):
                    dve.wait_ge(gu_hi_done, KC // 2 * block + q + 1)
                    dve.tensor_tensor(gu_lo[slot][:, :, 2 * q:2 * q + 2, :], we_gu[slot][:, :, 2 * q:2 * q + 2, :],
                                      gu_hi[slot % 2][:, :, 2 * q:2 * q + 2, :].bitcast(F32),
                                      ALU.subtract).then_inc(gu_lo_done, 1)

            gu_low(0, 0, 0, KC // 2)
            x_low(0, 0)
            x_low(0, 1)
            gu_low(1, 1, 0, KC // 2)
            dve.sem_inc(y_dve, 2)
            dve.wait_ge(steer_ready, 1)
            turns = dve.value_load(steer[0:1, 0:1], min_val=NE // UNROLL, max_val=BLOCKS // UNROLL)

            def split_ahead(slot, i, half):
                if slot in (1, 2):
                    gu_low(slot + 1, UNROLL * i + slot + 1, 2 * half, 2 * half + 2)
                elif slot == UNROLL - 1:
                    with dve.If(i < turns - 1):
                        gu_low(0, UNROLL * i + UNROLL, 2 * half, 2 * half + 2)
                        if half == 1:
                            gu_low(1, UNROLL * i + UNROLL + 1, 0, KC // 2)

            def take_y(i, slot):
                dve.wait_ge(y_ready, UNROLL * i + slot + 1)
                dve.wait_ge(stored[slot % 2], 16 * (2 * i + slot // 2 + 1))
                dve.tensor_copy(y[:, slot % 2, 512:1024], bank(5 + 2 * (slot % 2))).then_inc(y_dve, 1)

            with dve.Fori(0, turns) as i:
                for slot in range(UNROLL):
                    s = UNROLL * i + slot
                    split_ahead(slot, i, 0)
                    dve.wait_ge(silu_ready, s + 1)
                    dve.tensor_tensor(hh[:, :], sg[:, :], ps[:, 0, FE:2 * FE], ALU.mult).then_inc(hh_ready, 1)
                    x_low(s + 1, 0)
                    x_low(s + 1, 1)
                    if slot < UNROLL - 1:
                        split_ahead(slot, i, 1)
                    dve.wait_ge(hh_turned, s + 1)
                    dve.tensor_copy(hhT[:, slot % 2, :, :], ps[:, 3, 0:2 * P].rearrange("p (c t) -> p c t", c=2)
                                    ).then_inc(hhT_ready, 1)
                    if slot == UNROLL - 1:
                        split_ahead(slot, i, 1)
                    if slot:
                        take_y(i, slot - 1)
                take_y(i, UNROLL - 1)

            def weigh(t):
                r = rows_of(t)
                dve.wait_ge(pair_in[t], 16)
                for i in range(2):
                    dve.scalar_tensor_tensor(x[0:r, t, :], pair[0:r, t, i * D:(i + 1) * D], gates[0:r, i, t:t + 1],
                                             x[0:r, t, :], ALU.mult, ALU.add).then_inc(sum_ready, 1)
                    dve.wait_ge(sum_ready, 2 * t + i + 1)

            def final(t):
                r = rows_of(t)
                dve.wait_ge(rstd3_ready, t + 1)
                dve.scalar_tensor_tensor(pair[0:r, t, 0:D], x[0:r, t, :], stats[0:r, 5, t:t + 1], gf_bc[0:r, :],
                                         ALU.mult, ALU.mult).then_inc(final_ready, 1)

            weigh(0)
            for t in range(1, NT):
                weigh(t)
                final(t - 1)
            final(NT - 1)

        @block.tensor
        def _(pe):
            def turn_x(t):
                r = rows_of(t)
                pe.wait_ge(hn_ready, t + 1)
                if t >= 3:
                    pe.wait_ge(hT_dve, t - 2)
                for c in range(KC):
                    b = 2 + 2 * (t % 3) + c // 4
                    last = pe.transpose(ps[:, b, (c % 4) * P:(c % 4) * P + r], hn[0:r, t % 2, c * P:(c + 1) * P],
                                        ident[0:r, 0:r])
                last.then_inc(turned, 1)

            def project(n):
                kind, i, _ = groups[n]
                k = ring_of[kind]
                if n >= 2:
                    who, v = emptied[n - 2]
                    pe.wait_ge(proj_act if who == "act" else proj_dve, v)
                fresh = i == 0 and kind != "v"
                b = n % 2
                hi, lo = w_hi[k % RING], w_lo[k % RING]
                for c in range(KC):
                    if fresh:
                        pe.wait_ge(w_lo_done, KC * k + c + 1)
                    if kind in "figv":
                        cols = slice(KVW, 2 * KVW) if kind == "v" else slice(0, 512)
                        h_parts = (hT_hi[:, c, tok(i)], h_lo(c)[:, tok(i)])
                        w_parts = (hi[:, c, cols], lo[:, c, cols])
                        out = ps[0:rows_of(i), b, 0:cols.stop - cols.start]
                        stationary, moving = h_parts, w_parts
                    else:
                        m, half = (0, i) if kind == "k" else (i // 2, i % 2)
                        cols, toks = slice(m * P, (m + 1) * P), slice(half * HALF, (half + 1) * HALF)
                        stationary = (hi[:, c, cols], lo[:, c, cols])
                        moving = (hT_hi[:, c, toks], h_lo(c)[:, toks])
                        out = bank(b, HALF)
                    pe.matmul(out, stationary[0], moving[0], start=c == 0, stop=False)
                    pe.matmul(out, stationary[0], moving[1], start=False, stop=False)
                    last = pe.matmul(out, stationary[1], moving[0], start=False, stop=c == KC - 1)
                last.then_inc(proj_ready, 1)

            pe.wait_ge(consts, 1)
            turn_x(0)
            for t in range(NT):
                pe.wait_ge(hT_dve, t + 1)
                project(t)
                for following in ((1, 2), (3,), (4,), (), ())[t]:
                    turn_x(following)
            pe.wait_ge(ck_in, 16)
            pe.wait_ge(hT_dve, NT)
            pe.transpose(ps[:, 7, 0:P], kout[:, 0, :], ident[:, :]).then_inc(cache_turned, 1)
            for n in range(NT, first_filler):
                project(n)

            def scores(c):
                lo, hi, _, start = window(c)
                pe.wait_ge(qbd_ready, KV * (c + 1))
                if c == 0:
                    wait_emptied(pe, "k")
                    pe.wait_ge(cache_taken, 1)
                else:
                    pe.wait_ge(scores_taken, c)
                for m in range(GROUP):
                    last = pe.matmul(ps[:, 2 + m // 2, (m % 2) * 2 * P + lo:(m % 2) * 2 * P + hi], qbd[:, c % 2, m, :],
                                     kT[:, start:start + hi - lo], start=True, stop=True)
                last.then_inc(scores_ready, 1)

            def turn_p(c):
                pe.wait_ge(p_ready, c + 1)
                if c == 1:
                    pe.wait_ge(dve_consts, 1)
                if c >= 1:
                    pe.wait_ge(pt_dve, c)
                if c >= 3:
                    pe.wait_ge(pt_act, c - 2)
                r = P if c % 2 else CHUNK
                for m in range(GROUP):
                    if has_before(c):
                        pe.transpose(ps[:, 4, m * P:(m + 1) * P], s_buf[:, c % 2, m, 0:P], ident[:, :])
                    last = pe.transpose(ps[0:r, 5, m * P:(m + 1) * P], s_buf[:, c % 2, m, P:P + r], ident[:, :])
                last.then_inc(p_turned, 1)

            def attend(c):
                slot_a, slot_b = v_slots(c)
                rows_a = slice(CHUNK, P) if c % 2 else slice(0, P)
                rows_b = slice(0, P if c % 2 else CHUNK)
                if c == 0:
                    wait_emptied(pe, "v")
                if c == NCHUNK - 1:
                    pe.wait_ge(cv_in, 16)
                pe.wait_ge(pt_dve, c + 1)
                if has_before(c):
                    pe.wait_ge(pt_act, c - 1)
                if c:
                    pe.wait_ge(o_taken, c)
                for b in range(KV):
                    def probs(part, rows):
                        return pt[rows, c % 2, part, :].rearrange("p (m b q) -> p m b q", m=GROUP, b=KV)[:, :, b, :]
                    out = ps[b * HD:(b + 1) * HD, 6, 0:GROUP * CHUNK]
                    heads = slice(b * HD, (b + 1) * HD)
                    if has_before(c):
                        pe.matmul(out, V[rows_a, slot_a, heads], probs(0, rows_a), start=True, stop=False)
                    last = pe.matmul(out, V[rows_b, slot_b, heads], probs(1, rows_b), start=not has_before(c),
                                     stop=True)
                last.then_inc(pv_done, 1)

            def decays(t):
                r = rows_of(t)
                pe.wait_ge(logf_ready, t + 1)
                if t:
                    pe.wait_ge(state_ready, 2 * t)
                    pe.wait_ge(rec_ready, t)
                for h in range(BH):
                    cols = slice(h * BK, (h + 1) * BK)
                    pe.matmul(ps[:, 2 + h // 2, (h % 2) * 2 * P:(h % 2 + 1) * 2 * P], logf[0:r, t, cols],
                              decay_m[0:r, :, :], start=True, stop=True)
                    pe.transpose(ps[:, 4, h * P:h * P + r], kf[0:r, t, cols], ident[0:r, 0:r])
                pe.matmul(ps[0:r, 5, :], tail_m[0:r, 0:r], logf[0:r, t, :], start=True, stop=True).then_inc(cum_ready, 1)

            def inner(t):
                r = rows_of(t)
                qin, kin, _, _, kdec, _ = hgrn_buffers(t)
                pe.wait_ge(hops_ready, 4 * t + 4)
                if t:
                    pe.wait_ge(rec_taken, t)
                if t >= 2:
                    pe.wait_ge(logits_taken, t - 1)
                for h in range(BH):
                    pe.matmul(ps[0:r, 6, h * P:h * P + r], kin[:, h, 0:r], qin[:, h, 0:r], start=True, stop=True)
                for c in range(r // CHUNK):
                    rows = slice(c * CHUNK, (c + 1) * CHUNK)
                    for h in range(BH):
                        cols = slice(h * BK, (h + 1) * BK)
                        last = pe.matmul(ps[:, 4 if c else 7, cols], kdec[rows, h, :], vf[rows, t, cols],
                                         start=True, stop=True)
                last.then_inc(inner_ready, 1)

            for s, fill in enumerate(slots):
                if s == EARLY:
                    pe.wait_ge(o_taken, NCHUNK)
                    pe.transpose(ps[:, 6, 0:P], kT[:, SEQ - P:SEQ], ident[:, :])
                    pe.transpose(ps[0:DEC, 6, P:2 * P], kT[:, SEQ + WINDOW:], ident[:, :]).then_inc(kout_turned, 1)
                    decays(0)
                for n in fill:
                    project(n)
                if s < NCHUNK:
                    scores(s)
                if 1 <= s <= NCHUNK:
                    turn_p(s - 1)
                if 2 <= s < NCHUNK + 2:
                    attend(s - 2)
                if s == EARLY:
                    pe.wait_ge(kout_ready, 1)
                    inner(0)

            def sums(t):
                r = rows_of(t)
                _, _, qex, aT, _, _ = hgrn_buffers(t)
                pe.wait_ge(at_ready, t + 1)
                if t == NT - 1:
                    pe.wait_ge(s_in, 16)
                elif r > CHUNK:
                    pe.wait_ge(state_ready, 2 * t + 1)
                for h in range(BH):
                    cols = slice(h * BK, (h + 1) * BK)
                    terms = []
                    for c in range(r // CHUNK):
                        before = s_sample if t == NT - 1 else St[(2 * t + c) % 3]
                        if 2 * t + c:
                            terms.append((c, before))
                    pe.matmul(ps[0:r, 5, cols], aT[0:r, h, 0:r], vf[0:r, t, cols], start=True, stop=True)
                    for c, before in terms:
                        rows = slice(c * CHUNK, (c + 1) * CHUNK)
                        last = pe.matmul(ps[rows, 5, cols], qex[:, h, rows], before[:, cols], start=False,
                                         stop=True, skip_group_check=True)
                last.then_inc(rec_sum, 1)

            def turn_rec(t):
                r = rows_of(t)
                rec = hgrn_buffers(t)[5]
                pe.wait_ge(rec_ready, t + 1)
                for h in range(BH):
                    last = pe.transpose(ps[:, 6, h * P:h * P + r], rec[0:r, h * BK:(h + 1) * BK], ident[0:r, 0:r])
                last.then_inc(rec_turned, 1)

            def out_part(t, first, last_n):
                r = rows_of(t)
                for n in range(first, last_n):
                    half, c = n // KC, n % KC
                    k = len(W_GROUPS) + half
                    if c == 0:
                        if t == 0:
                            pe.wait_ge(w_lo_done, KC * (k + 1))
                            wait_emptied(pe, "g")
                            wait_emptied(pe, "b")
                        else:
                            pe.wait_ge(x2_ready, 2 * (t - 1) + half + 1)
                        pe.wait_ge(rec_taken, t + 1)
                    out, w_h, w_l = ps[0:r, half, :], w_high(k, c), w_lo[k % RING][:, c, :]
                    pe.matmul(out, mix_hi[:, c, 0:r], w_h, start=c == 0, stop=False)
                    pe.matmul(out, mix_hi[:, c, 0:r], w_l, start=False, stop=False)
                    last = pe.matmul(out, mix_lo[:, c, 0:r], w_h, start=False, stop=c == KC - 1)
                    if c == KC - 1:
                        last.then_inc(out_ready, 1)

            def turn_h2(t):
                r = rows_of(t)
                pe.wait_ge(h2_ready, t + 1)
                for c in range(KC):
                    last = pe.transpose(ps[:, turned_bank(t) + c // 4, (c % 4) * P:(c % 4) * P + r],
                                        h2[0:r, t % 2, c * P:(c + 1) * P], ident[0:r, 0:r])
                last.then_inc(h2_turned, 1)

            def route(t):
                r = rows_of(t)
                pe.wait_ge(h2T_act, t + 1)
                pe.wait_ge(h2T_dve, t + 1)
                if t:
                    pe.wait_ge(logits_taken, t)
                if t == NT - 2:
                    pe.wait_ge(state_ready, 2 * PROMPT_TILES + 1)
                for c in range(KC):
                    last = pe.matmul(ps[0:r, 7, 0:NG + NE], h2T[:, c * P:c * P + r], w_route[:, c, :],
                                     start=c == 0, stop=c == KC - 1)
                last.then_inc(logits_ready, 1)

            for t in range(NT):
                if t:
                    decays(t)
                if t >= 2:
                    turn_h2(t - 2)
                    route(t - 2)
                if t:
                    out_part(t - 1, 0, 4)
                    inner(t)
                    out_part(t - 1, 4, 9)
                sums(t)
                if t:
                    out_part(t - 1, 9, 2 * KC)
                turn_rec(t)
            out_part(NT - 1, 0, KC)
            turn_h2(NT - 2)
            out_part(NT - 1, KC, 2 * KC)
            route(NT - 2)
            turn_h2(NT - 1)
            route(NT - 1)

            pe.wait_ge(picks_ready, 1)
            pe.wait_ge(x2_ready, 2 * NT)
            pe.matmul(ps[:, 0, 0:NT * NE], ones[:, :], before[:, 0:NT, :].rearrange("p t e -> p (t e)"),
                      start=True, stop=False)
            pe.matmul(ps[:, 0, 0:NT * NE], earlier[:, :], picks[:, 2, :, :].rearrange("p t e -> p (t e)"),
                      start=False, stop=True)
            pe.matmul(ps[:, 1, 0:NE], ones[:, :], before[:, NT, :], start=True, stop=True).then_inc(rank_ready, 1)
            pe.wait_ge(hot_ready, 1)
            for i in range(2):
                for t in range(NT):
                    last = pe.matmul(ps[:, 4, 0:COLS], slot_hot[:, i, t, :], block_hot[:, i, t, :],
                                     start=i + t == 0, stop=i == 1 and t == NT - 1)
            last.then_inc(slots_ready, 1)

            def turn_half(slot, half, signal):
                for c in range(4 * half, 4 * half + 4):
                    last = pe.transpose(ps[:, 1 + half, (c % 4) * P:(c % 4 + 1) * P], xg[:, slot, c:D:KC], ident[:, :])
                last.then_inc(signal, 1)

            def down(i, slot):
                pe.wait_ge(hhT_ready, UNROLL * i + slot + 1)
                pe.wait_ge(y_act, UNROLL * i + slot + 1)
                pe.wait_ge(y_dve, UNROLL * i + slot + 1)
                for half in range(2):
                    for f in range(2):
                        last = pe.matmul(bank(4 + 2 * (slot % 2) + half), hhT[:, slot % 2, f, :],
                                         we_d[slot][:, f, 512 * half:512 * half + 512], start=f == 0, stop=f == 1)
                last.then_inc(y_ready, 1)

            pe.wait_ge(steer_ready, 1)
            turns = pe.value_load(steer[0:1, 0:1], min_val=NE // UNROLL, max_val=BLOCKS // UNROLL)
            pe.wait_ge(gathered[0], 16)
            turn_half(0, 0, x_turned_a)
            turn_half(0, 1, x_turned_b)
            with pe.Fori(0, turns) as i:
                for slot in range(UNROLL):
                    s = UNROLL * i + slot
                    following = (slot + 1) % UNROLL
                    pe.wait_ge(xT_dve, 2 * s + 2)
                    pe.wait_ge(gu_lo_done, KC // 2 * s + KC // 2)
                    gu_h, gu_l = gu_hi[slot % 2], gu_lo[slot]
                    for c in range(KC):
                        pe.matmul(bank(0), xT_hi[:, c, :], gu_h[:, :, c, :], start=c == 0, stop=False)
                        pe.matmul(bank(0), xT_hi[:, c, :], gu_l[:, :, c, :], start=False, stop=False)
                        last = pe.matmul(bank(0), xT_lo[:, c, :], gu_h[:, :, c, :], start=False, stop=c == KC - 1)
                    last.then_inc(gu_ready, 1)
                    pe.wait_ge(gathered[following], 16 * (i + (slot + 1) // UNROLL + 1))
                    turn_half(following, 0, x_turned_a)
                    turn_half(following, 1, x_turned_b)
                    if 0 < slot < UNROLL - 1:
                        down(i, slot - 1)
                    pe.wait_ge(hh_ready, s + 1)
                    for f in range(2):
                        last = pe.transpose(ps[:, 3, f * P:(f + 1) * P], hh[:, f:FE:2], ident[:, :])
                    last.then_inc(hh_turned, 1)
                down(i, UNROLL - 2)
                down(i, UNROLL - 1)
    return nc


def kernel(**inputs):
    import numpy as _np
    import concourse.bacc as _bacc
    from concourse import mybir as _mybir
    from concourse.bass_utils import run_bass_kernel_spmd as _run

    nc = _bacc.Bacc("TRN2", target_bir_lowering=False, num_devices=1)
    layout = {
        "x_p": ("x_prompt", (SEQ, D)), "x_s": ("x_sample", (DEC, D)),
        "cache_k": ("cache_k", (WINDOW, KVW)), "cache_v": ("cache_v", (WINDOW, KVW)),
        "state": ("state_hgrn", (BH, BK, BK)), "g1": ("norm1_g", (D,)), "w_in": ("w_in", (D, G0 + BW)),
        "sink": ("attn_sink", (HEADS,)), "lower": ("lower_bounds", (2, BW)), "ng": ("hgrn_norm_g", (BW,)),
        "w_o": ("w_o", (D, D)), "g2": ("norm2_g", (D,)), "w_rg": ("w_router_group", (D, NG)),
        "b_rg": ("b_router_group", (NG,)), "w_re": ("w_router_expert", (NG, D, EPG)),
        "b_re": ("b_router_expert", (NG, EPG)), "w_gate": ("w_gate", (NE, D, FE)), "w_up": ("w_up", (NE, D, FE)),
        "w_down": ("w_down", (NE, FE, D)), "gf": ("final_norm_g", (D,)),
    }
    results = {
        "y_p": ((SEQ, D), (1, SEQ, D)), "y_s": ((DEC, D), (1, DEC, D)),
        "k_win_p": ((WINDOW, KVW), (1, 1, WINDOW, KV, HD)), "v_win_p": ((WINDOW, KVW), (1, 1, WINDOW, KV, HD)),
        "state_p": ((BH, BK, BK), (1, 1, BH, BK, BK)),
        "k_win_s": ((WINDOW, KVW), (1, 1, WINDOW, KV, HD)), "v_win_s": ((WINDOW, KVW), (1, 1, WINDOW, KV, HD)),
        "state_s": ((BH, BK, BK), (1, 1, BH, BK, BK)),
    }
    arrays, io = {}, {}
    for name, (key, shape) in layout.items():
        arrays[f"in_{name}"] = _np.ascontiguousarray(inputs[key]).reshape(shape)
        io[name] = nc.dram_tensor(f"in_{name}", shape, _mybir.dt.float32, kind="ExternalInput").ap()
    for name, (shape, _) in results.items():
        io[name] = nc.dram_tensor(f"out_{name}", shape, _mybir.dt.float32, kind="ExternalOutput").ap()
    program(nc, io)
    r = _run(nc, [arrays], core_ids=[0])
    return tuple(r.results[0][f"out_{name}"].reshape(shape) for name, (_, shape) in results.items())
```
